# Optimizing a Trainium2 kernel written in Bass

```python
import jax
import jax.numpy as jnp
from jax import lax
import numpy as np

D_MODEL = 1024
BATCH = 1
SEQ = 256
DEPTH = 2

GRID_W = 64
CTX_LEN = 256
HEAD_DIM = 64
ATTN_SCALE = HEAD_DIM ** -0.5

NA_HEADS = 8
NA_WIDTH = NA_HEADS * HEAD_DIM
WIN_ROWS = 8
WIN_COLS = 16
QCOL_BLK = 16
KCOL_BAND = QCOL_BLK + WIN_COLS

POOL_WINDOWS = (2, 4, 8, 16)
POOL_GROUPS = 4
POOL_GW = 128
POOL_WIDTH = POOL_GROUPS * POOL_GW

SWA_HEADS = 8
SWA_KV_HEADS = 2
SWA_GROUP = SWA_HEADS // SWA_KV_HEADS
SWA_WIDTH = SWA_HEADS * HEAD_DIM
SWA_KV_WIDTH = SWA_KV_HEADS * HEAD_DIM
SWA_WINDOW = 128
SWA_BLK = 128
ROPE_THETA = 10000.0
ROPE_AXIS_DIM = HEAD_DIM // 2

N_BRANCHES = 3
BRANCH_W = 512
IN_DIM = 3 * NA_WIDTH + POOL_WIDTH + SWA_WIDTH + 2 * SWA_KV_WIDTH + N_BRANCHES * D_MODEL

N_GROUPS = 4
EXP_PER_GROUP = 8
N_EXPERTS = N_GROUPS * EXP_PER_GROUP
TOP_K = 2
D_EXPERT = 512
MOE_BLK = 128

N_MOD = 6
NORM_EPS = 1e-6
NEG_INF = -1e30

kernel_name = 'hybrid_natten_pool_swa_hmoe_dit'

def _in_slices():
    widths = (('a_q', NA_WIDTH), ('a_k', NA_WIDTH), ('a_v', NA_WIDTH), ('b_u', POOL_WIDTH),
              ('c_q', SWA_WIDTH), ('c_k', SWA_KV_WIDTH), ('c_v', SWA_KV_WIDTH),
              ('gates', N_BRANCHES * D_MODEL))
    out, off = {}, 0
    for name, w in widths:
        out[name] = slice(off, off + w)
        off += w
    return out

def rms_norm(x, g):
    xf = x.astype(jnp.float32)
    y = xf * lax.rsqrt(jnp.mean(xf * xf, axis=-1, keepdims=True) + NORM_EPS)
    return (y * g).astype(x.dtype)

def adaln_modulation(cvec, w_mod, b_mod):
    m = jax.nn.silu(cvec) @ w_mod + b_mod
    return jnp.split(m, N_MOD, axis=-1)

def modulate(h, shift, scale):
    return h * (1 + scale) + shift

def split_heads(t):
    return t.reshape(t.shape[:-1] + (t.shape[-1] // HEAD_DIM, HEAD_DIM))

def axial_rope_angles(n_tokens):
    t = jnp.arange(n_tokens, dtype=jnp.int32)
    row = (t // GRID_W).astype(jnp.float32)
    col = (t % GRID_W).astype(jnp.float32)
    inv = ROPE_THETA ** (-jnp.arange(0, ROPE_AXIS_DIM, 2, dtype=jnp.float32) / ROPE_AXIS_DIM)
    return row[:, None] * inv[None, :], col[:, None] * inv[None, :]

def _rotate(x, ang):
    cos = jnp.cos(ang)[None, :, None, :]
    sin = jnp.sin(ang)[None, :, None, :]
    x1, x2 = jnp.split(x, 2, axis=-1)
    return jnp.concatenate([x1 * cos - x2 * sin, x2 * cos + x1 * sin], axis=-1)

def axial_rotary(x, ang_r, ang_c):
    xr, xc = jnp.split(x, 2, axis=-1)
    return jnp.concatenate([_rotate(xr, ang_r), _rotate(xc, ang_c)], axis=-1).astype(x.dtype)

def context_attention(q, k, v, sink):
    n_keys = k.shape[1]
    s = jnp.einsum('bqhgd,bkhd->bhgqk', q, k, preferred_element_type=jnp.float32) * ATTN_SCALE
    if sink is not None:
        sink_col = jnp.broadcast_to(sink.astype(jnp.float32)[None, :, :, None, None], s.shape[:-1] + (1,))
        s = jnp.concatenate([s, sink_col], axis=-1)
    p = jax.nn.softmax(s, axis=-1)[..., :n_keys].astype(v.dtype)
    return jnp.einsum('bhgqk,bkhd->bqhgd', p, v)

def neighborhood_attention(q, k, v, kz, vz, rpb):
    B, S, H, dh = q.shape
    rows = S // GRID_W
    kh = min(WIN_ROWS, rows)
    ncb = GRID_W // QCOL_BLK
    qg = q.reshape(B, rows, ncb, QCOL_BLK, H, dh)
    kg = k.reshape(B, rows, GRID_W, H, dh)
    vg = v.reshape(B, rows, GRID_W, H, dh)
    qcol = np.arange(GRID_W).reshape(ncb, QCOL_BLK)
    band0 = np.clip(np.arange(ncb) * QCOL_BLK - WIN_COLS // 2, 0, GRID_W - KCOL_BAND)
    kcol = band0[:, None] + np.arange(KCOL_BAND)[None, :]
    wstart = np.clip(qcol - WIN_COLS // 2, 0, GRID_W - WIN_COLS)
    col_ok = (kcol[:, None, :] >= wstart[:, :, None]) & (kcol[:, None, :] < wstart[:, :, None] + WIN_COLS)
    dcol_idx = np.clip(kcol[:, None, :] - qcol[:, :, None] + WIN_COLS - 1, 0, 2 * WIN_COLS - 2)
    n_win = kh * KCOL_BAND

    def row_block(r):
        r0 = jnp.clip(r - kh // 2, 0, rows - kh)
        kb = lax.dynamic_slice_in_dim(kg, r0, kh, axis=1)[:, :, kcol]
        vb = lax.dynamic_slice_in_dim(vg, r0, kh, axis=1)[:, :, kcol]
        qb = lax.dynamic_index_in_dim(qg, r, axis=1, keepdims=False)
        s_win = jnp.einsum('bjqhd,brjkhd->bhjqrk', qb, kb, preferred_element_type=jnp.float32) * ATTN_SCALE
        drow = r0 + jnp.arange(kh) - r + WIN_ROWS - 1
        bias = rpb[:, drow[None, None, :, None], dcol_idx[:, :, None, :]]
        s_win = jnp.where(col_ok[:, :, None, :], s_win + bias.astype(jnp.float32), NEG_INF)
        s_win = s_win.reshape(B, H, ncb, QCOL_BLK, n_win)
        s_ctx = jnp.einsum('bjqhd,bchd->bhjqc', qb, kz, preferred_element_type=jnp.float32) * ATTN_SCALE
        p = jax.nn.softmax(jnp.concatenate([s_win, s_ctx], axis=-1), axis=-1).astype(v.dtype)
        p_win = p[..., :n_win].reshape(B, H, ncb, QCOL_BLK, kh, KCOL_BAND)
        o = (jnp.einsum('bhjqrk,brjkhd->bjqhd', p_win, vb)
             + jnp.einsum('bhjqc,bchd->bjqhd', p[..., n_win:], vz))
        return o.reshape(B, GRID_W, H, dh)

    out = lax.map(row_block, jnp.arange(rows, dtype=jnp.int32))
    return out.transpose(1, 0, 2, 3, 4).reshape(B, S, H * dh)

def multiscale_pool(u, w_pool, pool_scale):
    B, L, _ = u.shape
    uf = u.astype(jnp.float32)
    cs = jnp.concatenate([jnp.zeros((B, 1, POOL_WIDTH), jnp.float32), jnp.cumsum(uf, axis=1)], axis=1)
    t = np.arange(L)
    diffs = []
    for g, w in enumerate(POOL_WINDOWS):
        lo = np.clip(t - w // 2, 0, L)
        hi = np.clip(t + w // 2, 0, L)
        csg = cs[..., g * POOL_GW:(g + 1) * POOL_GW]
        mean = (csg[:, hi] - csg[:, lo]) / (hi - lo).astype(np.float32)[None, :, None]
        diffs.append(mean - uf[..., g * POOL_GW:(g + 1) * POOL_GW])
    d = jnp.stack(diffs, axis=2).astype(u.dtype)
    y = jnp.einsum('blgc,gce->blge', d, w_pool).reshape(B, L, POOL_WIDTH)
    return y * pool_scale

def windowed_gqa_sink(q, k, v, kz, vz, sink):
    B, S, HQ, dh = q.shape
    nb = S // SWA_BLK
    qg = q.reshape(B, S, SWA_KV_HEADS, SWA_GROUP, dh)
    pad = ((0, 0), (SWA_BLK, SWA_BLK), (0, 0), (0, 0))
    kp = jnp.pad(k, pad)
    vp = jnp.pad(v, pad)
    rel = (np.arange(3 * SWA_BLK) - SWA_BLK)[None, :] - np.arange(SWA_BLK)[:, None]
    near = np.abs(rel) <= SWA_WINDOW
    sink_l = sink.astype(jnp.float32).reshape(SWA_KV_HEADS, SWA_GROUP)[None, :, :, None, None]
    n_win = 3 * SWA_BLK

    def block(i):
        q0 = i * SWA_BLK
        qb = lax.dynamic_slice_in_dim(qg, q0, SWA_BLK, axis=1)
        kb = lax.dynamic_slice_in_dim(kp, q0, n_win, axis=1)
        vb = lax.dynamic_slice_in_dim(vp, q0, n_win, axis=1)
        kpos = q0 - SWA_BLK + jnp.arange(n_win)
        ok = near & ((kpos >= 0) & (kpos < S))[None, :]
        s_win = jnp.einsum('bqhgd,bkhd->bhgqk', qb, kb, preferred_element_type=jnp.float32) * ATTN_SCALE
        s_win = jnp.where(ok, s_win, NEG_INF)
        s_ctx = jnp.einsum('bqhgd,bkhd->bhgqk', qb, kz, preferred_element_type=jnp.float32) * ATTN_SCALE
        s_sink = jnp.broadcast_to(sink_l, s_win.shape[:-1] + (1,))
        p = jax.nn.softmax(jnp.concatenate([s_win, s_ctx, s_sink], axis=-1), axis=-1).astype(v.dtype)
        o = (jnp.einsum('bhgqk,bkhd->bqhgd', p[..., :n_win], vb)
             + jnp.einsum('bhgqk,bkhd->bqhgd', p[..., n_win:n_win + kz.shape[1]], vz))
        return o.reshape(B, SWA_BLK, HQ * dh)

    out = lax.map(block, jnp.arange(nb, dtype=jnp.int32))
    return out.transpose(1, 0, 2, 3).reshape(B, S, HQ * dh)

def merge_branches(ya, yb, yc, gate_logits, w_branch, w_out):
    ga, gb, gc = jnp.split(jax.nn.sigmoid(gate_logits), N_BRANCHES, axis=-1)
    m = ga * (ya @ w_branch[0]) + gb * (yb @ w_branch[1]) + gc * (yc @ w_branch[2])
    return m @ w_out

def expert_dispatch(h, experts, weights, w_gate, w_up, w_down):
    T, D = h.shape
    n_assign = T * TOP_K
    n_slots = -(-(n_assign + N_EXPERTS * (MOE_BLK - 1)) // MOE_BLK) * MOE_BLK
    n_blk = n_slots // MOE_BLK
    flat_e = experts.reshape(n_assign)
    order = jnp.argsort(flat_e)
    sorted_e = flat_e[order]
    counts = jnp.bincount(flat_e, length=N_EXPERTS)
    padded = ((counts + MOE_BLK - 1) // MOE_BLK) * MOE_BLK
    pad_end = jnp.cumsum(padded)
    pad_start = pad_end - padded
    start = jnp.cumsum(counts) - counts
    dest = pad_start[sorted_e] + jnp.arange(n_assign, dtype=jnp.int32) - start[sorted_e]
    token_of_slot = jnp.full((n_slots,), T, jnp.int32).at[dest].set(order // TOP_K)
    h_pad = jnp.concatenate([h, jnp.zeros((1, D), h.dtype)], axis=0)
    xs = h_pad[token_of_slot].reshape(n_blk, MOE_BLK, D)
    block_expert = jnp.minimum(
        jnp.searchsorted(pad_end, jnp.arange(n_blk, dtype=jnp.int32) * MOE_BLK, side='right'),
        N_EXPERTS - 1).astype(jnp.int32)

    def run_block(args):
        xb, e = args
        return (jax.nn.silu(xb @ w_gate[e]) * (xb @ w_up[e])) @ w_down[e]

    ys = lax.map(run_block, (xs, block_expert)).reshape(n_slots, D)
    w_sorted = weights.reshape(n_assign)[order].astype(h.dtype)
    return jnp.zeros((T, D), h.dtype).at[order // TOP_K].add(ys[dest] * w_sorted[:, None])

def hierarchical_moe(h, w_rg, b_rg, w_re, b_re, w_gate, w_up, w_down):
    T = h.shape[0]
    lg = jnp.dot(h, w_rg, preferred_element_type=jnp.float32) + b_rg
    pg = jax.nn.softmax(lg, axis=-1)
    _, g_top = lax.top_k(lg, 1)
    p_grp = jnp.take_along_axis(pg, g_top, axis=-1)
    le = (jnp.dot(h, w_re, preferred_element_type=jnp.float32) + b_re).reshape(T, N_GROUPS, EXP_PER_GROUP)
    le_g = jnp.take_along_axis(le, g_top[:, :, None], axis=1)[:, 0]
    top_p, top_i = lax.top_k(jax.nn.softmax(le_g, axis=-1), TOP_K)
    top_p = top_p / jnp.sum(top_p, axis=-1, keepdims=True)
    weights = p_grp * top_p
    experts = (g_top * EXP_PER_GROUP + top_i).astype(jnp.int32)
    return expert_dispatch(h, experts, weights, w_gate, w_up, w_down)

def setup_inputs(seed: int = 0) -> dict:
    key = jax.random.key(seed)
    ks = jax.random.split(key, 23)
    f32 = jnp.float32

    def nrm(k, shape, std):
        return jax.random.normal(k, shape, f32) * std

    D = D_MODEL
    return {
        'x': nrm(ks[0], (BATCH, SEQ, D), 1.0),
        'c': nrm(ks[1], (BATCH, D), 1.0),
        'ctx': nrm(ks[2], (BATCH, CTX_LEN, D), 1.0),
        'c_ctx': nrm(ks[3], (D,), 1.0),
        'w_mod': nrm(ks[4], (DEPTH, D, N_MOD * D), D ** -0.5),
        'b_mod': nrm(ks[5], (DEPTH, N_MOD * D), 0.02),
        'norm1_g': 1.0 + nrm(ks[6], (DEPTH, D), 0.02),
        'norm2_g': 1.0 + nrm(ks[7], (DEPTH, D), 0.02),
        'w_in': nrm(ks[8], (DEPTH, D, IN_DIM), D ** -0.5),
        'rpb_a': nrm(ks[9], (DEPTH, NA_HEADS, 2 * WIN_ROWS - 1, 2 * WIN_COLS - 1), 0.5),
        'w_pool': nrm(ks[10], (DEPTH, POOL_GROUPS, POOL_GW, POOL_GW), POOL_GW ** -0.5),
        'pool_scale': 1.0 + nrm(ks[11], (DEPTH, POOL_WIDTH), 0.1),
        'sink_c': nrm(ks[12], (DEPTH, SWA_HEADS), 1.0),
        'w_branch': nrm(ks[13], (DEPTH, N_BRANCHES, BRANCH_W, D), BRANCH_W ** -0.5),
        'w_out': nrm(ks[14], (DEPTH, D, D), D ** -0.5),
        'w_router_group': nrm(ks[15], (DEPTH, D, N_GROUPS), D ** -0.5),
        'b_router_group': nrm(ks[16], (DEPTH, N_GROUPS), 0.01),
        'w_router_expert': nrm(ks[17], (DEPTH, D, N_EXPERTS), D ** -0.5),
        'b_router_expert': nrm(ks[18], (DEPTH, N_EXPERTS), 0.01),
        'w_exp_gate': nrm(ks[19], (DEPTH, N_EXPERTS, D, D_EXPERT), D ** -0.5),
        'w_exp_up': nrm(ks[20], (DEPTH, N_EXPERTS, D, D_EXPERT), D ** -0.5),
        'w_exp_down': nrm(ks[21], (DEPTH, N_EXPERTS, D_EXPERT, D), D_EXPERT ** -0.5),
        'final_g': 1.0 + nrm(ks[22], (D,), 0.02),
    }

def reference(x, c, ctx, c_ctx, w_mod, b_mod, norm1_g, norm2_g, w_in, rpb_a, w_pool, pool_scale,
              sink_c, w_branch, w_out, w_router_group, b_router_group, w_router_expert,
              b_router_expert, w_exp_gate, w_exp_up, w_exp_down, final_g):
    B, S, D = x.shape
    Lc = ctx.shape[1]
    sl = _in_slices()
    ang_r, ang_c = axial_rope_angles(S)
    z = ctx
    for l in range(DEPTH):
        last = l == DEPTH - 1
        mx = adaln_modulation(c[:, None, :], w_mod[l], b_mod[l])
        mz = adaln_modulation(c_ctx[None, None, :], w_mod[l], b_mod[l])

        hx = modulate(rms_norm(x, norm1_g[l]), mx[0], mx[1])
        hz = modulate(rms_norm(z, norm1_g[l]), mz[0], mz[1])
        px_all = hx @ w_in[l]
        px = {n: px_all[..., s] for n, s in sl.items()}
        if last:
            pz = {n: hz @ w_in[l][:, sl[n]] for n in ('a_k', 'a_v', 'c_k', 'c_v')}
        else:
            pz_all = hz @ w_in[l]
            pz = {n: pz_all[..., s] for n, s in sl.items()}
        kz_a, vz_a = split_heads(pz['a_k']), split_heads(pz['a_v'])
        kz_c, vz_c = split_heads(pz['c_k']), split_heads(pz['c_v'])

        ya = neighborhood_attention(split_heads(px['a_q']), split_heads(px['a_k']),
                                    split_heads(px['a_v']), kz_a, vz_a, rpb_a[l])
        yb = multiscale_pool(px['b_u'], w_pool[l], pool_scale[l])
        q_c = axial_rotary(split_heads(px['c_q']), ang_r, ang_c)
        k_c = axial_rotary(split_heads(px['c_k']), ang_r, ang_c)
        yc = windowed_gqa_sink(q_c, k_c, split_heads(px['c_v']), kz_c, vz_c, sink_c[l])
        x = x + mx[2] * merge_branches(ya, yb, yc, px['gates'], w_branch[l], w_out[l])

        if not last:
            za = context_attention(split_heads(pz['a_q'])[:, :, :, None, :], kz_a, vz_a, None)
            zb = multiscale_pool(pz['b_u'], w_pool[l], pool_scale[l])
            zq_c = split_heads(pz['c_q']).reshape(B, Lc, SWA_KV_HEADS, SWA_GROUP, HEAD_DIM)
            zc = context_attention(zq_c, kz_c, vz_c, sink_c[l].reshape(SWA_KV_HEADS, SWA_GROUP))
            z = z + mz[2] * merge_branches(za.reshape(B, Lc, NA_WIDTH), zb, zc.reshape(B, Lc, SWA_WIDTH),
                                           pz['gates'], w_branch[l], w_out[l])

        moe_params = (w_router_group[l], b_router_group[l], w_router_expert[l], b_router_expert[l],
                      w_exp_gate[l], w_exp_up[l], w_exp_down[l])
        hx = modulate(rms_norm(x, norm2_g[l]), mx[3], mx[4])
        if last:
            fx = hierarchical_moe(hx.reshape(B * S, D), *moe_params).reshape(B, S, D)
        else:
            hz = modulate(rms_norm(z, norm2_g[l]), mz[3], mz[4])
            tokens = jnp.concatenate([hz.reshape(B * Lc, D), hx.reshape(B * S, D)], axis=0)
            f = hierarchical_moe(tokens, *moe_params)
            z = z + mz[5] * f[:B * Lc].reshape(B, Lc, D)
            fx = f[B * Lc:].reshape(B, S, D)
        x = x + mx[5] * fx
    return rms_norm(x, final_g)


_drawn_inputs = setup_inputs


def setup_inputs(seed=0):
    import zlib

    import numpy as np

    out = dict(_drawn_inputs(seed))
    spreads = {}
    factors = {'sink_c': 8.0, 'b_router_expert': 4.341, 'final_g': 8.031, 'b_router_group': 2.904}
    for name, (base, spread) in spreads.items():
        noise = np.random.default_rng([zlib.crc32(name.encode()), seed]).standard_normal(out[name].shape)
        drawn = base * np.exp(spread * noise) if base else spread * noise
        out[name] = jnp.asarray(drawn.astype(out[name].dtype))
    for name, factor in factors.items():
        out[name] = (out[name] * factor).astype(out[name].dtype)
    return out
```

```python
from contextlib import ExitStack

import concourse.bass as bass
from concourse import mybir

F32 = mybir.dt.float32
BF16 = mybir.dt.bfloat16
I32 = mybir.dt.int32
U32 = mybir.dt.uint32
ALU = mybir.AluOpType
ACT = mybir.ActivationFunctionType
AX = mybir.AxisListType.X

P = 128
D = 1024
KC = D // P
SEQ = 256
NTOK = 2 * SEQ
DEPTH = 2
HD = 64
HEADS = 8
ROWS, GW = 4, 64
SCALE = HD ** -0.5
IN_TILES = 5888 // P
COLS = {"aq": 0, "ak": 4, "av": 8, "u": 12, "cq": 16, "ck": 20, "cv": 21, "g": 22}
N_MOD = 6
EPS = 1e-6
NEG = -1e30
RPB_REPEATS = GW + 1
NG, EPG = 4, 8
NE = NG * EPG
FE = 512
BLK = 64
LATENT, CONTEXT = slice(0, SEQ), slice(SEQ, NTOK)

CONST_COLS = {"ident": 128, "rot": 128, "mean": 128, "cos": 256, "sin": 256, "colok": 64, "colneg": 64,
              "edge": 64, "small": 32, "swa": 512, "tri": 128, "iota": 512}
CONST_AT, _at = {}, 0
for _k, _w in CONST_COLS.items():
    CONST_AT[_k] = (_at, _at + _w)
    _at += _w
NCONST = _at


class Signal:

    def __init__(self, sem, counts):
        self.sem, self.counts, self.n, self.seen = sem, counts, 0, {}

    def tick(self, *step, by=1):
        self.n += by
        self.seen[step] = self.n
        return by

    def at(self, *step):
        return self.counts[step] if self.counts else 1


def mixer_jobs(l):
    both = l == 0
    jobs = [("tile", "ck", 0), ("tile", "cv", 0), ("rope", "ck", 0)]
    for c in range(4):
        jobs.append(("tile", "cq", c))
        if c:
            jobs.append(("rope", "cq", c - 1))
    jobs += [("tile", "u", 0), ("rope", "cq", 3), ("tile", "u", 1)]
    tiles = {"c": [("tile", k, c) for k in ("u", "aq", "ak", "av") for c in range(4)][2:],
             "a": [("tile", "g", c) for c in range(16)]}
    mods = [(0, n) for n in range(4, 12)] + [(1, n) for n in range(12)] if both else []
    pending = None
    for kind in ("c", "a"):
        heads = [(s, h) for s in (("x", "z") if both else ("x",)) for h in range(HEADS)]
        per = 16 // len(heads)
        for i, (s, h) in enumerate(heads):
            jobs.append(("qk", kind, s, h))
            if pending:
                jobs.append(pending)
                pending = None
            jobs += tiles[kind][i * per:(i + 1) * per][:1]
            mod = mods.pop(0) if mods else None
            if mod:
                jobs.append(("modp",) + mod)
            jobs += tiles[kind][i * per:(i + 1) * per][1:]
            jobs.append(("tr", kind, s, h))
            if mod:
                jobs.append(("modt",) + mod)
            if kind == "a" and i == 4:
                jobs.append(("pool",))
            if h % 2:
                pending = ("pv", kind, s, h // 2)
    jobs.append(pending)
    if both:
        at = max(i for i, j in enumerate(jobs) if j[0] == "modt")
        jobs.insert(at + 1, ("prefetch",))
    else:
        jobs.insert(0, ("prefetch",))
    return jobs


def hybrid_block(nc, t, out, counts=None):
    signals = {}
    h_rows = nc.dram_tensor("h_rows", (NTOK, D), F32).ap()
    y_rows = nc.dram_tensor("y_rows", (3 * NTOK + BLK, D), F32).ap()
    w_branch = t["w_branch"].rearrange("l b k n -> l (b k) n")
    ctx = ExitStack()
    with ctx:
        def sb(name, shape, dt=F32):
            return ctx.enter_context(nc.sbuf_tensor(name, shape, dt))

        def signal(name):
            s = Signal(ctx.enter_context(nc.semaphore(name)), counts and counts[name])
            signals[name] = s
            return s

        xt = sb("xt", [P, KC, NTOK])
        ht = sb("ht", [P, KC, NTOK])
        arena = sb("arena", [P, 46 * 256])
        moe = sb("moe", [P, 96 * 256])
        ws = sb("ws", [P, 3, 8, P])
        aux = sb("aux", [P, 4, 512])
        mrow = sb("mrow", [P, 512])
        ident, rot, mean_w = sb("ident", [P, P]), sb("rot", [P, P]), sb("mean_w", [P, P])
        cos, sin = sb("cos", [P, SEQ]), sb("sin", [P, SEQ])
        colok, colneg = sb("colok", [P, GW]), sb("colneg", [P, GW])
        edge = sb("edge", [P, 4, 16])
        small = sb("small", [P, 32])
        tri_b, ones_b = sb("tri_b", [P, P], BF16), sb("ones_b", [P, P], BF16)
        cond = sb("cond", [P, KC, 32])
        colv = sb("colv", [P, 144])
        modv = sb("modv", [P, DEPTH, 2, N_MOD * KC])
        gain = sb("gain", [P, 2, 2, KC])
        half_gate = sb("half_gate", [P, 2, KC])
        sink = sb("sink", [P, DEPTH, HEADS])
        wr = sb("wr", [P, KC, NG + NE])
        br = sb("br", [P, NG + NE])
        stat = sb("stat", [P, 2, 16])
        eps = sb("eps", [P, 1])
        route_w = sb("route_w", [P, 2, 4])
        dest = sb("dest", [P, 2, 4], U32)
        slot_tok = sb("slot_tok", [BLK, NTOK // BLK, NE], I32)
        n_of = sb("n_of", [1, NE], I32)
        start_of = sb("start_of", [1, NE], I32)
        idx = sb("idx", [BLK, 3], I32)
        ps = ctx.enter_context(nc.psum_tensor("ps", [P, 8, 512], F32))

        def part(base, kib, size, *dims, dt=F32):
            v = base[:, int(kib * 256):int((kib + size) * 256)]
            if dt is not F32:
                v = v.bitcast(dt)
            if len(dims) == 2:
                v = v.rearrange("p (a b) -> p a b", b=dims[1])
            if len(dims) == 3:
                v = v.rearrange("p (a b c) -> p a b c", b=dims[1], c=dims[2])
            return v

        aq, ak = part(arena, 0, 8, 4, NTOK), part(arena, 8, 8, 4, NTOK)
        av, u = part(arena, 16, 8, 4, 512), part(arena, 24, 8, 4, NTOK)
        cq, ck = part(arena, 32, 8, 4, NTOK), part(arena, 40, 4, 2, NTOK)
        cv = part(arena, 44, 2, 4, P)
        mt = part(arena, 8, 16, KC, NTOK)
        hr = part(arena, 0, 16, 4, D)
        xr = [part(arena, 16 + 4 * i, 4) for i in range(2)]
        xg = [part(arena, 24 + 2 * i, 2, KC, BLK) for i in range(2)]
        xr_o, xg_o = part(arena, 28, 4), part(arena, 32, 2, KC, BLK)
        hid = [part(arena, 34 + i, 1) for i in range(3)]
        hid_t = [part(arena, 37 + i, 1, 2, P) for i in range(3)]
        ysb = [part(arena, 40 + 2 * i, 2) for i in range(3)]
        yg = [[part(arena, 16 + 8 * i + 4 * k, 4) for k in range(2)] for i in range(2)]
        act_g = [aux[:, i, 0:256] for i in range(3)]
        ohp = aux[:, :, :].rearrange("p a b -> p (a b)").bitcast(BF16).rearrange("p (k t s) -> p k t s", k=2, t=4)
        r = part(arena, 24, 12)
        iota = part(arena, 40, 2)
        wgu = [moe[:, 48 * 256 * i:(48 * i + 32) * 256].rearrange("p (k g n) -> p k g n", k=KC, g=2) for i in range(2)]
        wd = [part(moe, 48 * i + 32, 16, 4, D) for i in range(2)]
        mw = [part(moe, 16 * i, 16, KC, 512) for i in range(3)]
        gates = part(moe, 48, 32, 16, NTOK)
        rows_in = part(moe, 48, 16, 4, D)
        vec_rows = part(moe, 80, 1, 2, P)
        cond_rows = part(moe, 82, 4)
        prob = [part(moe, 80 + 4 * i, 4, 2, 512) for i in range(2)]
        prob_t = [part(moe, 88 + 4 * i, 4, 4, SEQ) for i in range(2)]
        ck_raw, rt0, rt1 = prob[0][:, 0, :], prob[0][:, 1, 0:SEQ], prob[0][:, 1, SEQ:]
        sq, rs = [aux[:, i, :] for i in range(3)], aux[:, 3, :]
        swa = aux[:, 3, :].rearrange("p (q k) -> p q k", q=2)
        aux_flat = aux[:, :, :].rearrange("p a b -> p (a b)")
        pad = [aux_flat[:, i * 544:(i + 1) * 544].rearrange("p (s n) -> p s n", s=2) for i in range(2)]
        bias = [aux[:, i, :].rearrange("p (q r k) -> p q r k", q=2, r=ROWS) for i in range(4)]
        tile_bank, score_bank = [ps[:, i, :] for i in range(2)], ps[:, 2:4, :]
        prob_bank = ps[:, 4:6, :].rearrange("p b (k q) -> p (b k) q", q=SEQ)
        pv_bank, misc = ps[:, 6, :], ps[:, 7, :]

        names = """ident_in consts_in rows_in_done vecs_in router_in swa_in wst0 wst1 wst2 mwt0 mwt1 mwt2 bias0 bias1 bias2
            bias3 gu_in0 gu_in1 wd_in0 wd_in1 h_saved x_got0 x_got1 y_saved0 y_saved1 xo_got yo_saved yg_got0 yg_got1
            out_saved iota_in
            in_turned in_copied prep vec_ready cond_silu cond_turned cond_cols colv_ready sq_done mean_done rstd_sqrt rstd_done
            norm_mul norm_add tile_done tile_copied rope_done rope_out qk_done max_done exp_done
            scaled pt_done pt_copied_d pt_copied_a pv_done pv_copied modp_done modp_copied modt_done mod_summed mod_ready gains
            pool_pad pooled pool_done pool_copied bias_ready gate_done gate_tanh branch_done merged out_done added
            dchain achain pchain logits_done hturn_done hrow_copied r_exp r_onehot r_pos r_place r_tos r_tos_done routed
            idx_set xt_done xt_copied gu_done silu_done hid_done0 hid_done1 hidt_done hidt_copied down_done0 down_done1
            y_copied0 y_copied1 io_set xto_done xto_copied guo_done siluo_done hido_done hidto_done hidto_copied
            downo_done yo_copied comb comb_turned comb_added fin_scaled fin_turned fin_copied""".split()
        g = {n: signal(n) for n in names}
        ws_in = [g[f"wst{i}"] for i in range(3)]
        mw_in = [g[f"mwt{i}"] for i in range(3)]
        bias_in = [g[f"bias{i}"] for i in range(4)]
        gu_in, wd_in = [g["gu_in0"], g["gu_in1"]], [g["wd_in0"], g["wd_in1"]]
        x_got, y_saved = [g["x_got0"], g["x_got1"]], [g["y_saved0"], g["y_saved1"]]
        yg_got = [g["yg_got0"], g["yg_got1"]]
        hid_done, down_done = [g["hid_done0"], g["hid_done1"]], [g["down_done0"], g["down_done1"]]
        y_copied = [g["y_copied0"], g["y_copied1"]]

        def width(l):
            return NTOK if l == 0 else SEQ

        def streams(l):
            return [(0, LATENT), (1, CONTEXT)] if l == 0 else [(0, LATENT)]

        def kt_of(kind, h):
            return (ck[HD * (h % 2):HD * (h % 2) + HD, h // 4, :] if kind == "c"
                    else ak[HD * (h % 2):HD * (h % 2) + HD, h // 2, :])

        def q_of(kind):
            return cq if kind == "c" else aq

        def v_of(kind, h, tile):
            return (cv[:, tile, HD * (h // 4):HD * (h // 4) + HD] if kind == "c"
                    else av[:, tile, HD * h:HD * h + HD])

        def stream_items(l):
            items = []
            for j in mixer_jobs(l):
                if j[0] == "tile":
                    a = COLS[j[1]] + j[2]
                    items.append((t["w_in"][l, :, a * P:(a + 1) * P].rearrange("(k p) n -> p k n", p=P), 8, j))
                if j[0] == "pool":
                    items.append((t["w_pool"][l].rearrange("g c e -> c g e"), 4, j))
                if j[0] in ("modp", "prefetch"):
                    items.append((None, 0, j))
            for n in range(KC):
                a = COLS["g"] + 16 + n
                items.append((t["w_in"][l, :, a * P:(a + 1) * P].rearrange("(k p) n -> p k n", p=P), 8, ("g2", n)))
                for b0, m in ((0, 8), (8, 4)):
                    items.append((w_branch[l, b0 * P:(b0 + m) * P, n * P:(n + 1) * P].rearrange("(k p) n -> p k n", p=P),
                                  m, ("wb", b0, n)))
            for n in range(KC):
                items.append((t["w_out"][l, :, n * P:(n + 1) * P].rearrange("(k p) n -> p k n", p=P), 8, ("wo", n)))
            return items

        def plan_banks():
            order = [("in", c) for c in range(KC)]
            for l in range(DEPTH):
                order.append((l, "n1"))
                for j in mixer_jobs(l):
                    if j[0] == "tile":
                        order.append((l,) + j[1:])
                    if j[0] == "pool":
                        order += [(l, "pool", gr) for gr in range(4)]
                order += [(l, "g2", n) for n in range(KC)] + [(l, "wo", n) for n in range(KC)] + [(l, "n2")]
            order.append((DEPTH - 1, "fin"))
            return {step: i % 2 for i, step in enumerate(order)}

        tile_banks = plan_banks()

        def ws_release(l, job):
            if job[0] == "tile":
                return g["tile_done"], (l, job[1], job[2])
            if job[0] == "pool":
                return g["pool_done"], (l, 3)
            if job[0] == "g2":
                return g["gate_done"], (l, job[1])
            if job[0] == "wb":
                return g["branch_done"], (l, job[2])
            return g["out_done"], (l, job[1])

        block = ctx.enter_context(nc.Block())

        @block.sync
        def _(sp):
            def const(name, dst):
                a, b = CONST_AT[name]
                sp.dma_start(dst, t["consts"][:, a:b]).then_inc(g["consts_in"].sem, g["consts_in"].tick(name, by=16))

            for i, (src, c) in enumerate((("x", 0), ("ctx", 2))):
                sp.dma_start(rows_in[:, c:c + 2, :], t[src][0].rearrange("(t p) d -> p t d", p=P)) \
                    .then_inc(g["rows_in_done"].sem, g["rows_in_done"].tick(i, by=16))
            a, b = CONST_AT["ident"]
            sp.dma_start(ident[:, :], t["consts"][:, a:b]).then_inc(g["ident_in"].sem, g["ident_in"].tick(by=16))
            sp.dma_start(vec_rows[0:96, 0, :], t["b_mod"].rearrange("l (a p) -> (l a) p", p=P)) \
                .then_inc(g["vecs_in"].sem, g["vecs_in"].tick(0, by=16))
            for i, (name, n) in enumerate((("norm1_g", 16), ("norm2_g", 16), ("final_g", 8), ("pool_scale", 8))):
                src = t[name].rearrange("(a p) -> a p", p=P) if name == "final_g" else t[name].rearrange("l (a p) -> (l a) p", p=P)
                at = (0, 16, 32, 40)[i]
                sp.dma_start(vec_rows[at:at + n, 1, :], src).then_inc(g["vecs_in"].sem, g["vecs_in"].tick(1 + i, by=16))
            sp.dma_start(cond_rows[0:1, :], t["c"]).then_inc(g["vecs_in"].sem, g["vecs_in"].tick(5, by=16))
            sp.dma_start(cond_rows[1:2, :], t["c_ctx"].rearrange("(a d) -> a d", a=1)) \
                .then_inc(g["vecs_in"].sem, g["vecs_in"].tick(6, by=16))
            sp.dma_start(sink[:, :, :].rearrange("p l h -> p (l h)"),
                         t["sink_c"].rearrange("l h -> (l h)").partition_broadcast(P)) \
                .then_inc(g["vecs_in"].sem, g["vecs_in"].tick(7, by=16))

            mods = []

            def load_mod(l, n):
                i = len(mods)
                mods.append((l, n))
                if i >= 3:
                    sp.wait_ge(g["modp_done"].sem, g["modp_done"].at(*mods[i - 3]))
                sp.dma_start(mw[i % 3], t["w_mod"][l, :, n * 512:(n + 1) * 512].rearrange("(k p) n -> p k n", p=P)) \
                    .then_inc(mw_in[i % 3].sem, mw_in[i % 3].tick(l, n, by=16))

            def load_expert(l, e_src, slot):
                for k in range(2):
                    w = (t["w_exp_gate"], t["w_exp_up"])[k]
                    sp.dma_start(wgu[slot][:, :, k, :], e_src(w).rearrange("(k p) n -> p k n", p=P)) \
                        .then_inc(gu_in[slot].sem, 16)
                sp.dma_start(wd[slot], e_src(t["w_exp_down"]).rearrange("(k p) n -> p k n", p=P)) \
                    .then_inc(wd_in[slot].sem, 16)

            for n in range(3):
                load_mod(0, n)
            for name, dst in (("rot", rot), ("mean", mean_w), ("cos", cos), ("sin", sin), ("colok", colok),
                              ("colneg", colneg), ("small", small)):
                const(name, dst[:, :])
            const("edge", edge[:, :, :].rearrange("p a b -> p (a b)"))
            const("tri", arena[:, 0:P])
            load_mod(0, 3)
            held = []
            for l in range(DEPTH):
                for src, m, job in stream_items(l):
                    if job[0] == "modp":
                        load_mod(job[1], job[2])
                    elif job[0] == "prefetch":
                        if l == 0:
                            sp.wait_ge(g["modp_done"].sem, g["modp_done"].at(1, 11))
                        else:
                            sp.wait_ge(down_done[0].sem, 16 * l)
                        load_expert(l, lambda w: w[l, 0], 0)
                    else:
                        slot = len(held) % 3
                        if len(held) >= 3:
                            last, step = held[-3]
                            sp.wait_ge(last.sem, last.at(*step))
                        sp.dma_start(ws[:, slot, 0:m, :], src).then_inc(ws_in[slot].sem, ws_in[slot].tick(l, job, by=16))
                        held.append(ws_release(l, job))
                sp.wait_ge(g["merged"].sem, g["merged"].at(l, KC - 1))
                if l:
                    sp.wait_ge(down_done[1].sem, 16 * l)
                load_expert(l, lambda w: w[l, 1], 1)
                with sp.Fori(1, NE // 2) as i:
                    for slot in range(2):
                        sp.wait_ge(down_done[slot].sem, 16 * l + i)
                        load_expert(l, lambda w: w[l, bass.ds(2 * i + slot, 1)].rearrange("a k n -> (a k) n"), slot)
            sp.wait_ge(g["fin_copied"].sem, g["fin_copied"].at(1))
            sp.wait_ge(g["prep"].sem, g["prep"].at("fin", 1))
            sp.dma_start(out[0].rearrange("(t p) d -> p t d", p=P), hr[:, 0:2, :]) \
                .then_inc(g["out_saved"].sem, g["out_saved"].tick(0, by=16))
            sp.wait_ge(g["out_saved"].sem, 16)

        @block.tensor
        def _(pe):
            free = {}

            def claim(bank):
                if bank in free:
                    s, step = free.pop(bank)
                    pe.wait_ge(s.sem, s.at(*step))

            def next_tile_bank(*step):
                claim(tile_banks[step])
                return tile_banks[step]

            n_ws = [0]

            def weights(l, job):
                slot = n_ws[0] % 3
                n_ws[0] += 1
                pe.wait_ge(ws_in[slot].sem, ws_in[slot].at(l, job))
                return ws[:, slot]

            pe.wait_ge(g["ident_in"].sem, 16)
            pe.wait_ge(g["rows_in_done"].sem, 32)
            for c in range(KC):
                bank = next_tile_bank("in", c)
                for tile in range(4):
                    mm = pe.transpose(ps[:, bank, tile * P:(tile + 1) * P], rows_in[:, tile, c * P:(c + 1) * P], ident[:, :])
                mm.then_inc(g["in_turned"].sem, g["in_turned"].tick(c))
                free[bank] = (g["prep"], ("xt", c)) if c % 2 else (g["in_copied"], (c,))
            pe.wait_ge(g["vecs_in"].sem, 16 * 8)
            pe.transpose(misc[:, 0:96], vec_rows[0:96, 0, :], ident[0:96, 0:96])
            pe.transpose(misc[:, 96:144], vec_rows[0:48, 1, :], ident[0:48, 0:48])
            pe.wait_ge(g["cond_silu"].sem, g["cond_silu"].at(0))
            for c in range(KC):
                mm = pe.transpose(misc[:, 144 + 2 * c:146 + 2 * c], cond_rows[0:2, c * P:(c + 1) * P], ident[0:2, 0:2])
            mm.then_inc(g["cond_turned"].sem, g["cond_turned"].tick(0))
            free[7] = (g["cond_cols"], (0,))
            pe.wait_ge(g["cond_cols"].sem, g["cond_cols"].at(0))

            n_mod = [0]

            def modp(l, n):
                i = n_mod[0]
                n_mod[0] += 1
                claim(7)
                pe.wait_ge(mw_in[i % 3].sem, mw_in[i % 3].at(l, n))
                for k in range(KC):
                    q = k % 4
                    mm = pe.matmul(misc[32 * q:32 * q + 32, :], cond[:, k, :], mw[i % 3][:, k, :], start=(k < 4), stop=(k >= 4))
                mm.then_inc(g["modp_done"].sem, g["modp_done"].tick(l, n))
                free[7] = (g["modp_copied"], (l, n))

            def modt(l, n):
                claim(7)
                for q in range(4):
                    mm = pe.transpose(misc[:, q * P:(q + 1) * P], mrow[:, q * P:(q + 1) * P], ident[:, :])
                mm.then_inc(g["modt_done"].sem, g["modt_done"].tick(l, n))
                free[7] = (g["mod_summed"], (l, n))

            for n in range(4):
                modp(0, n)
                modt(0, n)

            def mean(l, which):
                bank = next_tile_bank(l, which)
                w = width(l) if which != "n1" else NTOK
                for c in range(KC):
                    pe.wait_ge(g["sq_done"].sem, g["sq_done"].at(l, which, c))
                    mm = pe.matmul(ps[:, bank, 0:w], mean_w[:, :], sq[c % 3][:, 0:w], start=(c == 0), stop=(c == KC - 1))
                    mm.then_inc(g["mean_done"].sem, g["mean_done"].tick(l, which, c))
                free[bank] = (g["rstd_sqrt"], (l, which))

            for l in range(DEPTH):
                w_all = width(l)
                if l == 0:
                    pe.wait_ge(g["consts_in"].sem, g["consts_in"].at("tri"))
                mean(l, "n1")
                for j in mixer_jobs(l):
                    if j[0] == "tile":
                        kind, c = j[1:]
                        w = weights(l, j)
                        bank = next_tile_bank(l, kind, c)
                        if kind == "ck":
                            pe.wait_ge(g["norm_add"].sem, g["norm_add"].at(l, "n1", KC - 1))
                        if kind in ("av", "cv"):
                            for tile in range(4):
                                for k in range(KC):
                                    mm = pe.matmul(ps[:, bank, tile * P:(tile + 1) * P], ht[:, k, tile * P:(tile + 1) * P],
                                                   w[:, k, :], start=(k == 0), stop=(k == KC - 1))
                        else:
                            cols = NTOK if kind in ("ak", "ck") else w_all
                            for k in range(KC):
                                mm = pe.matmul(ps[:, bank, 0:cols], w[:, k, :], ht[:, k, 0:cols], start=(k == 0), stop=(k == KC - 1))
                        mm.then_inc(g["tile_done"].sem, g["tile_done"].tick(l, kind, c))
                        free[bank] = (g["tile_copied"], (l, kind, c))
                    elif j[0] == "rope":
                        kind, c = j[1:]
                        claim(7)
                        pe.wait_ge(g["tile_copied"].sem, g["tile_copied"].at(l, kind, c))
                        src = ck_raw[:, 0:SEQ] if kind == "ck" else cq[:, c, 0:SEQ]
                        pe.matmul(misc[:, 0:SEQ], rot[:, :], src, start=True, stop=True) \
                            .then_inc(g["rope_done"].sem, g["rope_done"].tick(l, kind, c))
                        free[7] = (g["rope_out"], (l, kind, c))
                    elif j[0] == "qk":
                        kind, s, h = j[1:]
                        claim("s")
                        if kind == "c":
                            if s == "x" and h == 0:
                                pe.wait_ge(g["rope_out"].sem, g["rope_out"].at(l, "ck", 0))
                            if s == "x" and h < HEADS:
                                if h // 2 < 3:
                                    pe.wait_ge(g["rope_out"].sem, g["rope_out"].at(l, "cq", h // 2))
                                else:
                                    pe.wait_ge(g["rope_out"].sem, g["rope_out"].at(l, "cq", 3))
                            pe.wait_ge(g["tile_copied"].sem, g["tile_copied"].at(l, "cq", 3))
                        else:
                            pe.wait_ge(g["tile_copied"].sem, g["tile_copied"].at(l, "av", 3))
                        rows = slice(HD * (h % 2), HD * (h % 2) + HD)
                        keys = slice(0, NTOK) if s == "x" else CONTEXT
                        q0 = 0 if s == "x" else SEQ
                        n = NTOK if s == "x" else SEQ
                        for qt in range(2):
                            mm = pe.matmul(score_bank[:, qt, 0:n], q_of(kind)[rows, h // 2, q0 + qt * P:q0 + (qt + 1) * P],
                                           kt_of(kind, h)[:, keys], start=True, stop=True)
                        mm.then_inc(g["qk_done"].sem, g["qk_done"].tick(l, kind, s, h))
                        free["s"] = (g["exp_done"], (l, kind, s, h))
                    elif j[0] == "tr":
                        kind, s, h = j[1:]
                        claim("t")
                        claim("t2")
                        pe.wait_ge(g["scaled"].sem, g["scaled"].at(l, kind, s, h))
                        for tile in range(4 if s == "x" else 2):
                            for qt in range(2):
                                mm = pe.transpose(prob_bank[:, tile, qt * P:(qt + 1) * P],
                                                  prob[h % 2][:, qt, tile * P:(tile + 1) * P], ident[:, :])
                            if tile == 1:
                                mm.then_inc(g["pt_done"].sem, g["pt_done"].tick(l, kind, s, h, 0))
                            if tile == 3:
                                mm.then_inc(g["pt_done"].sem, g["pt_done"].tick(l, kind, s, h, 1))
                        free["t"] = (g["pt_copied_a"], (l, kind, s, h))
                        if s == "x":
                            free["t2"] = (g["pt_copied_d"], (l, kind, s, h))
                    elif j[0] == "pv":
                        kind, s, pair = j[1:]
                        claim(6)
                        pe.wait_ge(g["pt_copied_a"].sem, g["pt_copied_a"].at(l, kind, s, 2 * pair + 1))
                        if s == "x":
                            pe.wait_ge(g["pt_copied_d"].sem, g["pt_copied_d"].at(l, kind, s, 2 * pair + 1))
                        n = 4 if s == "x" else 2
                        for tile in range(n):
                            for hh in range(2):
                                mm = pe.matmul(pv_bank[HD * hh:HD * hh + HD, 0:SEQ], v_of(kind, 2 * pair + hh, tile + (4 - n)),
                                               prob_t[hh][:, tile, :], start=(tile == 0), stop=(tile == n - 1))
                        mm.then_inc(g["pv_done"].sem, g["pv_done"].tick(l, kind, s, pair))
                        free[6] = (g["pv_copied"], (l, kind, s, pair))
                    elif j[0] == "modp":
                        modp(*j[1:])
                    elif j[0] == "modt":
                        modt(*j[1:])
                    elif j[0] == "pool":
                        w = weights(l, j)
                        for gr in range(4):
                            bank = next_tile_bank(l, "pool", gr)
                            pe.wait_ge(g["pooled"].sem, g["pooled"].at(l, gr))
                            mm = pe.matmul(ps[:, bank, 0:w_all], w[:, gr, :], u[:, gr, 0:w_all], start=True, stop=True)
                            mm.then_inc(g["pool_done"].sem, g["pool_done"].tick(l, gr))
                            free[bank] = (g["pool_copied"], (l, gr))
                for key in ("s", "t", "t2", 6, 7):
                    claim(key)
                pe.wait_ge(g["pool_copied"].sem, g["pool_copied"].at(l, 3))
                pe.wait_ge(g["pv_copied"].sem, g["pv_copied"].at(l, "a", "z" if l == 0 else "x", 3))
                ys = (aq, u, cq)
                for n in range(KC):
                    w = weights(l, ("g2", n))
                    bank = next_tile_bank(l, "g2", n)
                    for k in range(KC):
                        mm = pe.matmul(ps[:, bank, 0:w_all], w[:, k, :], ht[:, k, 0:w_all], start=(k == 0), stop=(k == KC - 1))
                    mm.then_inc(g["gate_done"].sem, g["gate_done"].tick(l, n))
                    free[bank] = (g["gate_tanh"], (l, n))
                    for b in range(3):
                        if b != 1:
                            w = weights(l, ("wb", 0 if b == 0 else 8, n))
                        if b == 0 and n >= 2:
                            pe.wait_ge(g["merged"].sem, g["merged"].at(l, n - 2))
                        for k in range(4):
                            mm = pe.matmul(ps[:, 2 + 3 * (n % 2) + b, 0:w_all], w[:, (4 * b + k) % 8, :], ys[b][:, k, 0:w_all],
                                           start=(k == 0), stop=(k == 3))
                    mm.then_inc(g["branch_done"].sem, g["branch_done"].tick(l, n))
                for n in range(KC):
                    w = weights(l, ("wo", n))
                    bank = next_tile_bank(l, "wo", n)
                    if n == 0:
                        pe.wait_ge(g["merged"].sem, g["merged"].at(l, KC - 1))
                    for k in range(KC):
                        mm = pe.matmul(ps[:, bank, 0:w_all], w[:, k, :], mt[:, k, 0:w_all], start=(k == 0), stop=(k == KC - 1))
                    mm.then_inc(g["out_done"].sem, g["out_done"].tick(l, n))
                    free[bank] = (g["added"], (l, n))
                nt = w_all // P
                mean(l, "n2")
                pe.wait_ge(g["norm_add"].sem, g["norm_add"].at(l, "n2", KC - 1))
                pe.wait_ge(g["router_in"].sem, g["router_in"].at(l, 3))
                for tile in range(nt):
                    for k in range(KC):
                        mm = pe.matmul(misc[:, tile * 64:tile * 64 + 36], ht[:, k, tile * P:(tile + 1) * P], wr[:, k, :],
                                       start=(k == 0), stop=(k == KC - 1))
                mm.then_inc(g["logits_done"].sem, g["logits_done"].tick(l))
                for tile in range(nt):
                    for half in range(2):
                        bank = 2 + (2 * tile + half) % 4
                        claim(bank)
                        for c in range(4):
                            mm = pe.transpose(ps[:, bank, c * P:(c + 1) * P], ht[:, 4 * half + c, tile * P:(tile + 1) * P], ident[:, :])
                        mm.then_inc(g["hturn_done"].sem, g["hturn_done"].tick(l, tile, half))
                        free[bank] = (g["hrow_copied"], (l, tile, half))
                msk = r[:, 1024:1024 + 64].bitcast(BF16).rearrange("p (t e) -> p t e", e=NE)
                pe.wait_ge(g["r_onehot"].sem, g["r_onehot"].at(l))
                for tile in range(nt):
                    for before in range(tile):
                        pe.matmul(ps[:, 6, tile * NE:(tile + 1) * NE], ones_b[:, :], msk[:, before, :], start=(before == 0), stop=False)
                    pe.matmul(ps[:, 6, tile * NE:(tile + 1) * NE], tri_b[:, :], msk[:, tile, :], start=(tile == 0), stop=True)
                for tile in range(nt):
                    mm = pe.matmul(ps[:, 6, 4 * NE:5 * NE], ones_b[:, :], msk[:, tile, :], start=(tile == 0), stop=(tile == nt - 1))
                mm.then_inc(g["r_pos"].sem, g["r_pos"].tick(l))
                rk = [r[:, 1152 + 128 * k:1280 + 128 * k].bitcast(BF16).rearrange("p (t a e) -> p t (a e)", t=4, a=2) for k in range(2)]
                nb = w_all // BLK
                pe.wait_ge(g["r_place"].sem, g["r_place"].at(l))
                for b in range(nb):
                    for i in range(2 * nt):
                        k, tile = i // nt, i % nt
                        mm = pe.matmul(misc[0:BLK, b * 64:(b + 1) * 64], ohp[:, k, tile, b * BLK:(b + 1) * BLK], rk[k][:, tile, :],
                                       start=(i == 0), stop=(i == 2 * nt - 1))
                mm.then_inc(g["r_tos"].sem, g["r_tos"].tick(l))
                for bank in range(8):
                    claim(bank)
                pe.wait_ge(g["routed"].sem, g["routed"].at(l))

                def turn_x(dst_bank, rows, sem):
                    for c in range(KC):
                        mm = pe.transpose(ps[:, dst_bank, c * BLK:(c + 1) * BLK], rows[0:BLK, c * P:(c + 1) * P], ident[0:BLK, 0:BLK])
                    mm.then_inc(sem, 1)

                def gate_up(bank, xs, w, sem):
                    for k in range(KC):
                        for j in range(2):
                            mm = pe.matmul(ps[BLK * j:BLK * j + BLK, bank, :].rearrange("p (g n) -> p g n", g=2), xs[:, k, :],
                                           w[:, k, :, 256 * j:256 * j + 256], start=(k == 0), stop=(k == KC - 1))
                    mm.then_inc(sem, 1)

                def turn_h(bank, src, sem):
                    for c in range(2):
                        mm = pe.transpose(ps[:, bank, c * P:(c + 1) * P], src[:, c * P:(c + 1) * P], ident[:, :])
                    mm.then_inc(sem, 1)

                def down(bank, src, w, sem):
                    for k in range(4):
                        for j in range(2):
                            mm = pe.matmul(ps[BLK * j:BLK * j + BLK, bank, :], src[:, k % 2, BLK * (k // 2):BLK * (k // 2) + BLK],
                                           w[:, k, 512 * j:512 * j + 512], start=(k == 0), stop=(k == 3))
                    mm.then_inc(sem, 1)

                if l == 0:
                    n_more = pe.alloc_register("pe_more")
                    pe.reg_mov(n_more, 0)
                    pe.sem_inc(g["xto_done"].sem, 1)
                with pe.Fori(0, NE // 2) as i:
                    for s in range(2):
                        e, done = 2 * i + s, NE * l + 2 * i + s
                        mine = 16 * l + i
                        pe.wait_ge(x_got[s].sem, (mine + 1) * 16)
                        pe.nop(nofuse=True)
                        turn_x(0, xr[s], g["xt_done"].sem)
                        pe.wait_ge(g["xt_copied"].sem, done + 1)
                        pe.wait_ge(gu_in[s].sem, (mine + 1) * 32)
                        gate_up(2 + s, xg[s], wgu[s], g["gu_done"].sem)
                        n = pe.value_load(n_of[0:1, bass.ds(e, 1)], min_val=0, max_val=NTOK)
                        pe.wait_ge(wd_in[s].sem, (mine + 1) * 16)
                        pe.nop(nofuse=True)
                        with pe.Fori(1, nb) as b:
                            with pe.If(n > b * BLK):
                                more = pe.snap(n_more, min_val=0, max_val=64)
                                pe.wait_ge(g["xo_got"].sem, more * 16 + 16)
                                pe.nop(nofuse=True)
                                turn_x(7, xr_o, g["xto_done"].sem)
                                pe.wait_ge(g["xto_copied"].sem, more + 1)
                                pe.wait_ge(g["yo_copied"].sem, more + 1)
                                gate_up(6, xg_o, wgu[s], g["guo_done"].sem)
                                pe.wait_ge(g["hido_done"].sem, more + 1)
                                turn_h(7, hid[2], g["hidto_done"].sem)
                                pe.wait_ge(g["hidto_copied"].sem, more + 1)
                                down(6, hid_t[2], wd[s], g["downo_done"].sem)
                                pe.reg_add(n_more, n_more, 1)
                            pe.nop(nofuse=True)
                        pe.wait_ge(hid_done[s].sem, mine + 2)
                        turn_h(1, hid[s], g["hidt_done"].sem)
                        pe.wait_ge(g["hidt_copied"].sem, done + 1)
                        pe.wait_ge(y_copied[s].sem, mine + 1)
                        down(4 + s, hid_t[s], wd[s], down_done[s].sem)
                pe.wait_ge(g["comb"].sem, g["comb"].at(l, nt - 1))
                pe.wait_ge(y_copied[1].sem, 16 * (l + 1) + 1)
                for c in range(KC):
                    bank = 2 + c % 2
                    claim(bank)
                    for tile in range(nt):
                        mm = pe.transpose(ps[:, bank, tile * P:(tile + 1) * P], hr[:, tile, c * P:(c + 1) * P], ident[:, :])
                    mm.then_inc(g["comb_turned"].sem, g["comb_turned"].tick(l, c))
                    free[bank] = (g["comb_added"], (l, c))
                for bank in (2, 3):
                    claim(bank)
            mean(DEPTH - 1, "fin")
            for tile in range(2):
                for half in range(2):
                    for c in range(4):
                        pe.wait_ge(g["fin_scaled"].sem, g["fin_scaled"].at(4 * half + c))
                        mm = pe.transpose(ps[:, 2 + 2 * tile + half, c * P:(c + 1) * P],
                                          ht[:, 4 * half + c, tile * P:(tile + 1) * P], ident[:, :])
                    mm.then_inc(g["fin_turned"].sem, g["fin_turned"].tick(tile, half))

        @block.scalar
        def _(act):
            def chain(ins):
                ins.then_inc(g["achain"].sem, g["achain"].tick())
                act.wait_ge(g["achain"].sem, g["achain"].n)

            for c in range(1, KC, 2):
                act.wait_ge(g["in_turned"].sem, g["in_turned"].at(c))
                nc.scalar.activation(xt[:, c, :], tile_bank[c % 2], ACT.Copy).then_inc(g["prep"].sem, g["prep"].tick("xt", c))
            act.wait_ge(g["vecs_in"].sem, 16 * 8)
            nc.scalar.activation(cond_rows[0:2, :], cond_rows[0:2, :], ACT.Silu).then_inc(g["cond_silu"].sem, g["cond_silu"].tick(0))

            def modp_copy(l, n):
                act.wait_ge(g["modp_done"].sem, g["modp_done"].at(l, n))
                prev = (l, n - 1) if n else (l - 1, 11)
                if prev[0] >= 0:
                    act.wait_ge(g["modt_done"].sem, g["modt_done"].at(*prev))
                nc.scalar.activation(mrow[:, :], misc, ACT.Copy).then_inc(g["modp_copied"].sem, g["modp_copied"].tick(l, n))

            for n in range(4):
                modp_copy(0, n)

            def squares(l, which):
                w = width(l) if which != "n1" else NTOK
                if which == "n1" and l == 0:
                    act.wait_ge(g["in_copied"].sem, g["in_copied"].at(KC - 2))
                    act.wait_ge(g["prep"].sem, g["prep"].at("xt", KC - 1))
                elif which == "n1":
                    act.wait_ge(g["comb_added"].sem, g["comb_added"].at(l - 1, KC - 1))
                elif which == "n2":
                    act.wait_ge(g["added"].sem, g["added"].at(l, KC - 1))
                else:
                    act.wait_ge(g["comb_added"].sem, g["comb_added"].at(l, KC - 1))
                for c in range(KC):
                    if c >= 3:
                        act.wait_ge(g["mean_done"].sem, g["mean_done"].at(l, which, c - 3))
                    nc.scalar.activation(sq[c % 3][:, 0:w], xt[:, c, 0:w], ACT.Square) \
                        .then_inc(g["sq_done"].sem, g["sq_done"].tick(l, which, c))
                act.wait_ge(g["mean_done"].sem, g["mean_done"].at(l, which, KC - 1))
                bank = tile_banks[(l, which)]
                nc.scalar.activation(rs[:, 0:w], ps[:, bank, 0:w], ACT.Sqrt, bias=eps[:, 0:1]) \
                    .then_inc(g["rstd_sqrt"].sem, g["rstd_sqrt"].tick(l, which))

            def shift(l, which, first):
                for c in range(KC):
                    act.wait_ge(g["norm_mul"].sem, g["norm_mul"].at(l, which, c))
                    both = streams(0) if which == "n1" else streams(l)
                    for s, cols in both:
                        ins = nc.scalar.activation(ht[:, c, cols], ht[:, c, cols], ACT.Identity,
                                                   bias=modv[:, l, s, first + c:first + c + 1])
                    ins.then_inc(g["norm_add"].sem, g["norm_add"].tick(l, which, c))

            for l in range(DEPTH):
                w_all = width(l)
                if l == 0:
                    act.wait_ge(g["vec_ready"].sem, g["vec_ready"].at("eps"))
                squares(l, "n1")
                shift(l, "n1", 0)
                for j in mixer_jobs(l):
                    if j[0] == "tile":
                        kind, c = j[1:]
                        act.wait_ge(g["tile_done"].sem, g["tile_done"].at(l, kind, c))
                        bank = tile_banks[(l, kind, c)]
                        src = ps[:, bank, :]
                        if kind in ("aq", "cq"):
                            dst = (aq if kind == "aq" else cq)[:, c, 0:w_all]
                            ins = nc.scalar.activation(dst, src[:, 0:w_all], ACT.Copy, scale=SCALE)
                        elif kind == "ak":
                            ins = nc.scalar.activation(ak[:, c, :], src, ACT.Copy)
                        elif kind == "u":
                            ins = nc.scalar.activation(u[:, c, 0:w_all], src[:, 0:w_all], ACT.Copy)
                        elif kind == "ck":
                            ins = nc.scalar.activation(ck_raw, src, ACT.Copy)
                        elif kind == "cv":
                            ins = nc.scalar.activation(cv, src.rearrange("p (t n) -> p t n", n=P), ACT.Copy)
                        elif kind == "av":
                            ins = nc.scalar.activation(av[:, :, c * P:(c + 1) * P], src.rearrange("p (t n) -> p t n", n=P), ACT.Copy)
                        else:
                            ins = nc.scalar.activation(gates[:, c, 0:w_all], src[:, 0:w_all], ACT.Tanh, scale=0.5)
                        ins.then_inc(g["tile_copied"].sem, g["tile_copied"].tick(l, kind, c))
                    elif j[0] == "qk":
                        kind, s, h = j[1:]
                        act.wait_ge(g["max_done"].sem, g["max_done"].at(l, kind, s, h))
                        st, pb = stat[:, h % 2], prob[h % 2]
                        for qt in range(2):
                            if s == "x":
                                nc.scalar.activation(pb[:, qt, 0:SEQ], pb[:, qt, 0:SEQ], ACT.Exp, bias=st[:, qt:qt + 1],
                                                     accum_out=st[:, 2 + qt:3 + qt])
                                ins = nc.scalar.activation(pb[:, qt, SEQ:NTOK], score_bank[:, qt, SEQ:NTOK], ACT.Exp,
                                                           bias=st[:, qt:qt + 1], accum_out=st[:, 4 + qt:5 + qt])
                            else:
                                ins = nc.scalar.activation(pb[:, qt, 0:SEQ], score_bank[:, qt, 0:SEQ], ACT.Exp,
                                                           bias=st[:, qt:qt + 1], accum_out=st[:, 2 + qt:3 + qt])
                        if kind == "c":
                            ins = nc.scalar.activation(st[:, 6:8], st[:, 0:2], ACT.Exp, bias=sink[:, l, h:h + 1])
                        ins.then_inc(g["exp_done"].sem, g["exp_done"].tick(l, kind, s, h))
                    elif j[0] == "tr":
                        kind, s, h = j[1:]
                        act.wait_ge(g["pt_done"].sem, g["pt_done"].at(l, kind, s, h, 0))
                        nc.scalar.activation(prob_t[h % 2][:, 0:2, :], prob_bank[:, 0:2, :], ACT.Copy) \
                            .then_inc(g["pt_copied_a"].sem, g["pt_copied_a"].tick(l, kind, s, h))
                    elif j[0] == "pv":
                        kind, s, pair = j[1:]
                        act.wait_ge(g["pv_done"].sem, g["pv_done"].at(l, kind, s, pair))
                        cols = LATENT if s == "x" else CONTEXT
                        nc.scalar.activation(q_of(kind)[:, pair, cols], pv_bank[:, 0:SEQ], ACT.Copy) \
                            .then_inc(g["pv_copied"].sem, g["pv_copied"].tick(l, kind, s, pair))
                    elif j[0] == "modp":
                        modp_copy(*j[1:])
                    elif j[0] == "pool":
                        for gr in range(4):
                            act.wait_ge(g["pool_done"].sem, g["pool_done"].at(l, gr))
                            nc.scalar.activation(u[:, gr, 0:w_all], ps[:, tile_banks[(l, "pool", gr)], 0:w_all], ACT.Copy,
                                                 scale=colv[:, 136 + 4 * l + gr:137 + 4 * l + gr]) \
                                .then_inc(g["pool_copied"].sem, g["pool_copied"].tick(l, gr))
                for n in range(KC):
                    act.wait_ge(g["gate_done"].sem, g["gate_done"].at(l, n))
                    if n >= 2:
                        act.wait_ge(g["merged"].sem, g["merged"].at(l, n - 2))
                    nc.scalar.activation(aux[:, n % 2, 0:w_all], ps[:, tile_banks[(l, "g2", n)], 0:w_all], ACT.Tanh, scale=0.5) \
                        .then_inc(g["gate_tanh"].sem, g["gate_tanh"].tick(l, n))
                squares(l, "n2")
                shift(l, "n2", 3 * KC)
                nt = w_all // P
                for tile in range(nt):
                    for half in range(2):
                        act.wait_ge(g["hturn_done"].sem, g["hturn_done"].at(l, tile, half))
                        nc.scalar.activation(hr[:, tile, 512 * half:512 * half + 512], ps[:, 2 + (2 * tile + half) % 4, :], ACT.Copy) \
                            .then_inc(g["hrow_copied"].sem, g["hrow_copied"].tick(l, tile, half))
                    act.wait_ge(g["hrow_copied"].sem, g["hrow_copied"].at(l, tile, 1))
                    act.dma_start(h_rows[tile * P:(tile + 1) * P, :], hr[:, tile, :]) \
                        .then_inc(g["h_saved"].sem, g["h_saved"].tick(l, tile, by=16))
                for step in range(2):
                    act.wait_ge(g["r_exp"].sem, g["r_exp"].at(l, "in", step))
                    buf = r[:, 256:256 + 4 * nt] if step == 0 else r[:, 288:288 + nt]
                    nc.scalar.activation(buf, buf, ACT.Exp).then_inc(g["r_tos_done"].sem, g["r_tos_done"].tick(l, step))
                act.wait_ge(g["routed"].sem, g["routed"].at(l))
                nb = w_all // BLK

                def save_rows(src, row, signal):
                    for j in range(2):
                        act.dma_start(y_rows[bass.ds(row, BLK), j * 512:(j + 1) * 512], src[BLK * j:BLK * j + BLK, :]) \
                            .then_inc(signal.sem, 16)

                if l == 0:
                    n_more = act.alloc_register("act_more")
                    act.reg_mov(n_more, 0)
                    for s in range(2):
                        act.sem_inc(y_copied[s].sem, 1)
                        act.sem_inc(y_saved[s].sem, 32)
                    act.sem_inc(g["yo_copied"].sem, 1)
                    act.sem_inc(g["yo_saved"].sem, 32)
                with act.Fori(0, NE // 2) as i:
                    for s in range(2):
                        e, done, mine = 2 * i + s, NE * l + 2 * i + s, 16 * l + i
                        other = mine + 1 if s == 0 else mine + 2
                        act.wait_ge(g["gu_done"].sem, done + 1)
                        act.wait_ge(hid_done[s].sem, mine + 1)
                        nc.scalar.activation(act_g[s], ps[:, 2 + s, 0:256], ACT.Silu).then_inc(g["silu_done"].sem, 1)
                        n = act.value_load(n_of[0:1, bass.ds(e, 1)], min_val=0, max_val=NTOK)
                        row = act.value_load(start_of[0:1, bass.ds(e, 1)], min_val=0, max_val=2 * NTOK)
                        act.wait_ge(y_saved[1 - s].sem, other * 32)
                        with act.Fori(1, nb) as b:
                            with act.If(n > b * BLK):
                                more = act.snap(n_more, min_val=0, max_val=64)
                                act.wait_ge(g["guo_done"].sem, more + 1)
                                nc.scalar.activation(act_g[2], ps[:, 6, 0:256], ACT.Silu).then_inc(g["siluo_done"].sem, 1)
                                act.wait_ge(g["downo_done"].sem, more + 1)
                                act.wait_ge(g["yo_saved"].sem, more * 32 + 32)
                                nc.scalar.activation(ysb[2], ps[:, 6, :], ACT.Copy).then_inc(g["yo_copied"].sem, 1)
                                act.wait_ge(g["yo_copied"].sem, more + 2)
                                save_rows(ysb[2], act.snap(row + b * BLK, min_val=0, max_val=2 * NTOK), g["yo_saved"])
                                act.reg_add(n_more, n_more, 1)
                            act.nop()
                        act.wait_ge(down_done[s].sem, mine + 1)
                        act.wait_ge(y_saved[s].sem, mine * 32 + 32)
                        nc.scalar.activation(ysb[s], ps[:, 4 + s, :], ACT.Copy).then_inc(y_copied[s].sem, 1)
                        act.wait_ge(y_copied[s].sem, mine + 2)
                        act.wait_ge(g["yo_saved"].sem, act.snap(n_more, min_val=0, max_val=64) * 32 + 32)
                        save_rows(ysb[s], row, y_saved[s])
                act.wait_ge(y_saved[0].sem, 32 * 16 * (l + 1) + 32)
                act.wait_ge(y_saved[1].sem, 32 * 16 * (l + 1) + 32)
                act.wait_ge(g["yo_saved"].sem, act.snap(n_more, min_val=0, max_val=64) * 32 + 32)
                act.sem_inc(g["prep"].sem, g["prep"].tick("y", l))
            squares(DEPTH - 1, "fin")
            for tile in range(2):
                act.wait_ge(g["fin_turned"].sem, g["fin_turned"].at(tile, 1))
                nc.scalar.activation(hr[:, tile, 512:1024], ps[:, 3 + 2 * tile, :], ACT.Copy) \
                    .then_inc(g["prep"].sem, g["prep"].tick("fin", tile))

        @block.vector
        def _(dve):
            v = nc.vector

            def chain(ins):
                ins.then_inc(g["dchain"].sem, g["dchain"].tick())
                dve.wait_ge(g["dchain"].sem, g["dchain"].n)

            v.memset(eps[:, :], EPS).then_inc(g["vec_ready"].sem, g["vec_ready"].tick("eps"))
            chain(v.memset(cond[:, :, :], 0.0))
            chain(v.memset(ones_b[:, :], 1.0))
            for c in range(0, KC, 2):
                dve.wait_ge(g["in_turned"].sem, g["in_turned"].at(c))
                v.tensor_copy(xt[:, c, :], tile_bank[c % 2]).then_inc(g["in_copied"].sem, g["in_copied"].tick(c))
            dve.wait_ge(g["cond_turned"].sem, g["cond_turned"].at(0))
            chain(v.tensor_copy(colv[:, :], misc[:, 0:144]))
            v.tensor_copy(cond[:, :, 0:2], misc[:, 144:160].rearrange("p (k s) -> p k s", s=2)) \
                .then_inc(g["cond_cols"].sem, g["cond_cols"].tick(0))
            dve.wait_ge(g["consts_in"].sem, g["consts_in"].at("tri"))
            chain(v.tensor_copy(tri_b[:, :], arena[:, 0:P]))

            def mod_sum(l, n):
                dve.wait_ge(g["modt_done"].sem, g["modt_done"].at(l, n))
                cols = slice(4 * n, 4 * n + 4)
                v.tensor_reduce(modv[:, l, :, cols], misc.rearrange("p (q j r) -> p r q j", q=4, j=4)[:, 0:2], AX, ALU.add) \
                    .then_inc(g["mod_summed"].sem, g["mod_summed"].tick(l, n))
                dve.wait_ge(g["mod_summed"].sem, g["mod_summed"].at(l, n))
                bm = colv[:, 48 * l + 4 * n:48 * l + 4 * n + 4].unsqueeze(1).broadcast_to([P, 2, 4])
                v.tensor_tensor(modv[:, l, :, cols], modv[:, l, :, cols], bm, ALU.add) \
                    .then_inc(g["mod_ready"].sem, g["mod_ready"].tick(l, n))

            def gains(l, norm):
                dve.wait_ge(g["mod_ready"].sem, g["mod_ready"].at(l, 11 if l or norm else 3))
                first = KC * (1 + 3 * norm)
                for s in range(2):
                    ins = v.scalar_tensor_tensor(gain[:, norm, s, :], modv[:, l, s, first:first + KC], 1.0,
                                                 colv[:, 96 + 16 * norm + KC * l:96 + 16 * norm + KC * (l + 1)], ALU.add, ALU.mult)
                if norm:
                    chain(v.tensor_scalar(half_gate[:, :, :], modv[:, l, :, 2 * KC:3 * KC], 0.5, None, ALU.mult))
                else:
                    chain(ins)

            def scale_norm(l, which):
                w = width(l) if which != "n1" else NTOK
                dve.wait_ge(g["rstd_sqrt"].sem, g["rstd_sqrt"].at(l, which))
                v.reciprocal(rs[:, 0:w], rs[:, 0:w]).then_inc(g["rstd_done"].sem, g["rstd_done"].tick(l, which))
                dve.wait_ge(g["rstd_done"].sem, g["rstd_done"].at(l, which))
                for c in range(KC):
                    if which == "fin":
                        v.scalar_tensor_tensor(ht[:, c, 0:w], xt[:, c, 0:w], colv[:, 128 + c:129 + c], rs[:, 0:w], ALU.mult, ALU.mult) \
                            .then_inc(g["fin_scaled"].sem, g["fin_scaled"].tick(c))
                        continue
                    for s, cols in (streams(0) if which == "n1" else streams(l)):
                        ins = v.scalar_tensor_tensor(ht[:, c, cols], xt[:, c, cols], gain[:, int(which == "n2"), s, c:c + 1],
                                                     rs[:, cols], ALU.mult, ALU.mult)
                    ins.then_inc(g["norm_mul"].sem, g["norm_mul"].tick(l, which, c))

            for n in range(4):
                mod_sum(0, n)
            for l in range(DEPTH):
                w_all = width(l)
                gains(l, 0)
                if l:
                    gains(l, 1)
                scale_norm(l, "n1")
                last_tr = {}
                for j in mixer_jobs(l):
                    if j[0] == "rope":
                        kind, c = j[1:]
                        dve.wait_ge(g["rope_done"].sem, g["rope_done"].at(l, kind, c))
                        src = ck_raw[:, 0:SEQ] if kind == "ck" else cq[:, c, 0:SEQ]
                        v.tensor_tensor(rt0, misc[:, 0:SEQ], sin[:, :], ALU.mult)
                        chain(v.tensor_tensor(rt1, src, cos[:, :], ALU.mult))
                        if kind == "cq":
                            ins = v.tensor_tensor(src, rt0, rt1, ALU.add)
                        else:
                            for kv in range(2):
                                rows = slice(HD * kv, HD * kv + HD)
                                for half in range(2):
                                    to = slice(HD * half, HD * half + HD)
                                    v.tensor_copy(ck[to, kv, CONTEXT], ck_raw[rows, CONTEXT])
                                    ins = v.tensor_tensor(ck[to, kv, LATENT], rt0[rows], rt1[rows], ALU.add)
                        ins.then_inc(g["rope_out"].sem, g["rope_out"].tick(l, kind, c))
                        dve.wait_ge(g["rope_out"].sem, g["rope_out"].at(l, kind, c))
                    elif j[0] == "qk":
                        kind, s, h = j[1:]
                        st, pb = stat[:, h % 2], prob[h % 2]
                        if h % 2 in last_tr:
                            dve.wait_ge(g["pt_done"].sem, g["pt_done"].at(*last_tr[h % 2]))
                        if s == "x" and h == 0:
                            if kind == "c":
                                dve.wait_ge(g["swa_in"].sem, g["swa_in"].at(l))
                                dve.wait_ge(g["rope_out"].sem, g["rope_out"].at(l, "cq", 3))
                        if kind == "a" and s == "x":
                            dve.wait_ge(g["bias_ready"].sem, g["bias_ready"].at(l, h))
                        dve.wait_ge(g["qk_done"].sem, g["qk_done"].at(l, kind, s, h))
                        if s == "x":
                            for qt in range(2):
                                add = swa[:, qt, :] if kind == "c" else bias[h % 4][:, qt].rearrange("p r k -> p (r k)")
                                v.tensor_tensor_reduce(pb[:, qt, 0:SEQ], score_bank[:, qt, 0:SEQ], add, 1.0, NEG, ALU.add, ALU.max,
                                                       st[:, 8 + qt:9 + qt])
                            chain(v.tensor_reduce(st[:, 10:12], score_bank[:, :, SEQ:NTOK], AX, ALU.max))
                            chain(v.tensor_tensor(st[:, 8:10], st[:, 8:10], st[:, 10:12], ALU.max))
                        else:
                            chain(v.tensor_reduce(st[:, 8:10], score_bank[:, :, 0:SEQ], AX, ALU.max))
                        if kind == "c":
                            ins = v.tensor_scalar(st[:, 0:2], st[:, 8:10], sink[:, l, h:h + 1], -1.0, ALU.max, ALU.mult)
                        else:
                            ins = v.tensor_scalar(st[:, 0:2], st[:, 8:10], -1.0, None, ALU.mult)
                        ins.then_inc(g["max_done"].sem, g["max_done"].tick(l, kind, s, h))
                        dve.wait_ge(g["exp_done"].sem, g["exp_done"].at(l, kind, s, h))
                        total = st[:, 2:4]
                        if s == "x":
                            chain(v.tensor_tensor(st[:, 12:14], total, st[:, 4:6], ALU.add))
                            total = st[:, 12:14]
                        if kind == "c":
                            chain(v.tensor_tensor(st[:, 12:14], total, st[:, 6:8], ALU.add))
                            total = st[:, 12:14]
                        chain(v.reciprocal(st[:, 14:16], total))
                        n = NTOK if s == "x" else SEQ
                        for qt in range(2):
                            ins = v.tensor_scalar(pb[:, qt, 0:n], pb[:, qt, 0:n], st[:, 14 + qt:15 + qt], None, ALU.mult)
                        ins.then_inc(g["scaled"].sem, g["scaled"].tick(l, kind, s, h))
                    elif j[0] == "tr":
                        kind, s, h = j[1:]
                        if s == "x":
                            dve.wait_ge(g["pt_done"].sem, g["pt_done"].at(l, kind, s, h, 1))
                            v.tensor_copy(prob_t[h % 2][:, 2:4, :], prob_bank[:, 2:4, :]) \
                                .then_inc(g["pt_copied_d"].sem, g["pt_copied_d"].tick(l, kind, s, h))
                        last_tr[h % 2] = (l, kind, s, h, 1 if s == "x" else 0)
                    elif j[0] == "modt":
                        mod_sum(*j[1:])
                if l == 0:
                    gains(0, 1)
                for n in range(KC):
                    dve.wait_ge(g["branch_done"].sem, g["branch_done"].at(l, n))
                    dve.wait_ge(g["gate_tanh"].sem, g["gate_tanh"].at(l, n))
                    if n:
                        dve.wait_ge(g["merged"].sem, g["merged"].at(l, n - 1))
                    b0 = 2 + 3 * (n % 2)
                    for b, (gt, to) in enumerate(((gates[:, n], mt[:, n]), (gates[:, 8 + n], aux[:, 2]), (aux[:, n % 2], aux[:, 3]))):
                        ins = v.scalar_tensor_tensor(to[:, 0:w_all], gt[:, 0:w_all], 1.0, ps[:, b0 + b, 0:w_all], ALU.add, ALU.mult)
                    chain(ins)
                    chain(v.tensor_tensor(mt[:, n, 0:w_all], mt[:, n, 0:w_all], aux[:, 2, 0:w_all], ALU.add))
                    v.tensor_tensor(mt[:, n, 0:w_all], mt[:, n, 0:w_all], aux[:, 3, 0:w_all], ALU.add) \
                        .then_inc(g["merged"].sem, g["merged"].tick(l, n))
                for n in range(KC):
                    dve.wait_ge(g["out_done"].sem, g["out_done"].at(l, n))
                    for s, cols in streams(l):
                        ins = v.scalar_tensor_tensor(xt[:, n, cols], ps[:, tile_banks[(l, "wo", n)], cols], half_gate[:, s, n:n + 1],
                                                     xt[:, n, cols], ALU.mult, ALU.add)
                    ins.then_inc(g["added"].sem, g["added"].tick(l, n))
                dve.wait_ge(g["added"].sem, g["added"].at(l, KC - 1))
                scale_norm(l, "n2")
                nt, nb = w_all // P, w_all // BLK
                dve.wait_ge(g["logits_done"].sem, g["logits_done"].at(l))

                def tmp(at, *dims):
                    a = r[:, at:at + dims[0] * (dims[1] if len(dims) > 1 else 1)]
                    return a.rearrange("p (a b) -> p a b", b=dims[1]) if len(dims) > 1 else a

                def spread(a, m):
                    return a.unsqueeze(2).broadcast_to([P, nt, m])

                lg = tmp(0, nt, 36)
                gmax, gtop, emax, etop = tmp(144, nt), tmp(148, nt), tmp(152, nt), tmp(156, nt)
                p_grp, w_sum, emax2 = tmp(160, nt), tmp(164, nt), tmp(168, nt)
                gexp, goh, gsc = tmp(256, nt, 4), tmp(608, nt, 4), tmp(624, nt, 4)
                gap = tmp(288, nt)
                le, le2, esc = tmp(448, nt, 8), tmp(576, nt, 8), tmp(544, nt, 8)
                oh = [tmp(480, nt, 8), tmp(512, nt, 8)]
                ohe = [tmp(640, nt, NE), tmp(768, nt, NE)]
                wide = tmp(896, nt, NE)
                msk = r[:, 1024:1088].bitcast(BF16).rearrange("p (t e) -> p t e", e=NE)
                rk = [r[:, 1152 + 128 * k:1280 + 128 * k].bitcast(BF16).rearrange("p (t a e) -> p t a e", t=4, a=2) for k in range(2)]
                cnt, incl, start, one = tmp(1408, NE), tmp(1440, NE), tmp(1472, NE), tmp(1504, NE)
                pos = tmp(1536, nt, NE)
                pos_k = [tmp(1664, nt), tmp(1668, nt)]
                dest_k = [tmp(1680, nt), tmp(1684, nt)]
                tos = r[0:BLK, 1792:2304].rearrange("p (b a e) -> p b a e", a=2, e=NE)
                down4, down8 = small[:, 0:4], small[:, 4:12]

                dve.wait_ge(g["router_in"].sem, g["router_in"].at(l, 3))
                chain(v.tensor_tensor(lg, misc[:, 0:64 * nt].rearrange("p (t n) -> p t n", n=64)[:, :, 0:36],
                                      br[:, :].unsqueeze(1).broadcast_to([P, nt, 36]), ALU.add))

                def top_one_hot(values, best, score, order, top, out, m):
                    chain(v.tensor_reduce(best, values, AX, ALU.max))
                    chain(v.tensor_tensor(score, values, spread(best, m), ALU.is_ge))
                    chain(v.tensor_tensor(score, score, order.unsqueeze(1).broadcast_to([P, nt, m]), ALU.mult))
                    chain(v.tensor_reduce(top, score, AX, ALU.max))
                    chain(v.tensor_tensor(out, score, spread(top, m), ALU.is_equal))

                top_one_hot(lg[:, :, 0:4], gmax, gsc, down4, gtop, goh, 4)
                v.tensor_tensor(gexp, lg[:, :, 0:4], spread(gmax, 4), ALU.subtract) \
                    .then_inc(g["r_exp"].sem, g["r_exp"].tick(l, "in", 0))
                chain(v.tensor_tensor(wide.rearrange("p t (g i) -> p t g i", i=8), lg[:, :, 4:36].rearrange("p t (g i) -> p t g i", i=8),
                                      goh.unsqueeze(3).broadcast_to([P, nt, 4, 8]), ALU.mult))
                chain(v.tensor_reduce(le, wide.rearrange("p t (g i) -> p t i g", i=8), AX, ALU.add))
                top_one_hot(le, emax, esc, down8, etop, oh[0], 8)
                chain(v.scalar_tensor_tensor(le2, oh[0], NEG, le, ALU.mult, ALU.add))
                top_one_hot(le2, emax2, esc, down8, etop, oh[1], 8)
                v.tensor_tensor(gap, emax2, emax, ALU.subtract).then_inc(g["r_exp"].sem, g["r_exp"].tick(l, "in", 1))
                for k in range(2):
                    chain(v.tensor_tensor(ohe[k].rearrange("p t (g i) -> p t g i", i=8), goh.unsqueeze(3).broadcast_to([P, nt, 4, 8]),
                                          oh[k].unsqueeze(2).broadcast_to([P, nt, 4, 8]), ALU.mult))
                v.tensor_tensor(msk[:, 0:nt], ohe[0], ohe[1], ALU.add).then_inc(g["r_onehot"].sem, g["r_onehot"].tick(l))
                dve.wait_ge(g["r_tos_done"].sem, g["r_tos_done"].at(l, 1))
                chain(v.tensor_reduce(p_grp, gexp, AX, ALU.add))
                chain(v.reciprocal(p_grp, p_grp))
                chain(v.tensor_scalar(w_sum, gap, 1.0, None, ALU.add))
                chain(v.reciprocal(w_sum, w_sum))
                chain(v.tensor_tensor(route_w[:, 0, 0:nt], p_grp, w_sum, ALU.mult))
                chain(v.tensor_tensor(route_w[:, 1, 0:nt], route_w[:, 0, 0:nt], gap, ALU.mult))
                chain(v.memset(one, 1.0))
                dve.wait_ge(g["r_pos"].sem, g["r_pos"].at(l))
                chain(v.tensor_copy(pos, ps[:, 6, 0:nt * NE].rearrange("p (t e) -> p t e", e=NE)))
                chain(v.tensor_copy(cnt, ps[:, 6, 4 * NE:5 * NE]))
                chain(v.tensor_tensor_scan(incl, one, cnt, 0.0, ALU.mult, ALU.add))
                chain(v.tensor_tensor(start, incl, cnt, ALU.subtract))
                chain(v.tensor_copy(n_of[:, :], cnt[0:1]))
                chain(v.tensor_copy(start_of[:, :], start[0:1]))
                dve.wait_ge(g["iota_in"].sem, g["iota_in"].at(l))
                for k in range(2):
                    chain(v.tensor_tensor(wide, ohe[k], pos, ALU.mult))
                    chain(v.tensor_reduce(pos_k[k], wide, AX, ALU.add))
                    chain(v.tensor_tensor(wide, ohe[k], start.unsqueeze(1).broadcast_to([P, nt, NE]), ALU.mult))
                    chain(v.tensor_reduce(dest_k[k], wide, AX, ALU.add))
                    chain(v.tensor_tensor(dest[:, k, 0:nt], dest_k[k], pos_k[k], ALU.add))
                    for tile in range(nt):
                        v.tensor_scalar(ohp[:, k, tile, 0:w_all], iota[:, 0:w_all], pos_k[k][:, tile:tile + 1], None, ALU.is_equal)
                    v.tensor_scalar(rk[k][:, 0:nt, 0, :], ohe[k], small[:, 12:13], None, ALU.mult)
                    ins = v.tensor_tensor(rk[k][:, 0:nt, 1, :], ohe[k], spread(small[:, 16:16 + nt], NE), ALU.mult)
                ins.then_inc(g["r_place"].sem, g["r_place"].tick(l))
                dve.wait_ge(g["r_tos"].sem, g["r_tos"].at(l))
                chain(v.tensor_copy(tos[:, 0:nb], misc[0:BLK, 0:64 * nb].rearrange("p (b a e) -> p b a e", a=2, e=NE)))
                v.scalar_tensor_tensor(slot_tok[:, 0:nb, :], tos[:, 0:nb, 1, :], float(P), tos[:, 0:nb, 0, :], ALU.mult, ALU.add) \
                    .then_inc(g["routed"].sem, g["routed"].tick(l))

                if l == 0:
                    n_more = dve.alloc_register("dve_more")
                    dve.reg_mov(n_more, 0)
                    for s in range(2):
                        dve.sem_inc(hid_done[s].sem, 1)
                with dve.Fori(0, NE // 2) as i:
                    for s in range(2):
                        e, done, mine = 2 * i + s, NE * l + 2 * i + s, 16 * l + i
                        dve.wait_ge(g["xt_done"].sem, done + 1)
                        v.tensor_copy(xg[s], ps[:, 0, :].rearrange("p (k n) -> p k n", n=BLK)).then_inc(g["xt_copied"].sem, 1)
                        dve.wait_ge(g["silu_done"].sem, done + 1)
                        v.tensor_tensor(hid[s], act_g[s], ps[:, 2 + s, 256:512], ALU.mult).then_inc(hid_done[s].sem, 1)
                        n = dve.value_load(n_of[0:1, bass.ds(e, 1)], min_val=0, max_val=NTOK)
                        with dve.Fori(1, nb) as b:
                            with dve.If(n > b * BLK):
                                more = dve.snap(n_more, min_val=0, max_val=64)
                                dve.wait_ge(g["xto_done"].sem, more + 2)
                                v.tensor_copy(xg_o, ps[:, 7, :].rearrange("p (k n) -> p k n", n=BLK)).then_inc(g["xto_copied"].sem, 1)
                                dve.wait_ge(g["siluo_done"].sem, more + 1)
                                v.tensor_tensor(hid[2], act_g[2], ps[:, 6, 256:512], ALU.mult).then_inc(g["hido_done"].sem, 1)
                                dve.wait_ge(g["hidto_done"].sem, more + 1)
                                v.tensor_copy(hid_t[2], ps[:, 7, 0:256].rearrange("p (c n) -> p c n", n=P)) \
                                    .then_inc(g["hidto_copied"].sem, 1)
                                dve.reg_add(n_more, n_more, 1)
                            dve.nop()
                        dve.wait_ge(g["hidt_done"].sem, done + 1)
                        v.tensor_copy(hid_t[s], ps[:, 1, 0:256].rearrange("p (c n) -> p c n", n=P)).then_inc(g["hidt_copied"].sem, 1)
                for tile in range(nt):
                    got = yg_got[tile % 2]
                    dve.wait_ge(got.sem, got.at(l, tile, 1))
                    chain(v.tensor_scalar(hr[:, tile, :], yg[tile % 2][0], route_w[:, 0, tile:tile + 1], None, ALU.mult))
                    v.scalar_tensor_tensor(hr[:, tile, :], yg[tile % 2][1], route_w[:, 1, tile:tile + 1], hr[:, tile, :], ALU.mult, ALU.add) \
                        .then_inc(g["comb"].sem, g["comb"].tick(l, tile))
                for c in range(KC):
                    dve.wait_ge(g["comb_turned"].sem, g["comb_turned"].at(l, c))
                    for s, cols in streams(l):
                        ins = v.scalar_tensor_tensor(xt[:, c, cols], ps[:, 2 + c % 2, cols], modv[:, l, s, 5 * KC + c:5 * KC + c + 1],
                                                     xt[:, c, cols], ALU.mult, ALU.add)
                    ins.then_inc(g["comb_added"].sem, g["comb_added"].tick(l, c))
                dve.wait_ge(g["comb_added"].sem, g["comb_added"].at(l, KC - 1))
            scale_norm(DEPTH - 1, "fin")
            for tile in range(2):
                dve.wait_ge(g["fin_turned"].sem, g["fin_turned"].at(tile, 0))
                v.tensor_copy(hr[:, tile, 0:512], ps[:, 2 + 2 * tile, :]).then_inc(g["fin_copied"].sem, g["fin_copied"].tick(tile))

        @block.gpsimd
        def _(pool):
            q = nc.gpsimd

            def chain(ins):
                ins.then_inc(g["pchain"].sem, g["pchain"].tick())
                pool.wait_ge(g["pchain"].sem, g["pchain"].n)

            for l in range(DEPTH):
                w_all = width(l)
                nt, nb = w_all // P, w_all // BLK
                if l:
                    pool.wait_ge(g["routed"].sem, g["routed"].at(l - 1))
                for i, (dst, src) in enumerate((
                        (wr[:, :, 0:NG], t["w_router_group"][l].rearrange("(k p) n -> p k n", p=P)),
                        (wr[:, :, NG:], t["w_router_expert"][l].rearrange("(k p) n -> p k n", p=P)),
                        (br[:, 0:NG], t["b_router_group"][l].partition_broadcast(P)),
                        (br[:, NG:], t["b_router_expert"][l].partition_broadcast(P)))):
                    pool.dma_start(dst, src).then_inc(g["router_in"].sem, g["router_in"].tick(l, i, by=16))
                pool.wait_ge(g["norm_mul"].sem, g["norm_mul"].at(l, "n1", KC - 1))
                a, b = CONST_AT["swa"]
                pool.dma_start(aux[:, 3, :], t["consts"][:, a:b]).then_inc(g["swa_in"].sem, g["swa_in"].tick(l, by=16))
                ns = w_all // SEQ
                uv = u.rearrange("p g (s n) -> p g s n", n=SEQ)
                n_pad = SEQ + 16
                pool.wait_ge(g["tile_copied"].sem, g["tile_copied"].at(l, "u", 3))
                for gr in range(4):
                    one, two = pad
                    chain(q.memset(one[:, 0:ns, :], 0.0))
                    chain(q.tensor_copy(one[:, 0:ns, 8:8 + SEQ], uv[:, gr, 0:ns, :]))
                    lo, hi, off = 1, n_pad, (1, 0)
                    reach = 1
                    for step in range(gr + 1):
                        back, ahead = ((1, 0), (1, 1), (2, 2), (4, 4))[step]
                        lo, hi = ((1, 272), (2, 271), (4, 269), (8, 264))[step]
                        chain(q.tensor_tensor(two[:, 0:ns, lo:hi], one[:, 0:ns, lo - back:hi - back], one[:, 0:ns, lo + ahead:hi + ahead], ALU.add))
                        one, two = two, one
                    chain(q.tensor_scalar(two[:, 0:ns, 8:8 + SEQ], one[:, 0:ns, 8:8 + SEQ], 1.0 / (2 << gr), None, ALU.mult))
                    for side, at in ((0, 8), (1, SEQ)):
                        e = edge[:, gr, 8 * side:8 * side + 8].unsqueeze(1).broadcast_to([P, ns, 8])
                        chain(q.tensor_tensor(two[:, 0:ns, at:at + 8], two[:, 0:ns, at:at + 8], e, ALU.mult))
                    q.tensor_tensor(uv[:, gr, 0:ns, :], two[:, 0:ns, 8:8 + SEQ], uv[:, gr, 0:ns, :], ALU.subtract) \
                        .then_inc(g["pooled"].sem, g["pooled"].tick(l, gr))
                    pool.wait_ge(g["pooled"].sem, g["pooled"].at(l, gr))
                rpb = t["rpb_a"]
                for h in range(HEADS):
                    if h >= 4:
                        pool.wait_ge(g["max_done"].sem, g["max_done"].at(l, "a", "x", h - 4))
                    elif h == 3:
                        pool.wait_ge(g["max_done"].sem, g["max_done"].at(l, "c", "x", HEADS - 1))
                    for qt in range(2):
                        for j in range(2):
                            row = 7 - (2 * qt + j)
                            at = ((l * HEADS + h) * 15 + row) * RPB_REPEATS * 31 + 15
                            src = bass.AP(rpb.tensor, at, [[30, GW], [RPB_REPEATS * 31, ROWS], [1, GW]])
                            pool.dma_start(bias[h % 4][GW * j:GW * j + GW, qt], src) \
                                .then_inc(bias_in[h % 4].sem, bias_in[h % 4].tick(l, h, qt, j, by=16))
                    pool.wait_ge(bias_in[h % 4].sem, bias_in[h % 4].at(l, h, 1, 1))
                    b8 = bias[h % 4].rearrange("p q r k -> p (q r) k")
                    chain(q.tensor_tensor(b8, b8, colok[:, :].unsqueeze(1).broadcast_to([P, 8, GW]), ALU.mult))
                    q.tensor_tensor(b8, b8, colneg[:, :].unsqueeze(1).broadcast_to([P, 8, GW]), ALU.add) \
                        .then_inc(g["bias_ready"].sem, g["bias_ready"].tick(l, h))
                pool.wait_ge(g["merged"].sem, g["merged"].at(l, KC - 1))
                a, b = CONST_AT["iota"]
                pool.dma_start(iota, t["consts"][:, a:b]).then_inc(g["iota_in"].sem, g["iota_in"].tick(l, by=16))
                pool.wait_ge(g["routed"].sem, g["routed"].at(l))
                pool.wait_ge(g["h_saved"].sem, g["h_saved"].at(l, nt - 1))
                flat = slot_tok[:, :, :].rearrange("p b e -> p (b e)")
                rows_ap = h_rows[0:w_all, :]

                def gather(dst, i, signal):
                    pool.nop(nofuse=True)
                    pool.indirect_dma_start(out=dst, out_offset=None, in_=rows_ap,
                                            in_offset=bass.IndirectOffsetOnAxis(ap=idx[:, i:i + 1], axis=0)) \
                        .then_inc(signal.sem, 16)

                if l == 0:
                    n_more = pool.alloc_register("pool_more")
                    pool.reg_mov(n_more, 0)
                with pool.Fori(0, NE // 2) as i:
                    for s in range(2):
                        e, done, mine = 2 * i + s, NE * l + 2 * i + s, 16 * l + i
                        pool.wait_ge(hid_done[s].sem, mine + 1)
                        q.tensor_copy(idx[:, s:s + 1], flat[:, bass.ds(e, 1)]).then_inc(g["idx_set"].sem, 1)
                        pool.wait_ge(g["idx_set"].sem, done + 1)
                        gather(xr[s][0:BLK, :], s, x_got[s])
                        n = pool.value_load(n_of[0:1, bass.ds(e, 1)], min_val=0, max_val=NTOK)
                        with pool.Fori(1, nb) as b:
                            with pool.If(n > b * BLK):
                                more = pool.snap(n_more, min_val=0, max_val=64)
                                pool.wait_ge(g["xto_done"].sem, more + 1)
                                q.tensor_copy(idx[:, 2:3], flat[:, bass.ds(b * NE + e, 1)]).then_inc(g["io_set"].sem, 1)
                                pool.wait_ge(g["io_set"].sem, more + 1)
                                gather(xr_o[0:BLK, :], 2, g["xo_got"])
                                pool.wait_ge(g["xo_got"].sem, more * 16 + 16)
                                pool.reg_add(n_more, n_more, 1)
                            pool.nop(nofuse=True)
                pool.wait_ge(g["prep"].sem, g["prep"].at("y", l))
                for tile in range(nt):
                    if tile >= 2:
                        pool.wait_ge(g["comb"].sem, g["comb"].at(l, tile - 2))
                    for k in range(2):
                        pool.indirect_dma_start(out=yg[tile % 2][k], out_offset=None, in_=y_rows[0:2 * w_all, :],
                                                in_offset=bass.IndirectOffsetOnAxis(ap=dest[:, k, tile:tile + 1], axis=0)) \
                            .then_inc(yg_got[tile % 2].sem, yg_got[tile % 2].tick(l, tile, k, by=16))
    return {n: s.seen for n, s in signals.items()}


def constants():
    import numpy as np

    c = np.zeros((P, NCONST), np.float32)

    def put(name, a):
        lo, hi = CONST_AT[name]
        a = np.asarray(a, np.float32).reshape(P, -1)
        c[:, lo:lo + a.shape[1]] = a

    p = np.arange(P)
    put("ident", np.eye(P))
    rot = np.zeros((P, P))
    for m in range(P):
        rot[m + 16 if m % 32 < 16 else m - 16, m] = -1.0 if m % 32 < 16 else 1.0
    put("rot", rot)
    put("mean", np.full((P, P), 1.0 / D))
    tok = np.arange(SEQ)
    inv = (np.float32(10000.0) ** (-np.arange(0, 32, 2, dtype=np.float32) / np.float32(32))).astype(np.float32)
    where = np.where((p % 64 < 32)[:, None], (tok // GW)[None, :], (tok % GW)[None, :]).astype(np.float32)
    ang = where * inv[p % 16][:, None]
    put("cos", np.cos(ang))
    put("sin", np.sin(ang))
    col = np.arange(GW)
    start = np.clip(col - 8, 0, GW - 16)
    ok = (col[None, :] >= start[:, None]) & (col[None, :] < start[:, None] + 16)
    ok = np.concatenate([ok, ok])
    put("colok", ok)
    put("colneg", np.where(ok, 0.0, NEG))
    edge = np.ones((4, 16))
    for g in range(4):
        w = 2 << g
        for i in range(8):
            edge[g, i] = w / min(w, i + w // 2)
            edge[g, 8 + i] = w / min(w, 8 - i + w // 2)
    put("edge", np.broadcast_to(edge.reshape(1, 64), (P, 64)))
    small = np.zeros((P, 32))
    small[:, 0:4] = 4 - np.arange(4)
    small[:, 4:12] = 8 - np.arange(8)
    small[:, 12] = p
    small[:, 16:20] = np.arange(4)
    put("small", small)
    key = np.arange(SEQ)
    put("swa", np.stack([np.where(np.abs(key[None, :] - (128 * q + p)[:, None]) <= 128, 0.0, NEG) for q in range(2)], 1))
    put("tri", p[:, None] < p[None, :])
    put("iota", np.broadcast_to(np.arange(512), (P, 512)))
    return c


_INS = ["x", "c", "ctx", "c_ctx", "w_mod", "b_mod", "norm1_g", "norm2_g", "w_in", "rpb_a", "w_pool", "pool_scale",
        "sink_c", "w_branch", "w_out", "w_router_group", "b_router_group", "w_router_expert", "b_router_expert",
        "w_exp_gate", "w_exp_up", "w_exp_down", "final_g"]


def kernel(**inputs):
    import numpy as _np
    import concourse.bacc as _bacc
    from concourse import mybir as _mybir
    from concourse.bass_utils import run_bass_kernel_spmd as _run

    arrays = {f"in_{n}_dram": _np.ascontiguousarray(inputs[n]) for n in _INS}
    arrays["in_rpb_a_dram"] = _np.tile(inputs["rpb_a"], (1, 1, 1, RPB_REPEATS))
    arrays["in_consts_dram"] = constants()

    def build(counts):
        nc = _bacc.Bacc("TRN2", target_bir_lowering=False, num_devices=1)
        t = {n[3:-5]: nc.dram_tensor(n, a.shape, _mybir.dt.from_np(a.dtype), kind="ExternalInput").ap() for n, a in arrays.items()}
        out = nc.dram_tensor("out_0_dram", (1, SEQ, D), F32, kind="ExternalOutput").ap()
        return nc, hybrid_block(nc, t, out, counts)

    _, counts = build(None)
    nc, _ = build(counts)
    r = _run(nc, [arrays], core_ids=[0])
    return r.results[0]["out_0_dram"]
```

```python
from contextlib import ExitStack

import concourse.bass as bass
from concourse import mybir

F32 = mybir.dt.float32
BF16 = mybir.dt.bfloat16
I32 = mybir.dt.int32
U32 = mybir.dt.uint32
ALU = mybir.AluOpType
ACT = mybir.ActivationFunctionType
AX = mybir.AxisListType.X

P = 128
D = 1024
KC = D // P
SEQ = 256
NTOK = 2 * SEQ
DEPTH = 2
HD = 64
HEADS = 8
ROWS, GW = 4, 64
SCALE = HD ** -0.5
IN_TILES = 5888 // P
COLS = {"aq": 0, "ak": 4, "av": 8, "u": 12, "cq": 16, "ck": 20, "cv": 21, "g": 22}
N_MOD = 6
EPS = 1e-6
NEG = -1e30
RPB_REPEATS = GW + 1
NG, EPG = 4, 8
NE = NG * EPG
FE = 512
BLK = 64
LATENT, CONTEXT = slice(0, SEQ), slice(SEQ, NTOK)

CONST_COLS = {"ident": 128, "rot": 128, "mean": 128, "cos": 256, "sin": 256, "colok": 64, "colneg": 64,
              "edge": 64, "small": 32, "swa": 512, "tri": 128, "slots1": 512}
CONST_AT, _at = {}, 0
for _k, _w in CONST_COLS.items():
    CONST_AT[_k] = (_at, _at + _w)
    _at += _w
NCONST = _at


class Signal:

    def __init__(self, sem, counts):
        self.sem, self.counts, self.n, self.seen = sem, counts, 0, {}

    def tick(self, *step, by=1):
        self.n += by
        self.seen[step] = self.n
        return by

    def at(self, *step):
        return self.counts[step] if self.counts else 1


def mixer_jobs(l):
    both = l == 0
    jobs = [("tile", "ck", 0), ("tile", "cv", 0), ("rope", "ck", 0)]
    for c in range(4):
        jobs.append(("tile", "cq", c))
        if c:
            jobs.append(("rope", "cq", c - 1))
    jobs += [("tile", "u", 0), ("rope", "cq", 3), ("tile", "u", 1)]
    tiles = {"c": [("tile", k, c) for k in ("u", "aq", "ak", "av") for c in range(4)][2:],
             "a": [("tile", "g", c) for c in range(16)]}
    mods = [(0, n) for n in range(4, 12)] + [(1, n) for n in range(12)] if both else []
    pending = None
    for kind in ("c", "a"):
        heads = [(s, h) for s in (("x", "z") if both else ("x",)) for h in range(HEADS)]
        per = 16 // len(heads)
        for i, (s, h) in enumerate(heads):
            jobs.append(("qk", kind, s, h))
            if pending:
                jobs.append(pending)
                pending = None
            jobs += tiles[kind][i * per:(i + 1) * per][:1]
            mod = mods.pop(0) if mods else None
            if mod:
                jobs.append(("modp",) + mod)
            jobs += tiles[kind][i * per:(i + 1) * per][1:]
            jobs.append(("tr", kind, s, h))
            if mod:
                jobs.append(("modt",) + mod)
            if kind == "a" and i == 4:
                jobs.append(("pool",))
            if h % 2:
                pending = ("pv", kind, s, h // 2)
    jobs.append(pending)
    first = max(i for i, j in enumerate(jobs) if j[0] == "modt") if both else \
        min(i for i, j in enumerate(jobs) if j[:2] == ("qk", "a"))
    tiles = [i for i, j in enumerate(jobs) if j[0] == "tile" and i > first][:6]
    for piece in reversed(range(6)):
        jobs.insert(tiles[piece] + 1, ("prefetch", piece))
    return jobs


def hybrid_block(nc, t, out, counts=None):
    signals = {}
    y_rows = nc.dram_tensor("y_rows", (3 * NTOK + BLK, D), F32).ap()
    w_branch = t["w_branch"].rearrange("l b k n -> l (b k) n")
    ctx = ExitStack()
    with ctx:
        def sb(name, shape, dt=F32):
            return ctx.enter_context(nc.sbuf_tensor(name, shape, dt))

        def signal(name):
            s = Signal(ctx.enter_context(nc.semaphore(name)), counts and counts[name])
            signals[name] = s
            return s

        xt = sb("xt", [P, KC, NTOK])
        ht = sb("ht", [P, KC, NTOK])
        arena = sb("arena", [P, 46 * 256])
        moe = sb("moe", [P, 96 * 256])
        ws = sb("ws", [P, 3, 8, P])
        aux = sb("aux", [P, 4, 512])
        mrow = sb("mrow", [P, 512])
        ident, rot, mean_w = sb("ident", [P, P]), sb("rot", [P, P]), sb("mean_w", [P, P])
        cos, sin = sb("cos", [P, SEQ]), sb("sin", [P, SEQ])
        colok, colneg = sb("colok", [P, GW]), sb("colneg", [P, GW])
        edge = sb("edge", [P, 4, 16])
        small = sb("small", [P, 32])
        tri_b, ones_b = sb("tri_b", [P, P], BF16), sb("ones_b", [P, P], BF16)
        cond = sb("cond", [P, KC, 32])
        colv = sb("colv", [P, 144])
        modv = sb("modv", [P, DEPTH, 2, N_MOD * KC])
        gain = sb("gain", [P, 2, 2, KC])
        half_gate = sb("half_gate", [P, 2, KC])
        sink = sb("sink", [P, DEPTH, HEADS])
        wr = sb("wr", [P, KC, NG + NE])
        br = sb("br", [P, NG + NE])
        stat = sb("stat", [P, 2, 16])
        eps = sb("eps", [P, 1])
        route_w = sb("route_w", [P, 2, 4])
        dest = sb("dest", [P, 2, 4], U32)
        slots1 = sb("slots1", [P, NTOK])
        n_of = sb("n_of", [1, NE], I32)
        start_of = sb("start_of", [1, NE], I32)
        ps = ctx.enter_context(nc.psum_tensor("ps", [P, 8, 512], F32))

        def part(base, kib, size, *dims, dt=F32):
            v = base[:, int(kib * 256):int((kib + size) * 256)]
            if dt is not F32:
                v = v.bitcast(dt)
            if len(dims) == 2:
                v = v.rearrange("p (a b) -> p a b", b=dims[1])
            if len(dims) == 3:
                v = v.rearrange("p (a b c) -> p a b c", b=dims[1], c=dims[2])
            return v

        aq, ak = part(arena, 0, 8, 4, NTOK), part(arena, 8, 8, 4, NTOK)
        av, u = part(arena, 16, 8, 4, 512), part(arena, 24, 8, 4, NTOK)
        cq, ck = part(arena, 32, 8, 4, NTOK), part(arena, 40, 4, 2, NTOK)
        cv = part(arena, 44, 2, 4, P)
        mt = part(arena, 8, 16, KC, NTOK)
        hr = part(arena, 0, 16, 4, D)
        xg = [part(arena, 24 + 2 * i, 2, KC, BLK) for i in range(3)]
        pick = [part(arena, 30 + i, 1, 4, BLK) for i in range(3)]
        hid = [part(arena, 34 + i, 1) for i in range(3)]
        hid_t = [part(arena, 37 + i, 1, 2, P) for i in range(3)]
        ysb = [part(arena, 40 + 2 * i, 2) for i in range(3)]
        yg = [[part(arena, 16 + 8 * i + 4 * k, 4) for k in range(2)] for i in range(2)]
        act_g = [aux[:, i, 0:256] for i in range(3)]
        r = part(arena, 16, 8)
        place1 = part(arena, 33, 1)[:, 0:4 * (NE + 2)].rearrange("p (t e) -> p t e", t=4)
        wgu = [moe[:, 48 * 256 * i:(48 * i + 32) * 256].rearrange("p (k g n) -> p k g n", k=KC, g=2) for i in range(2)]
        wd = [part(moe, 48 * i + 32, 16, 4, D) for i in range(2)]
        mw = [part(moe, 16 * i, 16, KC, 512) for i in range(3)]
        gates = part(moe, 48, 32, 16, NTOK)
        rows_in = part(moe, 48, 16, 4, D)
        vec_rows = part(moe, 80, 1, 2, P)
        cond_rows = part(moe, 82, 4)
        prob = [part(moe, 80 + 4 * i, 4, 2, 512) for i in range(2)]
        prob_t = [part(moe, 88 + 4 * i, 4, 4, SEQ) for i in range(2)]
        ck_raw, rt0, rt1 = prob[0][:, 0, :], prob[0][:, 1, 0:SEQ], prob[0][:, 1, SEQ:]
        sq, rs = [aux[:, i, :] for i in range(3)], aux[:, 3, :]
        swa = aux[:, 3, :].rearrange("p (q k) -> p q k", q=2)
        aux_flat = aux[:, :, :].rearrange("p a b -> p (a b)")
        pad = [aux_flat[:, i * 544:(i + 1) * 544].rearrange("p (s n) -> p s n", s=2) for i in range(2)]
        bias = [aux[:, i, :].rearrange("p (q r k) -> p q r k", q=2, r=ROWS) for i in range(4)]
        tile_bank, score_bank = [ps[:, i, :] for i in range(2)], ps[:, 2:4, :]
        prob_bank = ps[:, 4:6, :].rearrange("p b (k q) -> p (b k) q", q=SEQ)
        pv_bank, misc = ps[:, 6, :], ps[:, 7, :]

        names = """ident_in mean_in consts_in rows_in_done vecs_in router_in swa_in wst0 wst1 wst2 mwt0 mwt1 mwt2 bias0 bias1 bias2
            bias3 gu_in0 gu_in1 wd_in0 wd_in1  y_saved0 y_saved1 yo_saved yg_got0 yg_got1
            out_saved 
            in_turned in_copied prep vec_ready cond_silu cond_turned cond_cols colv_ready sq_done mean_done rstd_sqrt rstd_done
            norm_mul norm_add tile_done tile_copied rope_done rope_out qk_done max_done exp_done
            scaled pt_done pt_copied_d pt_copied_a pv_done pv_copied modp_done modp_copied modt_done mod_summed mod_ready gains
            pool_pad pooled pool_done pool_copied bias_ready gate_done gate_tanh branch_done merged out_done added
            dchain achain pchain logits_t logits_copied logits_done hturn_done hrow_copied r_exp r_onehot r_pos r_exp_done routed
            pick_set picko_set dest_set xt_done xt_copied gu_done silu_done hid_done0 hid_done1 hidt_done hidt_copied down_done0 down_done1
            y_copied0 y_copied1 xto_done xto_copied guo_done siluo_done hido_done hidto_done hidto_copied
            downo_done yo_copied comb comb_turned comb_added fin_scaled fin_turned fin_copied""".split()
        g = {n: signal(n) for n in names}
        ws_in = [g[f"wst{i}"] for i in range(3)]
        mw_in = [g[f"mwt{i}"] for i in range(3)]
        bias_in = [g[f"bias{i}"] for i in range(4)]
        gu_in, wd_in = [g["gu_in0"], g["gu_in1"]], [g["wd_in0"], g["wd_in1"]]
        y_saved = [g["y_saved0"], g["y_saved1"]]
        yg_got = [g["yg_got0"], g["yg_got1"]]
        hid_done, down_done = [g["hid_done0"], g["hid_done1"]], [g["down_done0"], g["down_done1"]]
        y_copied = [g["y_copied0"], g["y_copied1"]]

        def width(l):
            return NTOK if l == 0 else SEQ

        def streams(l):
            return [(0, LATENT), (1, CONTEXT)] if l == 0 else [(0, LATENT)]

        def kt_of(kind, h):
            return (ck[HD * (h % 2):HD * (h % 2) + HD, h // 4, :] if kind == "c"
                    else ak[HD * (h % 2):HD * (h % 2) + HD, h // 2, :])

        def q_of(kind):
            return cq if kind == "c" else aq

        def v_of(kind, h, tile):
            return (cv[:, tile, HD * (h // 4):HD * (h // 4) + HD] if kind == "c"
                    else av[:, tile, HD * h:HD * h + HD])

        def stream_items(l):
            items = []
            for j in mixer_jobs(l):
                if j[0] == "tile":
                    a = COLS[j[1]] + j[2]
                    items.append((t["w_in"][l, :, a * P:(a + 1) * P].rearrange("(k p) n -> p k n", p=P), 8, j))
                if j[0] == "pool":
                    items.append((t["w_pool"][l].rearrange("g c e -> c g e"), 4, j))
                if j[0] in ("modp", "prefetch"):
                    items.append((None, 0, j))
            for n in range(KC):
                a = COLS["g"] + 16 + n
                items.append((t["w_in"][l, :, a * P:(a + 1) * P].rearrange("(k p) n -> p k n", p=P), 8, ("g2", n)))
                for b0, m in ((0, 8), (8, 4)):
                    items.append((w_branch[l, b0 * P:(b0 + m) * P, n * P:(n + 1) * P].rearrange("(k p) n -> p k n", p=P),
                                  m, ("wb", b0, n)))
            for n in range(KC):
                items.append((t["w_out"][l, :, n * P:(n + 1) * P].rearrange("(k p) n -> p k n", p=P), 8, ("wo", n)))
            return items

        def plan_banks():
            order = [("in", c) for c in range(KC)]
            for l in range(DEPTH):
                for j in mixer_jobs(l):
                    if j[0] == "tile":
                        order.append((l,) + j[1:])
                    if j[0] == "pool":
                        order += [(l, "pool", gr) for gr in range(4)]
                order += [(l, "g2", n) for n in range(KC)] + [(l, "wo", n) for n in range(KC)]
            return {step: i % 2 for i, step in enumerate(order)}

        tile_banks = plan_banks()

        def ws_release(l, job):
            if job[0] == "tile":
                return g["tile_done"], (l, job[1], job[2])
            if job[0] == "pool":
                return g["pool_done"], (l, 3)
            if job[0] == "g2":
                return g["gate_done"], (l, job[1])
            if job[0] == "wb":
                return g["branch_done"], (l, job[2])
            return g["out_done"], (l, job[1])

        block = ctx.enter_context(nc.Block())

        @block.sync
        def _(sp):
            def const(name, dst):
                a, b = CONST_AT[name]
                sp.dma_start(dst, t["consts"][:, a:b]).then_inc(g["consts_in"].sem, g["consts_in"].tick(name, by=16))

            for i, (src, c) in enumerate((("x", 0), ("ctx", 2))):
                sp.dma_start(rows_in[:, c:c + 2, :], t[src][0].rearrange("(t p) d -> p t d", p=P)) \
                    .then_inc(g["rows_in_done"].sem, g["rows_in_done"].tick(i, by=16))
            a, b = CONST_AT["ident"]
            sp.dma_start(ident[:, :], t["consts"][:, a:b]).then_inc(g["ident_in"].sem, g["ident_in"].tick(by=16))
            a, b = CONST_AT["mean"]
            sp.dma_start(mean_w[:, :], t["consts"][:, a:b]).then_inc(g["mean_in"].sem, g["mean_in"].tick(by=16))
            sp.dma_start(vec_rows[0:96, 0, :], t["b_mod"].rearrange("l (a p) -> (l a) p", p=P)) \
                .then_inc(g["vecs_in"].sem, g["vecs_in"].tick(0, by=16))
            for i, (name, n) in enumerate((("norm1_g", 16), ("norm2_g", 16), ("final_g", 8), ("pool_scale", 8))):
                src = t[name].rearrange("(a p) -> a p", p=P) if name == "final_g" else t[name].rearrange("l (a p) -> (l a) p", p=P)
                at = (0, 16, 32, 40)[i]
                sp.dma_start(vec_rows[at:at + n, 1, :], src).then_inc(g["vecs_in"].sem, g["vecs_in"].tick(1 + i, by=16))
            sp.dma_start(cond_rows[0:1, :], t["c"]).then_inc(g["vecs_in"].sem, g["vecs_in"].tick(5, by=16))
            sp.dma_start(cond_rows[1:2, :], t["c_ctx"].rearrange("(a d) -> a d", a=1)) \
                .then_inc(g["vecs_in"].sem, g["vecs_in"].tick(6, by=16))
            sp.dma_start(sink[:, :, :].rearrange("p l h -> p (l h)"),
                         t["sink_c"].rearrange("l h -> (l h)").partition_broadcast(P)) \
                .then_inc(g["vecs_in"].sem, g["vecs_in"].tick(7, by=16))

            mods = []

            def load_mod(l, n):
                i = len(mods)
                mods.append((l, n))
                if i >= 3:
                    sp.wait_ge(g["modp_done"].sem, g["modp_done"].at(*mods[i - 3]))
                sp.dma_start(mw[i % 3], t["w_mod"][l, :, n * 512:(n + 1) * 512].rearrange("(k p) n -> p k n", p=P)) \
                    .then_inc(mw_in[i % 3].sem, mw_in[i % 3].tick(l, n, by=16))

            def load_expert(e_src, slot, pieces=range(6)):
                for i in pieces:
                    if i < 4:
                        ks = slice(4 * (i // 2), 4 * (i // 2) + 4)
                        w = (t["w_exp_gate"], t["w_exp_up"])[i % 2]
                        sp.dma_start(wgu[slot][:, ks, i % 2, :], e_src(w).rearrange("(k p) n -> p k n", p=P)[:, ks, :]) \
                            .then_inc(gu_in[slot].sem, 16)
                    else:
                        ks = slice(2 * (i - 4), 2 * (i - 4) + 2)
                        sp.dma_start(wd[slot][:, ks, :], e_src(t["w_exp_down"]).rearrange("(k p) n -> p k n", p=P)[:, ks, :]) \
                            .then_inc(wd_in[slot].sem, 16)

            for n in range(4):
                load_mod(0, n)
            for name, dst in (("rot", rot), ("cos", cos), ("sin", sin), ("colok", colok),
                              ("colneg", colneg), ("small", small), ("slots1", slots1)):
                const(name, dst[:, :])
            const("edge", edge[:, :, :].rearrange("p a b -> p (a b)"))
            const("tri", arena[:, 0:P])
            held = []
            for l in range(DEPTH):
                for src, m, job in stream_items(l):
                    if job[0] == "modp":
                        load_mod(job[1], job[2])
                    elif job[0] == "prefetch":
                        if job[1] == 0 and l == 0:
                            sp.wait_ge(g["modp_done"].sem, g["modp_done"].at(1, 11))
                        elif job[1] == 0:
                            sp.wait_ge(down_done[0].sem, 16 * l)
                        load_expert(lambda w: w[l, 0], 0, [job[1]])
                    else:
                        slot = len(held) % 3
                        if len(held) >= 3:
                            last, step = held[-3]
                            sp.wait_ge(last.sem, last.at(*step))
                        sp.dma_start(ws[:, slot, 0:m, :], src).then_inc(ws_in[slot].sem, ws_in[slot].tick(l, job, by=16))
                        held.append(ws_release(l, job))
                sp.wait_ge(g["merged"].sem, g["merged"].at(l, KC - 1))
                if l:
                    sp.wait_ge(down_done[1].sem, 16 * l)
                load_expert(lambda w: w[l, 1], 1)
                with sp.Fori(1, NE // 2) as i:
                    for slot in range(2):
                        sp.wait_ge(down_done[slot].sem, 16 * l + i)
                        load_expert(lambda w: w[l, bass.ds(2 * i + slot, 1)].rearrange("a k n -> (a k) n"), slot)
            sp.wait_ge(g["fin_copied"].sem, g["fin_copied"].at(1))
            sp.wait_ge(g["prep"].sem, g["prep"].at("fin", 1))
            sp.dma_start(out[0].rearrange("(t p) d -> p t d", p=P), hr[:, 0:2, :]) \
                .then_inc(g["out_saved"].sem, g["out_saved"].tick(0, by=16))
            sp.wait_ge(g["out_saved"].sem, 16)

        @block.tensor
        def _(pe):
            free = {}

            def claim(bank):
                if bank in free:
                    s, step = free.pop(bank)
                    pe.wait_ge(s.sem, s.at(*step))

            def next_tile_bank(*step):
                claim(tile_banks[step])
                return tile_banks[step]

            n_ws = [0]

            def weights(l, job):
                slot = n_ws[0] % 3
                n_ws[0] += 1
                pe.wait_ge(ws_in[slot].sem, ws_in[slot].at(l, job))
                return ws[:, slot]

            pe.wait_ge(g["ident_in"].sem, 16)
            pe.wait_ge(g["rows_in_done"].sem, 32)
            for c in range(KC):
                bank = next_tile_bank("in", c)
                for tile in range(4):
                    mm = pe.transpose(ps[:, bank, tile * P:(tile + 1) * P], rows_in[:, tile, c * P:(c + 1) * P], ident[:, :])
                mm.then_inc(g["in_turned"].sem, g["in_turned"].tick(c))
                free[bank] = (g["prep"], ("xt", c)) if c % 2 else (g["in_copied"], (c,))
            pe.wait_ge(g["vecs_in"].sem, 16 * 8)
            pe.transpose(misc[:, 0:96], vec_rows[0:96, 0, :], ident[0:96, 0:96])
            pe.transpose(misc[:, 96:144], vec_rows[0:48, 1, :], ident[0:48, 0:48])
            pe.wait_ge(g["cond_silu"].sem, g["cond_silu"].at(0))
            for c in range(KC):
                mm = pe.transpose(misc[:, 144 + 2 * c:146 + 2 * c], cond_rows[0:2, c * P:(c + 1) * P], ident[0:2, 0:2])
            mm.then_inc(g["cond_turned"].sem, g["cond_turned"].tick(0))
            free[7] = (g["cond_cols"], (0,))
            pe.wait_ge(g["cond_cols"].sem, g["cond_cols"].at(0))

            n_mod = [0]

            def modp(l, n):
                i = n_mod[0]
                n_mod[0] += 1
                claim(7)
                pe.wait_ge(mw_in[i % 3].sem, mw_in[i % 3].at(l, n))
                for k in range(KC):
                    q = k % 4
                    mm = pe.matmul(misc[32 * q:32 * q + 32, :], cond[:, k, :], mw[i % 3][:, k, :], start=(k < 4), stop=(k >= 4))
                mm.then_inc(g["modp_done"].sem, g["modp_done"].tick(l, n))
                free[7] = (g["modp_copied"], (l, n))

            def modt(l, n):
                claim(7)
                for q in range(4):
                    mm = pe.transpose(misc[:, q * P:(q + 1) * P], mrow[:, q * P:(q + 1) * P], ident[:, :])
                mm.then_inc(g["modt_done"].sem, g["modt_done"].tick(l, n))
                free[7] = (g["mod_summed"], (l, n))

            def mean(l, which, c):
                w = width(l) if which != "n1" else NTOK
                if c == 0:
                    claim(6)
                pe.wait_ge(g["sq_done"].sem, g["sq_done"].at(l, which, c))
                pe.matmul(pv_bank[:, 0:w], mean_w[:, :], sq[c % 3][:, 0:w], start=(c == 0), stop=(c == KC - 1)) \
                    .then_inc(g["mean_done"].sem, g["mean_done"].tick(l, which, c))
                if c == KC - 1:
                    free[6] = (g["rstd_sqrt"], (l, which))

            pe.wait_ge(g["mean_in"].sem, 16)
            for c in range(KC):
                mean(0, "n1", c)
            for n in range(4):
                modp(0, n)
                modt(0, n)

            for l in range(DEPTH):
                w_all = width(l)
                if l == 0:
                    pe.wait_ge(g["consts_in"].sem, g["consts_in"].at("tri"))
                for j in mixer_jobs(l):
                    if j[0] == "tile":
                        kind, c = j[1:]
                        w = weights(l, j)
                        bank = next_tile_bank(l, kind, c)
                        if kind == "ck":
                            pe.wait_ge(g["norm_add"].sem, g["norm_add"].at(l, "n1", KC - 1))
                        if kind in ("av", "cv"):
                            for tile in range(4):
                                for k in range(KC):
                                    mm = pe.matmul(ps[:, bank, tile * P:(tile + 1) * P], ht[:, k, tile * P:(tile + 1) * P],
                                                   w[:, k, :], start=(k == 0), stop=(k == KC - 1))
                        else:
                            cols = NTOK if kind in ("ak", "ck") else w_all
                            for k in range(KC):
                                mm = pe.matmul(ps[:, bank, 0:cols], w[:, k, :], ht[:, k, 0:cols], start=(k == 0), stop=(k == KC - 1))
                        mm.then_inc(g["tile_done"].sem, g["tile_done"].tick(l, kind, c))
                        free[bank] = (g["tile_copied"], (l, kind, c))
                    elif j[0] == "rope":
                        kind, c = j[1:]
                        claim(7)
                        pe.wait_ge(g["tile_copied"].sem, g["tile_copied"].at(l, kind, c))
                        src = ck_raw[:, 0:SEQ] if kind == "ck" else cq[:, c, 0:SEQ]
                        pe.matmul(misc[:, 0:SEQ], rot[:, :], src, start=True, stop=True) \
                            .then_inc(g["rope_done"].sem, g["rope_done"].tick(l, kind, c))
                        free[7] = (g["rope_out"], (l, kind, c))
                    elif j[0] == "qk":
                        kind, s, h = j[1:]
                        claim("s")
                        if kind == "c":
                            if s == "x" and h == 0:
                                pe.wait_ge(g["rope_out"].sem, g["rope_out"].at(l, "ck", 0))
                            if s == "x" and h < HEADS:
                                if h // 2 < 3:
                                    pe.wait_ge(g["rope_out"].sem, g["rope_out"].at(l, "cq", h // 2))
                                else:
                                    pe.wait_ge(g["rope_out"].sem, g["rope_out"].at(l, "cq", 3))
                            pe.wait_ge(g["tile_copied"].sem, g["tile_copied"].at(l, "cq", 3))
                        else:
                            pe.wait_ge(g["tile_copied"].sem, g["tile_copied"].at(l, "av", 3))
                        rows = slice(HD * (h % 2), HD * (h % 2) + HD)
                        keys = slice(0, NTOK) if s == "x" else CONTEXT
                        q0 = 0 if s == "x" else SEQ
                        n = NTOK if s == "x" else SEQ
                        for qt in range(2):
                            mm = pe.matmul(score_bank[:, qt, 0:n], q_of(kind)[rows, h // 2, q0 + qt * P:q0 + (qt + 1) * P],
                                           kt_of(kind, h)[:, keys], start=True, stop=True)
                        mm.then_inc(g["qk_done"].sem, g["qk_done"].tick(l, kind, s, h))
                        free["s"] = (g["exp_done"], (l, kind, s, h))
                    elif j[0] == "tr":
                        kind, s, h = j[1:]
                        claim("t")
                        claim("t2")
                        pe.wait_ge(g["scaled"].sem, g["scaled"].at(l, kind, s, h))
                        for tile in range(4 if s == "x" else 2):
                            for qt in range(2):
                                mm = pe.transpose(prob_bank[:, tile, qt * P:(qt + 1) * P],
                                                  prob[h % 2][:, qt, tile * P:(tile + 1) * P], ident[:, :])
                            if tile == 1:
                                mm.then_inc(g["pt_done"].sem, g["pt_done"].tick(l, kind, s, h, 0))
                            if tile == 3:
                                mm.then_inc(g["pt_done"].sem, g["pt_done"].tick(l, kind, s, h, 1))
                        free["t"] = (g["pt_copied_a"], (l, kind, s, h))
                        if s == "x":
                            free["t2"] = (g["pt_copied_d"], (l, kind, s, h))
                    elif j[0] == "pv":
                        kind, s, pair = j[1:]
                        claim(6)
                        pe.wait_ge(g["pt_copied_a"].sem, g["pt_copied_a"].at(l, kind, s, 2 * pair + 1))
                        if s == "x":
                            pe.wait_ge(g["pt_copied_d"].sem, g["pt_copied_d"].at(l, kind, s, 2 * pair + 1))
                        n = 4 if s == "x" else 2
                        for tile in range(n):
                            for hh in range(2):
                                mm = pe.matmul(pv_bank[HD * hh:HD * hh + HD, 0:SEQ], v_of(kind, 2 * pair + hh, tile + (4 - n)),
                                               prob_t[hh][:, tile, :], start=(tile == 0), stop=(tile == n - 1))
                        mm.then_inc(g["pv_done"].sem, g["pv_done"].tick(l, kind, s, pair))
                        free[6] = (g["pv_copied"], (l, kind, s, pair))
                    elif j[0] == "modp":
                        modp(*j[1:])
                    elif j[0] == "modt":
                        modt(*j[1:])
                    elif j[0] == "pool":
                        w = weights(l, j)
                        for gr in range(4):
                            bank = next_tile_bank(l, "pool", gr)
                            pe.wait_ge(g["pooled"].sem, g["pooled"].at(l, gr))
                            mm = pe.matmul(ps[:, bank, 0:w_all], w[:, gr, :], u[:, gr, 0:w_all], start=True, stop=True)
                            mm.then_inc(g["pool_done"].sem, g["pool_done"].tick(l, gr))
                            free[bank] = (g["pool_copied"], (l, gr))
                for key in ("s", "t", "t2", 6, 7):
                    claim(key)
                pe.wait_ge(g["pool_copied"].sem, g["pool_copied"].at(l, 3))
                pe.wait_ge(g["pv_copied"].sem, g["pv_copied"].at(l, "a", "z" if l == 0 else "x", 3))
                ys = (aq, u, cq)
                for n in range(KC):
                    w = weights(l, ("g2", n))
                    bank = next_tile_bank(l, "g2", n)
                    for k in range(KC):
                        mm = pe.matmul(ps[:, bank, 0:w_all], w[:, k, :], ht[:, k, 0:w_all], start=(k == 0), stop=(k == KC - 1))
                    mm.then_inc(g["gate_done"].sem, g["gate_done"].tick(l, n))
                    free[bank] = (g["gate_tanh"], (l, n))
                    for b in range(3):
                        if b != 1:
                            w = weights(l, ("wb", 0 if b == 0 else 8, n))
                        if b == 0 and n >= 2:
                            pe.wait_ge(g["merged"].sem, g["merged"].at(l, n - 2))
                        for k in range(4):
                            mm = pe.matmul(ps[:, 2 + 3 * (n % 2) + b, 0:w_all], w[:, (4 * b + k) % 8, :], ys[b][:, k, 0:w_all],
                                           start=(k == 0), stop=(k == 3))
                    mm.then_inc(g["branch_done"].sem, g["branch_done"].tick(l, n))
                for n in range(KC):
                    w = weights(l, ("wo", n))
                    bank = next_tile_bank(l, "wo", n)
                    if n == 0:
                        pe.wait_ge(g["merged"].sem, g["merged"].at(l, KC - 1))
                    for k in range(KC):
                        mm = pe.matmul(ps[:, bank, 0:w_all], w[:, k, :], mt[:, k, 0:w_all], start=(k == 0), stop=(k == KC - 1))
                    mm.then_inc(g["out_done"].sem, g["out_done"].tick(l, n))
                    free[bank] = (g["added"], (l, n))
                    if n:
                        mean(l, "n2", n - 1)
                nt = w_all // P
                mean(l, "n2", KC - 1)
                pe.wait_ge(g["router_in"].sem, g["router_in"].at(l, 3))
                claim(6)
                for k in range(KC):
                    pe.wait_ge(g["norm_add"].sem, g["norm_add"].at(l, "n2", k))
                    mm = pe.matmul(ps[0:NG + NE, 6, 0:w_all], wr[:, k, :], ht[:, k, 0:w_all], start=(k == 0), stop=(k == KC - 1))
                mm.then_inc(g["logits_t"].sem, g["logits_t"].tick(l))
                pe.wait_ge(g["logits_copied"].sem, g["logits_copied"].at(l))
                for tile in range(nt):
                    mm = pe.transpose(misc[:, tile * 64:tile * 64 + 36], mrow[0:36, tile * P:(tile + 1) * P], ident[0:36, 0:36])
                mm.then_inc(g["logits_done"].sem, g["logits_done"].tick(l))
                for tile in range(nt):
                    for half in range(2):
                        bank = 2 + (2 * tile + half) % 4
                        claim(bank)
                        for c in range(4):
                            mm = pe.transpose(ps[:, bank, c * P:(c + 1) * P], ht[:, 4 * half + c, tile * P:(tile + 1) * P], ident[:, :])
                        mm.then_inc(g["hturn_done"].sem, g["hturn_done"].tick(l, tile, half))
                        free[bank] = (g["hrow_copied"], (l, tile, half))
                msk = r[:, 1024:1024 + 64].bitcast(BF16).rearrange("p (t e) -> p t e", e=NE)
                pe.wait_ge(g["r_onehot"].sem, g["r_onehot"].at(l))
                for tile in range(nt):
                    for before in range(tile):
                        pe.matmul(ps[:, 6, tile * NE:(tile + 1) * NE], ones_b[:, :], msk[:, before, :], start=(before == 0), stop=False)
                    pe.matmul(ps[:, 6, tile * NE:(tile + 1) * NE], tri_b[:, :], msk[:, tile, :], start=(tile == 0), stop=True)
                for tile in range(nt):
                    mm = pe.matmul(ps[:, 6, 4 * NE:5 * NE], ones_b[:, :], msk[:, tile, :], start=(tile == 0), stop=(tile == nt - 1))
                mm.then_inc(g["r_pos"].sem, g["r_pos"].tick(l))
                nb = w_all // BLK
                for bank in range(8):
                    claim(bank)
                pe.wait_ge(g["routed"].sem, g["routed"].at(l))

                pe.wait_ge(g["hrow_copied"].sem, g["hrow_copied"].at(l, nt - 1, 1))

                def pick_x(dst_bank, picks, sem, chunks=range(KC)):
                    for c in chunks:
                        for tile in range(nt):
                            mm = pe.matmul(ps[:, dst_bank, c * BLK:(c + 1) * BLK], hr[:, tile, c * P:(c + 1) * P], picks[:, tile, :],
                                           start=(tile == 0), stop=(tile == nt - 1))
                    if chunks[-1] == KC - 1:
                        mm.then_inc(sem, 1)

                def gate_up(bank, xs, w, sem):
                    for k in range(KC):
                        for j in range(2):
                            mm = pe.matmul(ps[BLK * j:BLK * j + BLK, bank, :].rearrange("p (g n) -> p g n", g=2), xs[:, k, :],
                                           w[:, k, :, 256 * j:256 * j + 256], start=(k == 0), stop=(k == KC - 1))
                    mm.then_inc(sem, 1)

                def turn_h(bank, src, sem):
                    for c in range(2):
                        mm = pe.transpose(ps[:, bank, c * P:(c + 1) * P], src[:, c * P:(c + 1) * P], ident[:, :])
                    mm.then_inc(sem, 1)

                def down(bank, src, w, sem):
                    for k in range(4):
                        for j in range(2):
                            mm = pe.matmul(ps[BLK * j:BLK * j + BLK, bank, :], src[:, k % 2, BLK * (k // 2):BLK * (k // 2) + BLK],
                                           w[:, k, 512 * j:512 * j + 512], start=(k == 0), stop=(k == 3))
                    mm.then_inc(sem, 1)

                if l == 0:
                    n_more = pe.alloc_register("pe_more")
                    pe.reg_mov(n_more, 0)
                pe.wait_ge(g["pick_set"].sem, (NE + 2) * l + 1)
                pick_x(0, pick[0], g["xt_done"].sem)
                with pe.Fori(0, NE // 2) as i:
                    for s in range(2):
                        e, done = 2 * i + s, NE * l + 2 * i + s
                        mine = 16 * l + i
                        pe.wait_ge(g["xt_copied"].sem, done + l + 1)
                        pe.wait_ge(gu_in[s].sem, (mine + 1) * 64)
                        gate_up(2 + s, xg[s], wgu[s], g["gu_done"].sem)
                        pe.wait_ge(g["pick_set"].sem, done + 2 * l + 2)
                        pick_x(0, pick[1 - s], g["xt_done"].sem, range(4))
                        n = pe.value_load(n_of[0:1, bass.ds(e, 1)], min_val=0, max_val=NTOK)
                        pe.wait_ge(wd_in[s].sem, (mine + 1) * 32)
                        pe.nop(nofuse=True)
                        with pe.If(n > BLK):
                            with pe.Fori(1, nb) as b:
                                with pe.If(n > b * BLK):
                                    more = pe.snap(n_more, min_val=0, max_val=64)
                                    pe.wait_ge(g["picko_set"].sem, more + 1)
                                    pick_x(7, pick[2], g["xto_done"].sem)
                                    pe.wait_ge(g["xto_copied"].sem, more + 1)
                                    pe.wait_ge(g["yo_copied"].sem, more + 1)
                                    gate_up(6, xg[2], wgu[s], g["guo_done"].sem)
                                    pe.wait_ge(g["hido_done"].sem, more + 1)
                                    turn_h(7, hid[2], g["hidto_done"].sem)
                                    pe.wait_ge(g["hidto_copied"].sem, more + 1)
                                    down(6, hid_t[2], wd[s], g["downo_done"].sem)
                                    pe.reg_add(n_more, n_more, 1)
                                pe.nop(nofuse=True)
                        pe.nop()
                        pe.wait_ge(hid_done[s].sem, mine + 2)
                        turn_h(1, hid[s], g["hidt_done"].sem)
                        pick_x(0, pick[1 - s], g["xt_done"].sem, range(4, KC))
                        pe.wait_ge(g["hidt_copied"].sem, done + 1)
                        pe.wait_ge(y_copied[s].sem, mine + 1)
                        down(4 + s, hid_t[s], wd[s], down_done[s].sem)
                after = (l + 1, "n1") if l + 1 < DEPTH else (l, "fin")
                pe.wait_ge(g["comb"].sem, g["comb"].at(l, nt - 1))
                pe.wait_ge(y_copied[1].sem, 16 * (l + 1) + 1)
                for c in range(KC):
                    bank = 2 + c % 2
                    claim(bank)
                    for tile in range(nt):
                        mm = pe.transpose(ps[:, bank, tile * P:(tile + 1) * P], hr[:, tile, c * P:(c + 1) * P], ident[:, :])
                    mm.then_inc(g["comb_turned"].sem, g["comb_turned"].tick(l, c))
                    free[bank] = (g["comb_added"], (l, c))
                    if c:
                        mean(*after, c - 1)
                for bank in (2, 3):
                    claim(bank)
                mean(*after, KC - 1)
            for tile in range(2):
                for half in range(2):
                    for c in range(4):
                        pe.wait_ge(g["fin_scaled"].sem, g["fin_scaled"].at(4 * half + c))
                        mm = pe.transpose(ps[:, 2 + 2 * tile + half, c * P:(c + 1) * P],
                                          ht[:, 4 * half + c, tile * P:(tile + 1) * P], ident[:, :])
                    mm.then_inc(g["fin_turned"].sem, g["fin_turned"].tick(tile, half))

        @block.scalar
        def _(act):
            def chain(ins):
                ins.then_inc(g["achain"].sem, g["achain"].tick())
                act.wait_ge(g["achain"].sem, g["achain"].n)

            for c in range(1, KC, 2):
                act.wait_ge(g["in_turned"].sem, g["in_turned"].at(c))
                nc.scalar.activation(xt[:, c, :], tile_bank[c % 2], ACT.Copy).then_inc(g["prep"].sem, g["prep"].tick("xt", c))
            act.wait_ge(g["vecs_in"].sem, 16 * 8)
            nc.scalar.activation(cond_rows[0:2, :], cond_rows[0:2, :], ACT.Silu).then_inc(g["cond_silu"].sem, g["cond_silu"].tick(0))

            def modp_copy(l, n):
                act.wait_ge(g["modp_done"].sem, g["modp_done"].at(l, n))
                prev = (l, n - 1) if n else (l - 1, 11)
                if prev[0] >= 0:
                    act.wait_ge(g["modt_done"].sem, g["modt_done"].at(*prev))
                nc.scalar.activation(mrow[:, :], misc, ACT.Copy).then_inc(g["modp_copied"].sem, g["modp_copied"].tick(l, n))

            def squares(l, which):
                w = width(l) if which != "n1" else NTOK
                if which == "n1" and l == 0:
                    act.wait_ge(g["in_copied"].sem, g["in_copied"].at(KC - 2))
                    act.wait_ge(g["prep"].sem, g["prep"].at("xt", KC - 1))
                for c in range(KC):
                    if which == "n2":
                        act.wait_ge(g["added"].sem, g["added"].at(l, c))
                    elif (l, which) != (0, "n1"):
                        act.wait_ge(g["comb_added"].sem, g["comb_added"].at(l if which == "fin" else l - 1, c))
                    if c >= 3:
                        act.wait_ge(g["mean_done"].sem, g["mean_done"].at(l, which, c - 3))
                    nc.scalar.activation(sq[c % 3][:, 0:w], xt[:, c, 0:w], ACT.Square) \
                        .then_inc(g["sq_done"].sem, g["sq_done"].tick(l, which, c))
                act.wait_ge(g["mean_done"].sem, g["mean_done"].at(l, which, KC - 1))
                nc.scalar.activation(rs[:, 0:w], pv_bank[:, 0:w], ACT.Sqrt, bias=eps[:, 0:1]) \
                    .then_inc(g["rstd_sqrt"].sem, g["rstd_sqrt"].tick(l, which))

            def shift(l, which, first):
                for c in range(KC):
                    act.wait_ge(g["norm_mul"].sem, g["norm_mul"].at(l, which, c))
                    both = streams(0) if which == "n1" else streams(l)
                    for s, cols in both:
                        ins = nc.scalar.activation(ht[:, c, cols], ht[:, c, cols], ACT.Identity,
                                                   bias=modv[:, l, s, first + c:first + c + 1])
                    ins.then_inc(g["norm_add"].sem, g["norm_add"].tick(l, which, c))

            for l in range(DEPTH):
                w_all = width(l)
                if l == 0:
                    act.wait_ge(g["vec_ready"].sem, g["vec_ready"].at("eps"))
                squares(l, "n1")
                if l == 0:
                    for n in range(4):
                        modp_copy(0, n)
                shift(l, "n1", 0)
                for j in mixer_jobs(l):
                    if j[0] == "tile":
                        kind, c = j[1:]
                        act.wait_ge(g["tile_done"].sem, g["tile_done"].at(l, kind, c))
                        bank = tile_banks[(l, kind, c)]
                        src = ps[:, bank, :]
                        if kind in ("aq", "cq"):
                            dst = (aq if kind == "aq" else cq)[:, c, 0:w_all]
                            ins = nc.scalar.activation(dst, src[:, 0:w_all], ACT.Copy, scale=SCALE)
                        elif kind == "ak":
                            ins = nc.scalar.activation(ak[:, c, :], src, ACT.Copy)
                        elif kind == "u":
                            ins = nc.scalar.activation(u[:, c, 0:w_all], src[:, 0:w_all], ACT.Copy)
                        elif kind == "ck":
                            ins = nc.scalar.activation(ck_raw, src, ACT.Copy)
                        elif kind == "cv":
                            ins = nc.scalar.activation(cv, src.rearrange("p (t n) -> p t n", n=P), ACT.Copy)
                        elif kind == "av":
                            ins = nc.scalar.activation(av[:, :, c * P:(c + 1) * P], src.rearrange("p (t n) -> p t n", n=P), ACT.Copy)
                        else:
                            ins = nc.scalar.activation(gates[:, c, 0:w_all], src[:, 0:w_all], ACT.Tanh, scale=0.5)
                        ins.then_inc(g["tile_copied"].sem, g["tile_copied"].tick(l, kind, c))
                    elif j[0] == "qk":
                        kind, s, h = j[1:]
                        act.wait_ge(g["max_done"].sem, g["max_done"].at(l, kind, s, h))
                        st, pb = stat[:, h % 2], prob[h % 2]
                        for qt in range(2):
                            if s == "x":
                                nc.scalar.activation(pb[:, qt, 0:SEQ], pb[:, qt, 0:SEQ], ACT.Exp, bias=st[:, qt:qt + 1],
                                                     accum_out=st[:, 2 + qt:3 + qt])
                                ins = nc.scalar.activation(pb[:, qt, SEQ:NTOK], score_bank[:, qt, SEQ:NTOK], ACT.Exp,
                                                           bias=st[:, qt:qt + 1], accum_out=st[:, 4 + qt:5 + qt])
                            else:
                                ins = nc.scalar.activation(pb[:, qt, 0:SEQ], score_bank[:, qt, 0:SEQ], ACT.Exp,
                                                           bias=st[:, qt:qt + 1], accum_out=st[:, 2 + qt:3 + qt])
                        if kind == "c":
                            ins = nc.scalar.activation(st[:, 6:8], st[:, 0:2], ACT.Exp, bias=sink[:, l, h:h + 1])
                        ins.then_inc(g["exp_done"].sem, g["exp_done"].tick(l, kind, s, h))
                    elif j[0] == "tr":
                        kind, s, h = j[1:]
                        act.wait_ge(g["pt_done"].sem, g["pt_done"].at(l, kind, s, h, 0))
                        nc.scalar.activation(prob_t[h % 2][:, 0:2, :], prob_bank[:, 0:2, :], ACT.Copy) \
                            .then_inc(g["pt_copied_a"].sem, g["pt_copied_a"].tick(l, kind, s, h))
                    elif j[0] == "pv":
                        kind, s, pair = j[1:]
                        act.wait_ge(g["pv_done"].sem, g["pv_done"].at(l, kind, s, pair))
                        cols = LATENT if s == "x" else CONTEXT
                        nc.scalar.activation(q_of(kind)[:, pair, cols], pv_bank[:, 0:SEQ], ACT.Copy) \
                            .then_inc(g["pv_copied"].sem, g["pv_copied"].tick(l, kind, s, pair))
                    elif j[0] == "modp":
                        modp_copy(*j[1:])
                    elif j[0] == "pool":
                        for gr in range(4):
                            act.wait_ge(g["pool_done"].sem, g["pool_done"].at(l, gr))
                            nc.scalar.activation(u[:, gr, 0:w_all], ps[:, tile_banks[(l, "pool", gr)], 0:w_all], ACT.Copy,
                                                 scale=colv[:, 136 + 4 * l + gr:137 + 4 * l + gr]) \
                                .then_inc(g["pool_copied"].sem, g["pool_copied"].tick(l, gr))
                for n in range(KC):
                    act.wait_ge(g["gate_done"].sem, g["gate_done"].at(l, n))
                    if n >= 2:
                        act.wait_ge(g["merged"].sem, g["merged"].at(l, n - 2))
                    nc.scalar.activation(aux[:, n % 2, 0:w_all], ps[:, tile_banks[(l, "g2", n)], 0:w_all], ACT.Tanh, scale=0.5) \
                        .then_inc(g["gate_tanh"].sem, g["gate_tanh"].tick(l, n))
                squares(l, "n2")
                shift(l, "n2", 3 * KC)
                nt = w_all // P
                act.wait_ge(g["logits_t"].sem, g["logits_t"].at(l))
                nc.scalar.activation(mrow[0:NG + NE, 0:w_all], ps[0:NG + NE, 6, 0:w_all], ACT.Copy) \
                    .then_inc(g["logits_copied"].sem, g["logits_copied"].tick(l))
                for tile in range(nt):
                    for half in range(2):
                        act.wait_ge(g["hturn_done"].sem, g["hturn_done"].at(l, tile, half))
                        nc.scalar.activation(hr[:, tile, 512 * half:512 * half + 512], ps[:, 2 + (2 * tile + half) % 4, :], ACT.Copy) \
                            .then_inc(g["hrow_copied"].sem, g["hrow_copied"].tick(l, tile, half))
                for step in range(2):
                    act.wait_ge(g["r_exp"].sem, g["r_exp"].at(l, "in", step))
                    buf = r[:, 256:256 + 4 * nt] if step == 0 else r[:, 288:288 + nt]
                    nc.scalar.activation(buf, buf, ACT.Exp).then_inc(g["r_exp_done"].sem, g["r_exp_done"].tick(l, step))
                act.wait_ge(g["routed"].sem, g["routed"].at(l))
                nb = w_all // BLK

                def save_rows(src, row, signal):
                    for j in range(2):
                        act.dma_start(y_rows[bass.ds(row, BLK), j * 512:(j + 1) * 512], src[BLK * j:BLK * j + BLK, :]) \
                            .then_inc(signal.sem, 16)

                if l == 0:
                    n_more = act.alloc_register("act_more")
                    act.reg_mov(n_more, 0)
                    for s in range(2):
                        act.sem_inc(y_copied[s].sem, 1)
                        act.sem_inc(y_saved[s].sem, 32)
                    act.sem_inc(g["yo_copied"].sem, 1)
                    act.sem_inc(g["yo_saved"].sem, 32)
                with act.Fori(0, NE // 2) as i:
                    for s in range(2):
                        e, done, mine = 2 * i + s, NE * l + 2 * i + s, 16 * l + i
                        other = mine + 1 if s == 0 else mine + 2
                        act.wait_ge(g["gu_done"].sem, done + 1)
                        act.wait_ge(hid_done[s].sem, mine + 1)
                        nc.scalar.activation(act_g[s], ps[:, 2 + s, 0:256], ACT.Silu).then_inc(g["silu_done"].sem, 1)
                        n = act.value_load(n_of[0:1, bass.ds(e, 1)], min_val=0, max_val=NTOK)
                        row = act.value_load(start_of[0:1, bass.ds(e, 1)], min_val=0, max_val=2 * NTOK)
                        act.wait_ge(y_saved[1 - s].sem, other * 32)
                        act.nop(nofuse=True)
                        with act.If(n > BLK):
                            with act.Fori(1, nb) as b:
                                with act.If(n > b * BLK):
                                    more = act.snap(n_more, min_val=0, max_val=64)
                                    act.wait_ge(g["guo_done"].sem, more + 1)
                                    nc.scalar.activation(act_g[2], ps[:, 6, 0:256], ACT.Silu).then_inc(g["siluo_done"].sem, 1)
                                    act.wait_ge(g["downo_done"].sem, more + 1)
                                    act.wait_ge(g["yo_saved"].sem, more * 32 + 32)
                                    nc.scalar.activation(ysb[2], ps[:, 6, :], ACT.Copy).then_inc(g["yo_copied"].sem, 1)
                                    act.wait_ge(g["yo_copied"].sem, more + 2)
                                    save_rows(ysb[2], act.snap(row + b * BLK, min_val=0, max_val=2 * NTOK), g["yo_saved"])
                                    act.reg_add(n_more, n_more, 1)
                                act.nop()
                        act.nop()
                        act.wait_ge(down_done[s].sem, mine + 1)
                        act.wait_ge(y_saved[s].sem, mine * 32 + 32)
                        nc.scalar.activation(ysb[s], ps[:, 4 + s, :], ACT.Copy).then_inc(y_copied[s].sem, 1)
                        act.wait_ge(y_copied[s].sem, mine + 2)
                        act.wait_ge(g["yo_saved"].sem, act.snap(n_more, min_val=0, max_val=64) * 32 + 32)
                        save_rows(ysb[s], row, y_saved[s])
                act.wait_ge(y_saved[0].sem, 32 * 16 * (l + 1) + 32)
                act.wait_ge(y_saved[1].sem, 32 * 16 * (l + 1) + 32)
                act.wait_ge(g["yo_saved"].sem, act.snap(n_more, min_val=0, max_val=64) * 32 + 32)
                act.sem_inc(g["prep"].sem, g["prep"].tick("y", l))
            squares(DEPTH - 1, "fin")
            for tile in range(2):
                act.wait_ge(g["fin_turned"].sem, g["fin_turned"].at(tile, 1))
                nc.scalar.activation(hr[:, tile, 512:1024], ps[:, 3 + 2 * tile, :], ACT.Copy) \
                    .then_inc(g["prep"].sem, g["prep"].tick("fin", tile))

        @block.vector
        def _(dve):
            v = nc.vector

            def chain(ins):
                ins.then_inc(g["dchain"].sem, g["dchain"].tick())
                dve.wait_ge(g["dchain"].sem, g["dchain"].n)

            v.memset(eps[:, :], EPS).then_inc(g["vec_ready"].sem, g["vec_ready"].tick("eps"))
            chain(v.memset(cond[:, :, :], 0.0))
            chain(v.memset(ones_b[:, :], 1.0))
            for c in range(0, KC, 2):
                dve.wait_ge(g["in_turned"].sem, g["in_turned"].at(c))
                v.tensor_copy(xt[:, c, :], tile_bank[c % 2]).then_inc(g["in_copied"].sem, g["in_copied"].tick(c))
            dve.wait_ge(g["cond_turned"].sem, g["cond_turned"].at(0))
            chain(v.tensor_copy(colv[:, :], misc[:, 0:144]))
            v.tensor_copy(cond[:, :, 0:2], misc[:, 144:160].rearrange("p (k s) -> p k s", s=2)) \
                .then_inc(g["cond_cols"].sem, g["cond_cols"].tick(0))

            def mod_sum(l, n):
                dve.wait_ge(g["modt_done"].sem, g["modt_done"].at(l, n))
                cols = slice(4 * n, 4 * n + 4)
                v.tensor_reduce(modv[:, l, :, cols], misc.rearrange("p (q j r) -> p r q j", q=4, j=4)[:, 0:2], AX, ALU.add) \
                    .then_inc(g["mod_summed"].sem, g["mod_summed"].tick(l, n))
                dve.wait_ge(g["mod_summed"].sem, g["mod_summed"].at(l, n))
                bm = colv[:, 48 * l + 4 * n:48 * l + 4 * n + 4].unsqueeze(1).broadcast_to([P, 2, 4])
                v.tensor_tensor(modv[:, l, :, cols], modv[:, l, :, cols], bm, ALU.add) \
                    .then_inc(g["mod_ready"].sem, g["mod_ready"].tick(l, n))

            def gains(l, norm):
                dve.wait_ge(g["mod_ready"].sem, g["mod_ready"].at(l, 11 if l or norm else 3))
                first = KC * (1 + 3 * norm)
                for s in range(2):
                    ins = v.scalar_tensor_tensor(gain[:, norm, s, :], modv[:, l, s, first:first + KC], 1.0,
                                                 colv[:, 96 + 16 * norm + KC * l:96 + 16 * norm + KC * (l + 1)], ALU.add, ALU.mult)
                if norm:
                    chain(v.tensor_scalar(half_gate[:, :, :], modv[:, l, :, 2 * KC:3 * KC], 0.5, None, ALU.mult))
                else:
                    chain(ins)

            def reciprocal_rms(l, which):
                w = width(l) if which != "n1" else NTOK
                dve.wait_ge(g["rstd_sqrt"].sem, g["rstd_sqrt"].at(l, which))
                v.reciprocal(rs[:, 0:w], rs[:, 0:w]).then_inc(g["rstd_done"].sem, g["rstd_done"].tick(l, which))
                dve.wait_ge(g["rstd_done"].sem, g["rstd_done"].at(l, which))

            def scale_norm(l, which):
                w = width(l) if which != "n1" else NTOK
                for c in range(KC):
                    if which == "fin":
                        v.scalar_tensor_tensor(ht[:, c, 0:w], xt[:, c, 0:w], colv[:, 128 + c:129 + c], rs[:, 0:w], ALU.mult, ALU.mult) \
                            .then_inc(g["fin_scaled"].sem, g["fin_scaled"].tick(c))
                        continue
                    for s, cols in (streams(0) if which == "n1" else streams(l)):
                        ins = v.scalar_tensor_tensor(ht[:, c, cols], xt[:, c, cols], gain[:, int(which == "n2"), s, c:c + 1],
                                                     rs[:, cols], ALU.mult, ALU.mult)
                    ins.then_inc(g["norm_mul"].sem, g["norm_mul"].tick(l, which, c))

            reciprocal_rms(0, "n1")
            for n in range(4):
                mod_sum(0, n)
            for l in range(DEPTH):
                w_all = width(l)
                gains(l, 0)
                if l:
                    gains(l, 1)
                    reciprocal_rms(l, "n1")
                scale_norm(l, "n1")
                if l == 0:
                    dve.wait_ge(g["consts_in"].sem, g["consts_in"].at("tri"))
                    chain(v.tensor_copy(tri_b[:, :], arena[:, 0:P]))
                last_tr = {}
                for j in mixer_jobs(l):
                    if j[0] == "rope":
                        kind, c = j[1:]
                        dve.wait_ge(g["rope_done"].sem, g["rope_done"].at(l, kind, c))
                        src = ck_raw[:, 0:SEQ] if kind == "ck" else cq[:, c, 0:SEQ]
                        v.tensor_tensor(rt0, misc[:, 0:SEQ], sin[:, :], ALU.mult)
                        chain(v.tensor_tensor(rt1, src, cos[:, :], ALU.mult))
                        if kind == "cq":
                            ins = v.tensor_tensor(src, rt0, rt1, ALU.add)
                        else:
                            for kv in range(2):
                                rows = slice(HD * kv, HD * kv + HD)
                                for half in range(2):
                                    to = slice(HD * half, HD * half + HD)
                                    v.tensor_copy(ck[to, kv, CONTEXT], ck_raw[rows, CONTEXT])
                                    ins = v.tensor_tensor(ck[to, kv, LATENT], rt0[rows], rt1[rows], ALU.add)
                        ins.then_inc(g["rope_out"].sem, g["rope_out"].tick(l, kind, c))
                        dve.wait_ge(g["rope_out"].sem, g["rope_out"].at(l, kind, c))
                    elif j[0] == "qk":
                        kind, s, h = j[1:]
                        st, pb = stat[:, h % 2], prob[h % 2]
                        if h % 2 in last_tr:
                            dve.wait_ge(g["pt_done"].sem, g["pt_done"].at(*last_tr[h % 2]))
                        if s == "x" and h == 0:
                            if kind == "c":
                                dve.wait_ge(g["swa_in"].sem, g["swa_in"].at(l))
                                dve.wait_ge(g["rope_out"].sem, g["rope_out"].at(l, "cq", 3))
                        if kind == "a" and s == "x":
                            dve.wait_ge(g["bias_ready"].sem, g["bias_ready"].at(l, h))
                        dve.wait_ge(g["qk_done"].sem, g["qk_done"].at(l, kind, s, h))
                        if s == "x":
                            for qt in range(2):
                                add = swa[:, qt, :] if kind == "c" else bias[h % 4][:, qt].rearrange("p r k -> p (r k)")
                                v.tensor_tensor_reduce(pb[:, qt, 0:SEQ], score_bank[:, qt, 0:SEQ], add, 1.0, NEG, ALU.add, ALU.max,
                                                       st[:, 8 + qt:9 + qt])
                            chain(v.tensor_reduce(st[:, 10:12], score_bank[:, :, SEQ:NTOK], AX, ALU.max))
                            chain(v.tensor_tensor(st[:, 8:10], st[:, 8:10], st[:, 10:12], ALU.max))
                        else:
                            chain(v.tensor_reduce(st[:, 8:10], score_bank[:, :, 0:SEQ], AX, ALU.max))
                        if kind == "c":
                            ins = v.tensor_scalar(st[:, 0:2], st[:, 8:10], sink[:, l, h:h + 1], -1.0, ALU.max, ALU.mult)
                        else:
                            ins = v.tensor_scalar(st[:, 0:2], st[:, 8:10], -1.0, None, ALU.mult)
                        ins.then_inc(g["max_done"].sem, g["max_done"].tick(l, kind, s, h))
                        dve.wait_ge(g["exp_done"].sem, g["exp_done"].at(l, kind, s, h))
                        total = st[:, 2:4]
                        if s == "x":
                            chain(v.tensor_tensor(st[:, 12:14], total, st[:, 4:6], ALU.add))
                            total = st[:, 12:14]
                        if kind == "c":
                            chain(v.tensor_tensor(st[:, 12:14], total, st[:, 6:8], ALU.add))
                            total = st[:, 12:14]
                        chain(v.reciprocal(st[:, 14:16], total))
                        n = NTOK if s == "x" else SEQ
                        for qt in range(2):
                            ins = v.tensor_scalar(pb[:, qt, 0:n], pb[:, qt, 0:n], st[:, 14 + qt:15 + qt], None, ALU.mult)
                        ins.then_inc(g["scaled"].sem, g["scaled"].tick(l, kind, s, h))
                    elif j[0] == "tr":
                        kind, s, h = j[1:]
                        if s == "x":
                            dve.wait_ge(g["pt_done"].sem, g["pt_done"].at(l, kind, s, h, 1))
                            v.tensor_copy(prob_t[h % 2][:, 2:4, :], prob_bank[:, 2:4, :]) \
                                .then_inc(g["pt_copied_d"].sem, g["pt_copied_d"].tick(l, kind, s, h))
                        last_tr[h % 2] = (l, kind, s, h, 1 if s == "x" else 0)
                    elif j[0] == "modt":
                        mod_sum(*j[1:])
                if l == 0:
                    gains(0, 1)
                for n in range(KC):
                    dve.wait_ge(g["branch_done"].sem, g["branch_done"].at(l, n))
                    dve.wait_ge(g["gate_tanh"].sem, g["gate_tanh"].at(l, n))
                    if n:
                        dve.wait_ge(g["merged"].sem, g["merged"].at(l, n - 1))
                    b0 = 2 + 3 * (n % 2)
                    for b, (gt, to) in enumerate(((gates[:, n], mt[:, n]), (gates[:, 8 + n], aux[:, 2]), (aux[:, n % 2], aux[:, 3]))):
                        ins = v.scalar_tensor_tensor(to[:, 0:w_all], gt[:, 0:w_all], 1.0, ps[:, b0 + b, 0:w_all], ALU.add, ALU.mult)
                    chain(ins)
                    chain(v.tensor_tensor(mt[:, n, 0:w_all], mt[:, n, 0:w_all], aux[:, 2, 0:w_all], ALU.add))
                    v.tensor_tensor(mt[:, n, 0:w_all], mt[:, n, 0:w_all], aux[:, 3, 0:w_all], ALU.add) \
                        .then_inc(g["merged"].sem, g["merged"].tick(l, n))
                for n in range(KC):
                    dve.wait_ge(g["out_done"].sem, g["out_done"].at(l, n))
                    for s, cols in streams(l):
                        ins = v.scalar_tensor_tensor(xt[:, n, cols], ps[:, tile_banks[(l, "wo", n)], cols], half_gate[:, s, n:n + 1],
                                                     xt[:, n, cols], ALU.mult, ALU.add)
                    ins.then_inc(g["added"].sem, g["added"].tick(l, n))
                dve.wait_ge(g["added"].sem, g["added"].at(l, KC - 1))
                reciprocal_rms(l, "n2")
                scale_norm(l, "n2")
                nt, nb = w_all // P, w_all // BLK
                dve.wait_ge(g["logits_done"].sem, g["logits_done"].at(l))

                def tmp(at, *dims):
                    a = r[:, at:at + dims[0] * (dims[1] if len(dims) > 1 else 1)]
                    return a.rearrange("p (a b) -> p a b", b=dims[1]) if len(dims) > 1 else a

                def spread(a, m):
                    return a.unsqueeze(2).broadcast_to([P, nt, m])

                lg = tmp(0, nt, 36)
                gmax, gtop, emax, etop = tmp(144, nt), tmp(148, nt), tmp(152, nt), tmp(156, nt)
                p_grp, w_sum, emax2 = tmp(160, nt), tmp(164, nt), tmp(168, nt)
                gexp, goh, gsc = tmp(256, nt, 4), tmp(608, nt, 4), tmp(624, nt, 4)
                gap = tmp(288, nt)
                le, le2, esc = tmp(448, nt, 8), tmp(576, nt, 8), tmp(544, nt, 8)
                oh = [tmp(480, nt, 8), tmp(512, nt, 8)]
                ohe = [tmp(640, nt, NE), tmp(768, nt, NE)]
                wide = tmp(896, nt, NE)
                both = tmp(1152, nt, NE)
                msk = r[:, 1024:1088].bitcast(BF16).rearrange("p (t e) -> p t e", e=NE)
                cnt, incl, start, one = tmp(1408, NE), tmp(1440, NE), tmp(1472, NE), tmp(1504, NE)
                pos = tmp(1536, nt, NE)
                pos_k = [tmp(1664, nt), tmp(1668, nt)]
                dest_k = [tmp(1680, nt), tmp(1684, nt)]
                down4, down8 = small[:, 0:4], small[:, 4:12]

                dve.wait_ge(g["router_in"].sem, g["router_in"].at(l, 3))
                chain(v.tensor_tensor(lg, misc[:, 0:64 * nt].rearrange("p (t n) -> p t n", n=64)[:, :, 0:36],
                                      br[:, :].unsqueeze(1).broadcast_to([P, nt, 36]), ALU.add))

                def top_one_hot(values, best, score, order, top, out, m):
                    chain(v.tensor_reduce(best, values, AX, ALU.max))
                    chain(v.tensor_tensor(score, values, spread(best, m), ALU.is_ge))
                    chain(v.tensor_tensor(score, score, order.unsqueeze(1).broadcast_to([P, nt, m]), ALU.mult))
                    chain(v.tensor_reduce(top, score, AX, ALU.max))
                    chain(v.tensor_tensor(out, score, spread(top, m), ALU.is_equal))

                top_one_hot(lg[:, :, 0:4], gmax, gsc, down4, gtop, goh, 4)
                v.tensor_tensor(gexp, lg[:, :, 0:4], spread(gmax, 4), ALU.subtract) \
                    .then_inc(g["r_exp"].sem, g["r_exp"].tick(l, "in", 0))
                chain(v.tensor_tensor(wide.rearrange("p t (g i) -> p t g i", i=8), lg[:, :, 4:36].rearrange("p t (g i) -> p t g i", i=8),
                                      goh.unsqueeze(3).broadcast_to([P, nt, 4, 8]), ALU.mult))
                chain(v.tensor_reduce(le, wide.rearrange("p t (g i) -> p t i g", i=8), AX, ALU.add))
                top_one_hot(le, emax, esc, down8, etop, oh[0], 8)
                chain(v.scalar_tensor_tensor(le2, oh[0], NEG, le, ALU.mult, ALU.add))
                top_one_hot(le2, emax2, esc, down8, etop, oh[1], 8)
                v.tensor_tensor(gap, emax2, emax, ALU.subtract).then_inc(g["r_exp"].sem, g["r_exp"].tick(l, "in", 1))
                for k in range(2):
                    chain(v.tensor_tensor(ohe[k].rearrange("p t (g i) -> p t g i", i=8), goh.unsqueeze(3).broadcast_to([P, nt, 4, 8]),
                                          oh[k].unsqueeze(2).broadcast_to([P, nt, 4, 8]), ALU.mult))
                v.tensor_tensor(msk[:, 0:nt], ohe[0], ohe[1], ALU.add).then_inc(g["r_onehot"].sem, g["r_onehot"].tick(l))
                chain(v.tensor_tensor(both, ohe[0], ohe[1], ALU.add))
                chain(v.memset(place1[:, :, :], 0.0))
                chain(v.memset(one, 1.0))
                dve.wait_ge(g["r_pos"].sem, g["r_pos"].at(l))
                chain(v.tensor_copy(pos, ps[:, 6, 0:nt * NE].rearrange("p (t e) -> p t e", e=NE)))
                chain(v.tensor_copy(cnt, ps[:, 6, 4 * NE:5 * NE]))
                chain(v.tensor_tensor_scan(incl, one, cnt, 0.0, ALU.mult, ALU.add))
                chain(v.tensor_tensor(start, incl, cnt, ALU.subtract))
                chain(v.tensor_copy(n_of[:, :], cnt[0:1]))
                v.tensor_copy(start_of[:, :], start[0:1]).then_inc(g["routed"].sem, g["routed"].tick(l))
                chain(v.scalar_tensor_tensor(place1[:, 0:nt, 0:NE], pos, 1.0, both, ALU.add, ALU.mult)) 

                def set_pick(i, e, first, signal):
                    v.tensor_tensor(pick[i][:, 0:nt, :], place1[:, 0:nt, bass.ds(e, 1)].broadcast_to([P, nt, BLK]),
                                    slots1[:, bass.ds(first, BLK)].unsqueeze(1).broadcast_to([P, nt, BLK]), ALU.is_equal) \
                        .then_inc(signal.sem, 1)

                for i in range(2):
                    v.tensor_tensor(pick[i][:, 0:nt, :], place1[:, 0:nt, i:i + 1].broadcast_to([P, nt, BLK]),
                                    slots1[:, 0:BLK].unsqueeze(1).broadcast_to([P, nt, BLK]), ALU.is_equal) \
                        .then_inc(g["pick_set"].sem, 1)
                for k in range(2):
                    chain(v.tensor_tensor(wide, ohe[k], pos, ALU.mult))
                    chain(v.tensor_reduce(pos_k[k], wide, AX, ALU.add))
                    chain(v.tensor_tensor(wide, ohe[k], start.unsqueeze(1).broadcast_to([P, nt, NE]), ALU.mult))
                    chain(v.tensor_reduce(dest_k[k], wide, AX, ALU.add))
                    ins = v.tensor_tensor(dest[:, k, 0:nt], dest_k[k], pos_k[k], ALU.add)
                    ins.then_inc(g["dest_set"].sem, g["dest_set"].tick(l, k))
                dve.wait_ge(g["r_exp_done"].sem, g["r_exp_done"].at(l, 1))
                chain(v.tensor_reduce(p_grp, gexp, AX, ALU.add))
                chain(v.reciprocal(p_grp, p_grp))
                chain(v.tensor_scalar(w_sum, gap, 1.0, None, ALU.add))
                chain(v.reciprocal(w_sum, w_sum))
                chain(v.tensor_tensor(route_w[:, 0, 0:nt], p_grp, w_sum, ALU.mult))
                chain(v.tensor_tensor(route_w[:, 1, 0:nt], route_w[:, 0, 0:nt], gap, ALU.mult))

                if l == 0:
                    n_more = dve.alloc_register("dve_more")
                    dve.reg_mov(n_more, 0)
                    for s in range(2):
                        dve.sem_inc(hid_done[s].sem, 1)
                dve.wait_ge(g["xt_done"].sem, (NE + 1) * l + 1)
                v.tensor_copy(xg[0], ps[:, 0, :].rearrange("p (k n) -> p k n", n=BLK)).then_inc(g["xt_copied"].sem, 1)
                with dve.Fori(0, NE // 2) as i:
                    for s in range(2):
                        e, done, mine = 2 * i + s, NE * l + 2 * i + s, 16 * l + i
                        dve.wait_ge(g["silu_done"].sem, done + 1)
                        v.tensor_tensor(hid[s], act_g[s], ps[:, 2 + s, 256:512], ALU.mult).then_inc(hid_done[s].sem, 1)
                        n = dve.value_load(n_of[0:1, bass.ds(e, 1)], min_val=0, max_val=NTOK)
                        with dve.If(n > BLK):
                            with dve.Fori(1, nb) as b:
                                with dve.If(n > b * BLK):
                                    more = dve.snap(n_more, min_val=0, max_val=64)
                                    set_pick(2, e, b * BLK, g["picko_set"])
                                    dve.wait_ge(g["xto_done"].sem, more + 1)
                                    v.tensor_copy(xg[2], ps[:, 7, :].rearrange("p (k n) -> p k n", n=BLK)).then_inc(g["xto_copied"].sem, 1)
                                    dve.wait_ge(g["siluo_done"].sem, more + 1)
                                    v.tensor_tensor(hid[2], act_g[2], ps[:, 6, 256:512], ALU.mult).then_inc(g["hido_done"].sem, 1)
                                    dve.wait_ge(g["hidto_done"].sem, more + 1)
                                    v.tensor_copy(hid_t[2], ps[:, 7, 0:256].rearrange("p (c n) -> p c n", n=P)) \
                                        .then_inc(g["hidto_copied"].sem, 1)
                                    dve.reg_add(n_more, n_more, 1)
                                dve.nop()
                        dve.nop()
                        dve.wait_ge(g["hidt_done"].sem, done + 1)
                        v.tensor_copy(hid_t[s], ps[:, 1, 0:256].rearrange("p (c n) -> p c n", n=P)).then_inc(g["hidt_copied"].sem, 1)
                        dve.wait_ge(g["xt_done"].sem, done + l + 2)
                        v.tensor_copy(xg[1 - s], ps[:, 0, :].rearrange("p (k n) -> p k n", n=BLK)).then_inc(g["xt_copied"].sem, 1)
                        set_pick(s, e + 2, 0, g["pick_set"])
                for tile in range(nt):
                    got = yg_got[tile % 2]
                    dve.wait_ge(got.sem, got.at(l, tile, 1))
                    chain(v.tensor_scalar(hr[:, tile, :], yg[tile % 2][0], route_w[:, 0, tile:tile + 1], None, ALU.mult))
                    v.scalar_tensor_tensor(hr[:, tile, :], yg[tile % 2][1], route_w[:, 1, tile:tile + 1], hr[:, tile, :], ALU.mult, ALU.add) \
                        .then_inc(g["comb"].sem, g["comb"].tick(l, tile))
                for c in range(KC):
                    dve.wait_ge(g["comb_turned"].sem, g["comb_turned"].at(l, c))
                    for s, cols in streams(l):
                        ins = v.scalar_tensor_tensor(xt[:, c, cols], ps[:, 2 + c % 2, cols], modv[:, l, s, 5 * KC + c:5 * KC + c + 1],
                                                     xt[:, c, cols], ALU.mult, ALU.add)
                    ins.then_inc(g["comb_added"].sem, g["comb_added"].tick(l, c))
                dve.wait_ge(g["comb_added"].sem, g["comb_added"].at(l, KC - 1))
            reciprocal_rms(DEPTH - 1, "fin")
            scale_norm(DEPTH - 1, "fin")
            for tile in range(2):
                dve.wait_ge(g["fin_turned"].sem, g["fin_turned"].at(tile, 0))
                v.tensor_copy(hr[:, tile, 0:512], ps[:, 2 + 2 * tile, :]).then_inc(g["fin_copied"].sem, g["fin_copied"].tick(tile))

        @block.gpsimd
        def _(pool):
            q = nc.gpsimd

            def chain(ins):
                ins.then_inc(g["pchain"].sem, g["pchain"].tick())
                pool.wait_ge(g["pchain"].sem, g["pchain"].n)

            for l in range(DEPTH):
                w_all = width(l)
                nt, nb = w_all // P, w_all // BLK
                if l:
                    pool.wait_ge(g["routed"].sem, g["routed"].at(l - 1))
                for i, (dst, src) in enumerate((
                        (wr[:, :, 0:NG], t["w_router_group"][l].rearrange("(k p) n -> p k n", p=P)),
                        (wr[:, :, NG:], t["w_router_expert"][l].rearrange("(k p) n -> p k n", p=P)),
                        (br[:, 0:NG], t["b_router_group"][l].partition_broadcast(P)),
                        (br[:, NG:], t["b_router_expert"][l].partition_broadcast(P)))):
                    pool.dma_start(dst, src).then_inc(g["router_in"].sem, g["router_in"].tick(l, i, by=16))
                pool.wait_ge(g["norm_mul"].sem, g["norm_mul"].at(l, "n1", KC - 1))
                a, b = CONST_AT["swa"]
                pool.dma_start(aux[:, 3, :], t["consts"][:, a:b]).then_inc(g["swa_in"].sem, g["swa_in"].tick(l, by=16))
                ns = w_all // SEQ
                uv = u.rearrange("p g (s n) -> p g s n", n=SEQ)
                n_pad = SEQ + 16
                pool.wait_ge(g["tile_copied"].sem, g["tile_copied"].at(l, "u", 3))
                for gr in range(4):
                    one, two = pad
                    chain(q.memset(one[:, 0:ns, :], 0.0))
                    chain(q.tensor_copy(one[:, 0:ns, 8:8 + SEQ], uv[:, gr, 0:ns, :]))
                    lo, hi, off = 1, n_pad, (1, 0)
                    reach = 1
                    for step in range(gr + 1):
                        back, ahead = ((1, 0), (1, 1), (2, 2), (4, 4))[step]
                        lo, hi = ((1, 272), (2, 271), (4, 269), (8, 264))[step]
                        chain(q.tensor_tensor(two[:, 0:ns, lo:hi], one[:, 0:ns, lo - back:hi - back], one[:, 0:ns, lo + ahead:hi + ahead], ALU.add))
                        one, two = two, one
                    chain(q.tensor_scalar(two[:, 0:ns, 8:8 + SEQ], one[:, 0:ns, 8:8 + SEQ], 1.0 / (2 << gr), None, ALU.mult))
                    for side, at in ((0, 8), (1, SEQ)):
                        e = edge[:, gr, 8 * side:8 * side + 8].unsqueeze(1).broadcast_to([P, ns, 8])
                        chain(q.tensor_tensor(two[:, 0:ns, at:at + 8], two[:, 0:ns, at:at + 8], e, ALU.mult))
                    q.tensor_tensor(uv[:, gr, 0:ns, :], two[:, 0:ns, 8:8 + SEQ], uv[:, gr, 0:ns, :], ALU.subtract) \
                        .then_inc(g["pooled"].sem, g["pooled"].tick(l, gr))
                    pool.wait_ge(g["pooled"].sem, g["pooled"].at(l, gr))
                rpb = t["rpb_a"]
                for h in range(HEADS):
                    if h >= 4:
                        pool.wait_ge(g["max_done"].sem, g["max_done"].at(l, "a", "x", h - 4))
                    elif h == 3:
                        pool.wait_ge(g["max_done"].sem, g["max_done"].at(l, "c", "x", HEADS - 1))
                    for qt in range(2):
                        for j in range(2):
                            row = 7 - (2 * qt + j)
                            at = ((l * HEADS + h) * 15 + row) * RPB_REPEATS * 31 + 15
                            src = bass.AP(rpb.tensor, at, [[30, GW], [RPB_REPEATS * 31, ROWS], [1, GW]])
                            pool.dma_start(bias[h % 4][GW * j:GW * j + GW, qt], src) \
                                .then_inc(bias_in[h % 4].sem, bias_in[h % 4].tick(l, h, qt, j, by=16))
                    pool.wait_ge(bias_in[h % 4].sem, bias_in[h % 4].at(l, h, 1, 1))
                    b8 = bias[h % 4].rearrange("p q r k -> p (q r) k")
                    chain(q.tensor_tensor(b8, b8, colok[:, :].unsqueeze(1).broadcast_to([P, 8, GW]), ALU.mult))
                    q.tensor_tensor(b8, b8, colneg[:, :].unsqueeze(1).broadcast_to([P, 8, GW]), ALU.add) \
                        .then_inc(g["bias_ready"].sem, g["bias_ready"].tick(l, h))
                pool.wait_ge(g["dest_set"].sem, g["dest_set"].at(l, 1))
                pool.wait_ge(g["prep"].sem, g["prep"].at("y", l))
                pool.wait_ge(g["pick_set"].sem, (NE + 2) * (l + 1))
                pool.wait_ge(g["xt_copied"].sem, (NE + 1) * (l + 1))
                for tile in range(nt):
                    if tile >= 2:
                        pool.wait_ge(g["comb"].sem, g["comb"].at(l, tile - 2))
                    for k in range(2):
                        pool.indirect_dma_start(out=yg[tile % 2][k], out_offset=None, in_=y_rows[0:2 * w_all, :],
                                                in_offset=bass.IndirectOffsetOnAxis(ap=dest[:, k, tile:tile + 1], axis=0)) \
                            .then_inc(yg_got[tile % 2].sem, yg_got[tile % 2].tick(l, tile, k, by=16))
    return {n: s.seen for n, s in signals.items()}


def constants():
    import numpy as np

    c = np.zeros((P, NCONST), np.float32)

    def put(name, a):
        lo, hi = CONST_AT[name]
        a = np.asarray(a, np.float32).reshape(P, -1)
        c[:, lo:lo + a.shape[1]] = a

    p = np.arange(P)
    put("ident", np.eye(P))
    rot = np.zeros((P, P))
    for m in range(P):
        rot[m + 16 if m % 32 < 16 else m - 16, m] = -1.0 if m % 32 < 16 else 1.0
    put("rot", rot)
    put("mean", np.full((P, P), 1.0 / D))
    tok = np.arange(SEQ)
    inv = (np.float32(10000.0) ** (-np.arange(0, 32, 2, dtype=np.float32) / np.float32(32))).astype(np.float32)
    where = np.where((p % 64 < 32)[:, None], (tok // GW)[None, :], (tok % GW)[None, :]).astype(np.float32)
    ang = where * inv[p % 16][:, None]
    put("cos", np.cos(ang))
    put("sin", np.sin(ang))
    col = np.arange(GW)
    start = np.clip(col - 8, 0, GW - 16)
    ok = (col[None, :] >= start[:, None]) & (col[None, :] < start[:, None] + 16)
    ok = np.concatenate([ok, ok])
    put("colok", ok)
    put("colneg", np.where(ok, 0.0, NEG))
    edge = np.ones((4, 16))
    for g in range(4):
        w = 2 << g
        for i in range(8):
            edge[g, i] = w / min(w, i + w // 2)
            edge[g, 8 + i] = w / min(w, 8 - i + w // 2)
    put("edge", np.broadcast_to(edge.reshape(1, 64), (P, 64)))
    small = np.zeros((P, 32))
    small[:, 0:4] = 4 - np.arange(4)
    small[:, 4:12] = 8 - np.arange(8)
    small[:, 12] = p
    small[:, 16:20] = np.arange(4)
    put("small", small)
    key = np.arange(SEQ)
    put("swa", np.stack([np.where(np.abs(key[None, :] - (128 * q + p)[:, None]) <= 128, 0.0, NEG) for q in range(2)], 1))
    put("tri", p[:, None] < p[None, :])
    put("slots1", np.broadcast_to(1 + np.arange(512), (P, 512)))
    return c


_INS = ["x", "c", "ctx", "c_ctx", "w_mod", "b_mod", "norm1_g", "norm2_g", "w_in", "rpb_a", "w_pool", "pool_scale",
        "sink_c", "w_branch", "w_out", "w_router_group", "b_router_group", "w_router_expert", "b_router_expert",
        "w_exp_gate", "w_exp_up", "w_exp_down", "final_g"]


def kernel(**inputs):
    import numpy as _np
    import concourse.bacc as _bacc
    from concourse import mybir as _mybir
    from concourse.bass_utils import run_bass_kernel_spmd as _run

    arrays = {f"in_{n}_dram": _np.ascontiguousarray(inputs[n]) for n in _INS}
    arrays["in_rpb_a_dram"] = _np.tile(inputs["rpb_a"], (1, 1, 1, RPB_REPEATS))
    arrays["in_consts_dram"] = constants()

    def build(counts):
        nc = _bacc.Bacc("TRN2", target_bir_lowering=False, num_devices=1)
        t = {n[3:-5]: nc.dram_tensor(n, a.shape, _mybir.dt.from_np(a.dtype), kind="ExternalInput").ap() for n, a in arrays.items()}
        out = nc.dram_tensor("out_0_dram", (1, SEQ, D), F32, kind="ExternalOutput").ap()
        return nc, hybrid_block(nc, t, out, counts)

    _, counts = build(None)
    nc, _ = build(counts)
    r = _run(nc, [arrays], core_ids=[0])
    return r.results[0]["out_0_dram"]
```

```python
from contextlib import ExitStack

import concourse.bass as bass
from concourse import mybir

F32 = mybir.dt.float32
F32R = mybir.dt.float32r
BF16 = mybir.dt.bfloat16
I32 = mybir.dt.int32
U32 = mybir.dt.uint32
ALU = mybir.AluOpType
ACT = mybir.ActivationFunctionType
AX = mybir.AxisListType.X

P = 128
D = 1024
KC = D // P
SEQ = 256
NTOK = 2 * SEQ
DEPTH = 2
HD = 64
SBUF_TOP = 229344
HEADS = 8
ROWS, GW = 4, 64
SCALE = HD ** -0.5
IN_TILES = 5888 // P
COLS = {"aq": 0, "ak": 4, "av": 8, "u": 12, "cq": 16, "ck": 20, "cv": 21, "g": 22}
N_MOD = 6
MB = 384
MOD_BLOCKS, MBC = N_MOD * D // MB, MB // P
FIRST_MODS = -(-2 * D // MB)
EPS = 1e-6
NEG = -1e30
RPB_REPEATS = GW + 1
NG, EPG = 4, 8
NE = NG * EPG
FE = 512
BLK = 64
HALF = BLK // 2
LATENT, CONTEXT = slice(0, SEQ), slice(SEQ, NTOK)

CONST_COLS = {"ident": 128, "rot": 128, "mean": 128, "cos": 256, "sin": 256, "colok": 64, "colneg": 64,
              "edge": 64, "small": 32, "swa": 512, "tri": 128, "slots1": 512}
CONST_AT, _at = {}, 0
for _k, _w in CONST_COLS.items():
    CONST_AT[_k] = (_at, _at + _w)
    _at += _w
NCONST = _at


class Signal:

    def __init__(self, sem, counts):
        self.sem, self.counts, self.n, self.seen = sem, counts, 0, {}

    def tick(self, *step, by=1):
        self.n += by
        self.seen[step] = self.n
        return by

    def at(self, *step):
        return self.counts[step] if self.counts else 1


def mixer_jobs(l):
    both = l == 0
    jobs = [("tile", "ck", 0), ("tile", "cv", 0), ("rope", "ck", 0)]
    for c in range(4):
        jobs.append(("tile", "cq", c))
        if c == 1:
            jobs.append(("vt", "cv", 0))
        if c:
            jobs.append(("rope", "cq", c - 1))
    jobs += [("tile", "u", 0), ("rope", "cq", 3), ("tile", "u", 1)]
    tiles = [("tile", k, c) for k in ("u", "aq", "ak", "av") for c in range(4)][2:] + [("tile", "g", c) for c in range(16)]
    mods = [(0, n) for n in range(FIRST_MODS, MOD_BLOCKS)] + [(1, n) for n in range(MOD_BLOCKS)] if both else []
    pending = None
    for kind in ("c", "a"):
        heads = [(s, h) for s in (("x", "z") if both else ("x",)) for h in range(HEADS)]
        for i, (s, h) in enumerate(heads):
            n = 1 if not both and kind == "a" and i >= len(heads) - 2 else 16 // len(heads)
            here, tiles = tiles[:n], tiles[n:]
            jobs.append(("qk", kind, s, h))
            if pending:
                jobs.append(pending)
                if both and pending[:3] == ("pv", "a", "z"):
                    jobs.append(("ys", 0, pending[3]))
                pending = None
            if both and kind == "a" and 0 <= i - 11 < 4:
                jobs.append(("ys", 2, i - 11))
            jobs += here[:1]
            mod = mods.pop(0) if mods else None
            if mod:
                jobs.append(("modp",) + mod)
            jobs += here[1:]
            if kind == "a" and i == len(heads) - 1:
                jobs.append(("pool",))
            jobs.append(("tr", kind, s, h))
            jobs += [("vt",) + j[1:] for j in here if j[1] == "av"]
            if mod:
                jobs.append(("modt",) + mod)
            if h % 2:
                pending = ("pv", kind, s, h // 2)
    jobs.append(pending)
    if both:
        jobs += [("ys", 0, 3)] + [("ys", 1, k) for k in range(4)]
    return jobs


def hybrid_block(nc, t, out, counts=None):
    signals = {}
    y_rows = nc.dram_tensor("y_rows", (3 * NTOK + BLK, D), F32).ap()
    w_branch = t["w_branch"].rearrange("l b k n -> l (b k) n")
    ctx = ExitStack()
    with ctx:
        def sb(name, shape, dt=F32):
            return ctx.enter_context(nc.sbuf_tensor(name, shape, dt))

        def signal(name):
            s = Signal(ctx.enter_context(nc.semaphore(name)), counts and counts[name])
            signals[name] = s
            return s

        def placed(name, shape, at, dt=F32):
            return nc.alloc_sbuf_tensor_at(name, shape, dt, offset=at)

        MOE_AT = SBUF_TOP - 96 * 1024
        ARENA_AT = MOE_AT - 46 * 1024
        HT_AT = ARENA_AT - 4 * KC * NTOK
        WS_AT = HT_AT - 3 * 4 * D
        xt = sb("xt", [P, KC, NTOK])
        ht = placed("ht", [P, KC, NTOK], HT_AT)
        arena = placed("arena", [P, 46 * 256], ARENA_AT)
        moe = placed("moe", [P, 96 * 256], MOE_AT)
        ws = placed("ws", [P, 3, 8, P], WS_AT)
        aux = sb("aux", [P, 4, 512])
        mrow = sb("mrow", [P, 512])
        ident, rot, mean_w = sb("ident", [P, P]), sb("rot", [P, P]), sb("mean_w", [P, P])
        cos, sin = sb("cos", [P, SEQ]), sb("sin", [P, SEQ])
        colok, colneg = sb("colok", [P, GW]), sb("colneg", [P, GW])
        edge = sb("edge", [P, 4, 16])
        small = sb("small", [P, 32])
        tri_b, ones_b = sb("tri_b", [P, P], BF16), sb("ones_b", [P, P], BF16)
        cond = sb("cond", [P, KC, 32])
        colv = sb("colv", [P, 144])
        modv = sb("modv", [P, DEPTH, 2, N_MOD * KC])
        gain = sb("gain", [P, 2, 2, KC])
        half_gate = sb("half_gate", [P, 2, KC])
        sink = sb("sink", [P, DEPTH, HEADS])
        wr = sb("wr", [P, KC, NG + NE])
        br = sb("br", [P, NG + NE])
        stat = sb("stat", [P, 2, 16])
        eps = sb("eps", [P, 1])
        route_w = sb("route_w", [P, 2, 4])
        dest = sb("dest", [P, 2, 4], U32)
        slots1 = sb("slots1", [P, NTOK])
        n_of = sb("n_of", [1, NE], I32)
        start_of = sb("start_of", [1, NE], I32)
        ps = ctx.enter_context(nc.psum_tensor("ps", [P, 8, 512], F32))

        def part(base, kib, size, *dims, dt=F32):
            v = base[:, int(kib * 256):int((kib + size) * 256)]
            if dt is not F32:
                v = v.bitcast(dt)
            if len(dims) == 2:
                v = v.rearrange("p (a b) -> p a b", b=dims[1])
            if len(dims) == 3:
                v = v.rearrange("p (a b c) -> p a b c", b=dims[1], c=dims[2])
            return v

        aq, ak = part(arena, 0, 8, 4, NTOK), part(arena, 8, 8, 4, NTOK)
        av, u = part(arena, 16, 8, 4, 512), part(arena, 24, 8, 4, NTOK)
        cq, ck = part(arena, 32, 8, 4, NTOK), part(arena, 40, 4, 2, NTOK)
        cv = part(arena, 44, 2, 4, P)
        mt = part(arena, 8, 16, KC, NTOK)
        hr = part(arena, 0, 16, 4, D)
        xg = [part(arena, 24 + 2 * i, 2, KC, BLK) for i in range(3)]
        pick = [part(arena, 30 + i, 1, 4, BLK) for i in range(3)]
        hid = [part(arena, 34 + i, 1) for i in range(3)]
        hid_t = [part(arena, 37 + i, 1, 2, P) for i in range(3)]
        ysb = [part(arena, 40 + 2 * i, 2) for i in range(3)]
        sq_tile = [part(arena, 32 + 4 * i, 4, KC, P) for i in range(2)]
        yg = [[part(arena, 16 + 8 * i + 4 * k, 4) for k in range(2)] for i in range(2)]
        act_g = [aux[:, i, 0:256] for i in range(3)]
        r = part(arena, 16, 8)
        place1 = part(arena, 33, 1)[:, 0:4 * (NE + 2)].rearrange("p (t e) -> p t e", t=4)
        wgu = [moe[:, 48 * 256 * i:(48 * i + 32) * 256].rearrange("p (k g n) -> p k g n", k=KC, g=2) for i in range(2)]
        wd = [part(moe, 48 * i + 32, 16, 4, D) for i in range(2)]
        mw = [part(moe, 12 * i, 12, KC, MB) for i in range(2)]
        w_hi = placed("w_hi", [P, 2, KC, P], MOE_AT + 24 * 1024, F32R)
        w_lo = placed("w_lo", [P, 3, KC, P], WS_AT, F32R)
        ys_hi = placed("ys_hi", [P, 12, NTOK], MOE_AT, F32R)
        ys_lo = [placed(f"y{b}_lo", [P, 4, NTOK], ARENA_AT + kib * 1024, F32R) for b, kib in enumerate((0, 24, 32))]
        ht_hi = placed("ht_hi", [P, KC, NTOK], MOE_AT + 32 * 1024, F32R)
        ht_lo = placed("ht_lo", [P, KC, NTOK], HT_AT, F32R)
        mt_hi = placed("mt_hi", [P, KC, NTOK], MOE_AT + 48 * 1024, F32R)
        mt_lo = placed("mt_lo", [P, KC, NTOK], ARENA_AT + 8 * 1024, F32R)
        gates = part(moe, 48, 32, 16, NTOK)
        rows_in = part(moe, 48, 16, 4, D)
        vec_rows = part(moe, 80, 1, 2, P)
        cond_rows = part(moe, 82, 4)
        prob = [part(moe, 80 + 4 * i, 4, 2, 512) for i in range(2)]
        prob_t = [part(moe, 88 + 4 * i, 4, 4, SEQ) for i in range(2)]
        cv_raw = prob[1][:, 0, :]
        ck_raw, rt0, rt1 = prob[0][:, 0, :], prob[0][:, 1, 0:SEQ], prob[0][:, 1, SEQ:]
        sq, rs = [aux[:, i, :] for i in range(3)], aux[:, 3, :]
        swa = aux[:, 3, :].rearrange("p (q k) -> p q k", q=2)
        aux_flat = aux[:, :, :].rearrange("p a b -> p (a b)")
        pad = [aux_flat[:, i * 544:(i + 1) * 544].rearrange("p (s n) -> p s n", s=2) for i in range(2)]
        bias = [aux[:, i, :].rearrange("p (q r k) -> p q r k", q=2, r=ROWS) for i in range(4)]
        tile_bank, score_bank = [ps[:, i, :] for i in range(2)], ps[:, 2:4, :]
        prob_bank = ps[:, 4:6, :].rearrange("p b (k q) -> p (b k) q", q=SEQ)
        pv_bank, misc = ps[:, 6, :], ps[:, 7, :]

        names = """ident_in mean_in consts_in rows_in_done vecs_in router_in swa_in wst0 wst1 wst2 mwt0 mwt1 bias0 bias1 bias2
            bias3 gu_in0 gu_in1 wd_in0 wd_in1 y_saved0 y_saved1 yo_saved yt_saved yg_got0 yg_got1 out_saved
            in_turned in_copied prep vec_ready cond_silu cond_turned cond_cols sq_done mean_done rstd_sqrt
            rstd_done norm_mul norm_add h_hi h_lo w_hi_set w_lo_set mt_hi_set mt_lo_set vt_done vt_copied
            tile_done tile_copied rope_done rope_out qk_done max_done exp_done scaled pt_done pt_copied_d
            pt_copied_a pv_done pv_copied modp_done modp_copied modt_done mod_summed mod_ready pooled
            pool_done pool_copied bias_ready gate_done gate_tanh ys_hi_set ys_lo_set branches_ab branch_done
            merged out_done added dchain achain pchain logits_t logits_copied logits_done hturn_done
            hrow_copied r_exp r_onehot r_pos r_exp_done routed pick_set picko_set dest_set xt_done xt_copied
            gu_done silu_done hid_done0 hid_done1 hidt_done hidt_copied down_done0 down_done1 y_copied0
            y_copied1 xto_done xto_copied guo_done siluo_done hido_done hidto_done hidto_copied downo_done
            yo_copied comb_half comb comb_turned comb_added fin_scaled fin_turned fin_copied""".split()
        g = {n: signal(n) for n in names}
        ws_in = [g[f"wst{i}"] for i in range(3)]
        mw_in = [g[f"mwt{i}"] for i in range(2)]
        bias_in = [g[f"bias{i}"] for i in range(4)]
        gu_in, wd_in = [g["gu_in0"], g["gu_in1"]], [g["wd_in0"], g["wd_in1"]]
        y_saved = [g["y_saved0"], g["y_saved1"]]
        yg_got = [g["yg_got0"], g["yg_got1"]]
        hid_done, down_done = [g["hid_done0"], g["hid_done1"]], [g["down_done0"], g["down_done1"]]
        y_copied = [g["y_copied0"], g["y_copied1"]]

        def width(l):
            return NTOK if l == 0 else SEQ

        def streams(l):
            return [(0, LATENT), (1, CONTEXT)] if l == 0 else [(0, LATENT)]

        def kt_of(kind, h):
            return (ck[HD * (h % 2):HD * (h % 2) + HD, h // 4, :] if kind == "c"
                    else ak[HD * (h % 2):HD * (h % 2) + HD, h // 2, :])

        def q_of(kind):
            return cq if kind == "c" else aq

        def v_of(kind, h, tile):
            return (cv[:, tile, HD * (h // 4):HD * (h // 4) + HD] if kind == "c"
                    else av[:, tile, HD * h:HD * h + HD])

        def stream_items(l):
            items, now, later = [], [], []
            for j in mixer_jobs(l):
                if j[0] == "qk":
                    items += now
                    now, later = later, []
                if j[0] == "tile":
                    a = COLS[j[1]] + j[2]
                    items.append((t["w_in"][l, :, a * P:(a + 1) * P].rearrange("(k p) n -> p k n", p=P), 8, j))
                    items += now
                    now = []
                if j[0] == "pool":
                    items.append((t["w_pool"][l].rearrange("g c e -> c g e"), 4, j))
                if j[0] == "modp":
                    later.append((None, 0, j))
            items += now + later
            for n in range(KC):
                a = COLS["g"] + 16 + n
                items.append((t["w_in"][l, :, a * P:(a + 1) * P].rearrange("(k p) n -> p k n", p=P), 8, ("g2", n)))
                for b0, m in ((0, 8), (8, 4)):
                    items.append((w_branch[l, b0 * P:(b0 + m) * P, n * P:(n + 1) * P].rearrange("(k p) n -> p k n", p=P),
                                  m, ("wb", b0, n)))
            for n in range(KC):
                items.append((t["w_out"][l, :, n * P:(n + 1) * P].rearrange("(k p) n -> p k n", p=P), 8, ("wo", n)))
            return items

        def plan_banks():
            order = [("in", c) for c in range(KC)]
            for l in range(DEPTH):
                for j in mixer_jobs(l):
                    if j[0] == "tile":
                        order.append((l,) + j[1:])
                    if j[0] == "pool":
                        order += [(l, "pool", gr) for gr in range(4)]
                order += [(l, "g2", n) for n in range(KC)] + [(l, "wo", n) for n in range(KC)]
            return {step: i % 2 for i, step in enumerate(order)}

        tile_banks = plan_banks()
        ws_slots, split_order = {}, []
        for l in range(DEPTH):
            for _, _, j in stream_items(l):
                if j[0] != "modp":
                    ws_slots[(l, j)] = len(ws_slots) % 3
                if j[0] in ("tile", "g2", "wo") or (j[0] == "wb" and l == 0):
                    split_order.append((l, j))
        split_at = {item: i for i, item in enumerate(split_order)}

        def ws_release(l, job):
            if job[0] == "tile":
                return g["tile_done"], (l, job[1], job[2])
            if job[0] == "pool":
                return g["pool_done"], (l, 3)
            if job[0] == "g2":
                return g["gate_done"], (l, job[1])
            if job[0] == "wb" and job[1] == 0 and l == 0:
                return g["branches_ab"], (l, job[2])
            if job[0] == "wb":
                return g["branch_done"], (l, job[2])
            return g["out_done"], (l, job[1])

        block = ctx.enter_context(nc.Block())

        @block.sync
        def _(sp):
            def const(name, dst):
                a, b = CONST_AT[name]
                sp.dma_start(dst, t["consts"][:, a:b]).then_inc(g["consts_in"].sem, g["consts_in"].tick(name, by=16))

            for i, (src, c) in enumerate((("x", 0), ("ctx", 2))):
                sp.dma_start(rows_in[:, c:c + 2, :], t[src][0].rearrange("(t p) d -> p t d", p=P)) \
                    .then_inc(g["rows_in_done"].sem, g["rows_in_done"].tick(i, by=16))
            a, b = CONST_AT["ident"]
            sp.dma_start(ident[:, :], t["consts"][:, a:b]).then_inc(g["ident_in"].sem, g["ident_in"].tick(by=16))
            a, b = CONST_AT["mean"]
            sp.dma_start(mean_w[:, :], t["consts"][:, a:b]).then_inc(g["mean_in"].sem, g["mean_in"].tick(by=16))
            sp.dma_start(vec_rows[0:96, 0, :], t["b_mod"].rearrange("l (a p) -> (l a) p", p=P)) \
                .then_inc(g["vecs_in"].sem, g["vecs_in"].tick(0, by=16))
            for i, (name, n) in enumerate((("norm1_g", 16), ("norm2_g", 16), ("final_g", 8), ("pool_scale", 8))):
                src = t[name].rearrange("(a p) -> a p", p=P) if name == "final_g" else t[name].rearrange("l (a p) -> (l a) p", p=P)
                at = (0, 16, 32, 40)[i]
                sp.dma_start(vec_rows[at:at + n, 1, :], src).then_inc(g["vecs_in"].sem, g["vecs_in"].tick(1 + i, by=16))
            sp.dma_start(cond_rows[0:1, :], t["c"]).then_inc(g["vecs_in"].sem, g["vecs_in"].tick(5, by=16))
            sp.dma_start(cond_rows[1:2, :], t["c_ctx"].rearrange("(a d) -> a d", a=1)) \
                .then_inc(g["vecs_in"].sem, g["vecs_in"].tick(6, by=16))
            sp.dma_start(sink[:, :, :].rearrange("p l h -> p (l h)"),
                         t["sink_c"].rearrange("l h -> (l h)").partition_broadcast(P)) \
                .then_inc(g["vecs_in"].sem, g["vecs_in"].tick(7, by=16))

            mods = []

            def load_mod(l, n):
                i = len(mods)
                mods.append((l, n))
                if i >= 2:
                    sp.wait_ge(g["modp_done"].sem, g["modp_done"].at(*mods[i - 2]))
                sp.dma_start(mw[i % 2], t["w_mod"][l, :, n * MB:(n + 1) * MB].rearrange("(k p) n -> p k n", p=P)) \
                    .then_inc(mw_in[i % 2].sem, mw_in[i % 2].tick(l, n, by=16))

            def load_expert(e_src, slot, pieces=range(6)):
                for i in pieces:
                    if i < 4:
                        ks = slice(4 * (i // 2), 4 * (i // 2) + 4)
                        w = (t["w_exp_gate"], t["w_exp_up"])[i % 2]
                        sp.dma_start(wgu[slot][:, ks, i % 2, :], e_src(w).rearrange("(k p) n -> p k n", p=P)[:, ks, :]) \
                            .then_inc(gu_in[slot].sem, 16)
                    else:
                        ks = slice(2 * (i - 4), 2 * (i - 4) + 2)
                        sp.dma_start(wd[slot][:, ks, :], e_src(t["w_exp_down"]).rearrange("(k p) n -> p k n", p=P)[:, ks, :]) \
                            .then_inc(wd_in[slot].sem, 16)

            for n in range(FIRST_MODS):
                load_mod(0, n)
            for name, dst in (("rot", rot), ("cos", cos), ("sin", sin), ("colok", colok),
                              ("colneg", colneg), ("small", small), ("slots1", slots1)):
                const(name, dst[:, :])
            const("edge", edge[:, :, :].rearrange("p a b -> p (a b)"))
            const("tri", arena[:, 0:P])
            held = []
            for l in range(DEPTH):
                for src, m, job in stream_items(l):
                    if job[0] == "modp":
                        load_mod(job[1], job[2])
                    else:
                        slot = len(held) % 3
                        if len(held) >= 3:
                            last, step = held[-3]
                            sp.wait_ge(last.sem, last.at(*step))
                        sp.dma_start(ws[:, slot, 0:m, :], src).then_inc(ws_in[slot].sem, ws_in[slot].tick(l, job, by=16))
                        held.append(ws_release(l, job))
                sp.wait_ge(g["out_done"].sem, g["out_done"].at(l, KC - 1))
                load_expert(lambda w: w[l, 0], 0)
                load_expert(lambda w: w[l, 1], 1)
                with sp.Fori(1, NE // 2) as i:
                    for slot in range(2):
                        def source(w):
                            return w[l, bass.ds(2 * i + slot, 1)].rearrange("a k n -> (a k) n")

                        sp.wait_ge(g["hidt_done"].sem, NE * l + 2 * i + slot - 1)
                        load_expert(source, slot, range(4))
                        sp.wait_ge(down_done[slot].sem, 16 * l + i)
                        load_expert(source, slot, range(4, 6))
            sp.wait_ge(g["fin_copied"].sem, g["fin_copied"].at(1))
            sp.wait_ge(g["prep"].sem, g["prep"].at("fin", 1))
            sp.dma_start(out[0].rearrange("(t p) d -> p t d", p=P), hr[:, 0:2, :]) \
                .then_inc(g["out_saved"].sem, g["out_saved"].tick(0, by=16))
            sp.wait_ge(g["out_saved"].sem, 16)

        @block.tensor
        def _(pe):
            free = {}

            def claim(bank):
                if bank in free:
                    s, step = free.pop(bank)
                    pe.wait_ge(s.sem, s.at(*step))

            def next_tile_bank(*step):
                claim(tile_banks[step])
                return tile_banks[step]

            def product(l, job, bank, cols, hi, lo, ready=None, rows=range(KC), hi_at=0):
                slot, w = ws_slots[(l, job)], w_hi[:, split_at[(l, job)] % 2]
                pe.wait_ge(g["w_lo_set"].sem, g["w_lo_set"].at(l, job))
                for i, k in enumerate(rows):
                    if ready:
                        pe.wait_ge(g[ready].sem, g[ready].at(l, k))
                    a_hi, a_lo = hi[:, hi_at + i, 0:cols], lo[:, i, 0:cols]
                    pe.matmul(ps[:, bank, 0:cols], w[:, k, :], a_hi, start=(i == 0), stop=False)
                    pe.matmul(ps[:, bank, 0:cols], w[:, k, :], a_lo, start=False, stop=False)
                    mm = pe.matmul(ps[:, bank, 0:cols], w_lo[:, slot, k, :], a_hi, start=False, stop=(k == rows[-1]))
                return mm

            def weights(l, job):
                slot = ws_slots[(l, job)]
                pe.wait_ge(ws_in[slot].sem, ws_in[slot].at(l, job))
                return ws[:, slot]

            pe.wait_ge(g["ident_in"].sem, 16)
            pe.wait_ge(g["rows_in_done"].sem, 32)
            for c in range(KC):
                bank = next_tile_bank("in", c)
                for tile in range(4):
                    mm = pe.transpose(ps[:, bank, tile * P:(tile + 1) * P], rows_in[:, tile, c * P:(c + 1) * P], ident[:, :])
                mm.then_inc(g["in_turned"].sem, g["in_turned"].tick(c))
                free[bank] = (g["prep"], ("xt", c)) if c % 2 else (g["in_copied"], (c,))
            pe.wait_ge(g["vecs_in"].sem, 16 * 8)
            pe.transpose(misc[:, 0:96], vec_rows[0:96, 0, :], ident[0:96, 0:96])
            pe.transpose(misc[:, 96:144], vec_rows[0:48, 1, :], ident[0:48, 0:48])
            pe.wait_ge(g["cond_silu"].sem, g["cond_silu"].at(0))
            for c in range(KC):
                mm = pe.transpose(misc[:, 144 + 2 * c:146 + 2 * c], cond_rows[0:2, c * P:(c + 1) * P], ident[0:2, 0:2])
            mm.then_inc(g["cond_turned"].sem, g["cond_turned"].tick(0))
            free[7] = (g["cond_cols"], (0,))
            pe.wait_ge(g["cond_cols"].sem, g["cond_cols"].at(0))

            n_mod = [0]

            def modp(l, n):
                i = n_mod[0]
                n_mod[0] += 1
                claim(7)
                pe.wait_ge(mw_in[i % 2].sem, mw_in[i % 2].at(l, n))
                for k in range(KC):
                    q = k % 4
                    mm = pe.matmul(misc[32 * q:32 * q + 32, 0:MB], cond[:, k, :], mw[i % 2][:, k, :], start=(k < 4), stop=(k >= 4))
                mm.then_inc(g["modp_done"].sem, g["modp_done"].tick(l, n))
                free[7] = (g["modp_copied"], (l, n))

            def modt(l, n):
                claim(7)
                for q in range(MBC):
                    mm = pe.transpose(misc[:, q * P:(q + 1) * P], mrow[:, q * P:(q + 1) * P], ident[:, :])
                mm.then_inc(g["modt_done"].sem, g["modt_done"].tick(l, n))
                free[7] = (g["mod_summed"], (l, n))

            def mean(l, which, c):
                w = width(l) if which != "n1" else NTOK
                if c == 0:
                    claim(6)
                pe.wait_ge(g["sq_done"].sem, g["sq_done"].at(l, which, c))
                pe.matmul(pv_bank[:, 0:w], mean_w[:, :], sq[c % 3][:, 0:w], start=(c == 0), stop=(c == KC - 1)) \
                    .then_inc(g["mean_done"].sem, g["mean_done"].tick(l, which, c))
                if c == KC - 1:
                    free[6] = (g["rstd_sqrt"], (l, which))

            pe.wait_ge(g["mean_in"].sem, 16)
            for c in range(KC):
                mean(0, "n1", c)
            for n in range(FIRST_MODS):
                modp(0, n)
                modt(0, n)

            for l in range(DEPTH):
                w_all = width(l)
                if l == 0:
                    pe.wait_ge(g["consts_in"].sem, g["consts_in"].at("tri"))
                for j in mixer_jobs(l):
                    if j[0] == "tile":
                        kind, c = j[1:]
                        bank = next_tile_bank(l, kind, c)
                        cols = NTOK if kind in ("ak", "av", "ck", "cv") else w_all
                        mm = product(l, j, bank, cols, ht_hi, ht_lo, "h_lo" if kind == "ck" else None)
                        mm.then_inc(g["tile_done"].sem, g["tile_done"].tick(l, kind, c))
                        free[bank] = (g["tile_copied"], (l, kind, c))
                    elif j[0] == "rope":
                        kind, c = j[1:]
                        claim(7)
                        pe.wait_ge(g["tile_copied"].sem, g["tile_copied"].at(l, kind, c))
                        src = ck_raw[:, 0:SEQ] if kind == "ck" else cq[:, c, 0:SEQ]
                        pe.matmul(misc[:, 0:SEQ], rot[:, :], src, start=True, stop=True) \
                            .then_inc(g["rope_done"].sem, g["rope_done"].tick(l, kind, c))
                        free[7] = (g["rope_out"], (l, kind, c))
                    elif j[0] == "vt":
                        kind, c = j[1:]
                        claim(7)
                        pe.wait_ge(g["tile_copied"].sem, g["tile_copied"].at(l, kind, c))
                        src = cv_raw if kind == "cv" else gates[:, c, :]
                        for tile in range(4):
                            mm = pe.transpose(misc[:, tile * P:(tile + 1) * P], src[:, tile * P:(tile + 1) * P], ident[:, :])
                        mm.then_inc(g["vt_done"].sem, g["vt_done"].tick(l, kind, c))
                        free[7] = (g["vt_copied"], (l, kind, c))
                    elif j[0] == "qk":
                        kind, s, h = j[1:]
                        claim("s")
                        if kind == "c":
                            if s == "x" and h == 0:
                                pe.wait_ge(g["rope_out"].sem, g["rope_out"].at(l, "ck", 0))
                            if s == "x" and h < HEADS:
                                if h // 2 < 3:
                                    pe.wait_ge(g["rope_out"].sem, g["rope_out"].at(l, "cq", h // 2))
                                else:
                                    pe.wait_ge(g["rope_out"].sem, g["rope_out"].at(l, "cq", 3))
                            pe.wait_ge(g["tile_copied"].sem, g["tile_copied"].at(l, "cq", 3))
                            pe.wait_ge(g["vt_copied"].sem, g["vt_copied"].at(l, "cv", 0))
                        else:
                            pe.wait_ge(g["vt_copied"].sem, g["vt_copied"].at(l, "av", 3))
                        rows = slice(HD * (h % 2), HD * (h % 2) + HD)
                        keys = slice(0, NTOK) if s == "x" else CONTEXT
                        q0 = 0 if s == "x" else SEQ
                        n = NTOK if s == "x" else SEQ
                        for qt in range(2):
                            mm = pe.matmul(score_bank[:, qt, 0:n], q_of(kind)[rows, h // 2, q0 + qt * P:q0 + (qt + 1) * P],
                                           kt_of(kind, h)[:, keys], start=True, stop=True)
                        mm.then_inc(g["qk_done"].sem, g["qk_done"].tick(l, kind, s, h))
                        free["s"] = (g["exp_done"], (l, kind, s, h))
                    elif j[0] == "tr":
                        kind, s, h = j[1:]
                        claim("t")
                        claim("t2")
                        pe.wait_ge(g["scaled"].sem, g["scaled"].at(l, kind, s, h))
                        for tile in range(4 if s == "x" else 2):
                            for qt in range(2):
                                mm = pe.transpose(prob_bank[:, tile, qt * P:(qt + 1) * P],
                                                  prob[h % 2][:, qt, tile * P:(tile + 1) * P], ident[:, :])
                            if tile == 1:
                                mm.then_inc(g["pt_done"].sem, g["pt_done"].tick(l, kind, s, h, 0))
                            if tile == 3:
                                mm.then_inc(g["pt_done"].sem, g["pt_done"].tick(l, kind, s, h, 1))
                        free["t"] = (g["pt_copied_a"], (l, kind, s, h))
                        if s == "x":
                            free["t2"] = (g["pt_copied_d"], (l, kind, s, h))
                    elif j[0] == "pv":
                        kind, s, pair = j[1:]
                        claim(6)
                        pe.wait_ge(g["pt_copied_a"].sem, g["pt_copied_a"].at(l, kind, s, 2 * pair + 1))
                        if s == "x":
                            pe.wait_ge(g["pt_copied_d"].sem, g["pt_copied_d"].at(l, kind, s, 2 * pair + 1))
                        n = 4 if s == "x" else 2
                        for tile in range(n):
                            for hh in range(2):
                                mm = pe.matmul(pv_bank[HD * hh:HD * hh + HD, 0:SEQ], v_of(kind, 2 * pair + hh, tile + (4 - n)),
                                               prob_t[hh][:, tile, :], start=(tile == 0), stop=(tile == n - 1))
                        mm.then_inc(g["pv_done"].sem, g["pv_done"].tick(l, kind, s, pair))
                        free[6] = (g["pv_copied"], (l, kind, s, pair))
                    elif j[0] == "modp":
                        modp(*j[1:])
                    elif j[0] == "modt":
                        modt(*j[1:])
                    elif j[0] == "pool":
                        w = weights(l, j)
                        for gr in range(4):
                            bank = next_tile_bank(l, "pool", gr)
                            pe.wait_ge(g["pooled"].sem, g["pooled"].at(l, gr))
                            mm = pe.matmul(ps[:, bank, 0:w_all], w[:, gr, :], u[:, gr, 0:w_all], start=True, stop=True)
                            mm.then_inc(g["pool_done"].sem, g["pool_done"].tick(l, gr))
                            free[bank] = (g["pool_copied"], (l, gr))
                for key in ("s", "t", "t2", 6, 7):
                    claim(key)
                pe.wait_ge(g["pool_copied"].sem, g["pool_copied"].at(l, 3))
                pe.wait_ge(g["pv_copied"].sem, g["pv_copied"].at(l, "a", "z" if l == 0 else "x", 3))
                ys = (aq, u, cq)
                for n in range(KC):
                    bank = next_tile_bank(l, "g2", n)
                    mm = product(l, ("g2", n), bank, w_all, ht_hi, ht_lo)
                    mm.then_inc(g["gate_done"].sem, g["gate_done"].tick(l, n))
                    free[bank] = (g["gate_tanh"], (l, n))
                    for b in range(3):
                        if l == 0:
                            if n == 0:
                                for k in range(4):
                                    pe.wait_ge(g["ys_lo_set"].sem, g["ys_lo_set"].at(b, k))
                            if b == 0 and n >= 2:
                                pe.wait_ge(g["merged"].sem, g["merged"].at(l, n - 2))
                            mm = product(l, ("wb", 0 if b < 2 else 8, n), 2 + 3 * (n % 2) + b, w_all, ys_hi, ys_lo[b],
                                         rows=range(4, 8) if b == 1 else range(4), hi_at=4 * b)
                            if b == 1:
                                mm.then_inc(g["branches_ab"].sem, g["branches_ab"].tick(l, n))
                            continue
                        if b != 1:
                            w = weights(l, ("wb", 0 if b == 0 else 8, n))
                        if b == 0 and n >= 2:
                            pe.wait_ge(g["merged"].sem, g["merged"].at(l, n - 2))
                        for k in range(4):
                            mm = pe.matmul(ps[:, 2 + 3 * (n % 2) + b, 0:w_all], w[:, (4 * b + k) % 8, :], ys[b][:, k, 0:w_all],
                                           start=(k == 0), stop=(k == 3))
                    mm.then_inc(g["branch_done"].sem, g["branch_done"].tick(l, n))
                for n in range(KC):
                    bank = next_tile_bank(l, "wo", n)
                    mm = product(l, ("wo", n), bank, w_all, mt_hi, mt_lo, None if n else "mt_lo_set")
                    mm.then_inc(g["out_done"].sem, g["out_done"].tick(l, n))
                    free[bank] = (g["added"], (l, n))
                    if n:
                        mean(l, "n2", n - 1)
                nt = w_all // P
                mean(l, "n2", KC - 1)
                pe.wait_ge(g["router_in"].sem, g["router_in"].at(l, 3))
                claim(6)
                for k in range(KC):
                    pe.wait_ge(g["norm_add"].sem, g["norm_add"].at(l, "n2", k))
                    mm = pe.matmul(ps[0:NG + NE, 6, 0:w_all], wr[:, k, :], ht[:, k, 0:w_all], start=(k == 0), stop=(k == KC - 1))
                mm.then_inc(g["logits_t"].sem, g["logits_t"].tick(l))
                pe.wait_ge(g["logits_copied"].sem, g["logits_copied"].at(l))
                for tile in range(nt):
                    mm = pe.transpose(misc[:, tile * 64:tile * 64 + 36], mrow[0:36, tile * P:(tile + 1) * P], ident[0:36, 0:36])
                mm.then_inc(g["logits_done"].sem, g["logits_done"].tick(l))
                for tile in range(nt):
                    for half in range(2):
                        bank = 2 + (2 * tile + half) % 4
                        claim(bank)
                        for c in range(4):
                            mm = pe.transpose(ps[:, bank, c * P:(c + 1) * P], ht[:, 4 * half + c, tile * P:(tile + 1) * P], ident[:, :])
                        mm.then_inc(g["hturn_done"].sem, g["hturn_done"].tick(l, tile, half))
                        free[bank] = (g["hrow_copied"], (l, tile, half))
                msk = r[:, 1024:1024 + 64].bitcast(BF16).rearrange("p (t e) -> p t e", e=NE)
                pe.wait_ge(g["r_onehot"].sem, g["r_onehot"].at(l))
                for tile in range(nt):
                    for before in range(tile):
                        pe.matmul(ps[:, 6, tile * NE:(tile + 1) * NE], ones_b[:, :], msk[:, before, :], start=(before == 0), stop=False)
                    pe.matmul(ps[:, 6, tile * NE:(tile + 1) * NE], tri_b[:, :], msk[:, tile, :], start=(tile == 0), stop=True)
                for tile in range(nt):
                    mm = pe.matmul(ps[:, 6, 4 * NE:5 * NE], ones_b[:, :], msk[:, tile, :], start=(tile == 0), stop=(tile == nt - 1))
                mm.then_inc(g["r_pos"].sem, g["r_pos"].tick(l))
                nb = w_all // BLK
                for bank in range(8):
                    claim(bank)
                pe.wait_ge(g["routed"].sem, g["routed"].at(l))

                pe.wait_ge(g["hrow_copied"].sem, g["hrow_copied"].at(l, nt - 1, 1))

                def pick_x(dst_bank, picks, sem, chunks=range(KC)):
                    for c in chunks:
                        for tile in range(nt):
                            mm = pe.matmul(ps[:, dst_bank, c * BLK:(c + 1) * BLK], hr[:, tile, c * P:(c + 1) * P], picks[:, tile, :],
                                           start=(tile == 0), stop=(tile == nt - 1))
                    if chunks[-1] == KC - 1:
                        mm.then_inc(sem, 1)

                def gate_up(bank, xs, w, sem):
                    for k in range(KC):
                        for j in range(2):
                            mm = pe.matmul(ps[BLK * j:BLK * j + BLK, bank, :].rearrange("p (g n) -> p g n", g=2), xs[:, k, :],
                                           w[:, k, :, 256 * j:256 * j + 256], start=(k == 0), stop=(k == KC - 1))
                    mm.then_inc(sem, 1)

                def turn_h(bank, src, sem):
                    for c in range(2):
                        mm = pe.transpose(ps[:, bank, c * P:(c + 1) * P], src[:, c * P:(c + 1) * P], ident[:, :])
                    mm.then_inc(sem, 1)

                def down(bank, src, w, sem):
                    for k in range(4):
                        for j in range(2):
                            mm = pe.matmul(ps[BLK * j:BLK * j + BLK, bank, :], src[:, k % 2, BLK * (k // 2):BLK * (k // 2) + BLK],
                                           w[:, k, 512 * j:512 * j + 512], start=(k == 0), stop=(k == 3))
                    mm.then_inc(sem, 1)

                if l == 0:
                    n_more = pe.alloc_register("pe_more")
                    pe.reg_mov(n_more, 0)
                pe.wait_ge(g["pick_set"].sem, (NE + 2) * l + 1)
                pick_x(0, pick[0], g["xt_done"].sem)
                with pe.Fori(0, NE // 2) as i:
                    for s in range(2):
                        e, done = 2 * i + s, NE * l + 2 * i + s
                        mine = 16 * l + i
                        pe.wait_ge(g["xt_copied"].sem, done + l + 1)
                        pe.wait_ge(gu_in[s].sem, (mine + 1) * 64)
                        gate_up(2 + s, xg[s], wgu[s], g["gu_done"].sem)
                        pe.wait_ge(g["pick_set"].sem, done + 2 * l + 2)
                        pick_x(0, pick[1 - s], g["xt_done"].sem, range(4))
                        n = pe.value_load(n_of[0:1, bass.ds(e, 1)], min_val=0, max_val=NTOK)
                        pe.wait_ge(wd_in[s].sem, (mine + 1) * 32)
                        pe.nop(nofuse=True)
                        with pe.If(n > BLK):
                            with pe.Fori(1, nb) as b:
                                with pe.If(n > b * BLK):
                                    more = pe.snap(n_more, min_val=0, max_val=64)
                                    pe.wait_ge(g["picko_set"].sem, more + 1)
                                    pick_x(7, pick[2], g["xto_done"].sem)
                                    pe.wait_ge(g["xto_copied"].sem, more + 1)
                                    pe.wait_ge(g["yo_copied"].sem, more + 1)
                                    gate_up(6, xg[2], wgu[s], g["guo_done"].sem)
                                    pe.wait_ge(g["hido_done"].sem, more + 1)
                                    turn_h(7, hid[2], g["hidto_done"].sem)
                                    pe.wait_ge(g["hidto_copied"].sem, more + 1)
                                    down(6, hid_t[2], wd[s], g["downo_done"].sem)
                                    pe.reg_add(n_more, n_more, 1)
                                pe.nop(nofuse=True)
                        pe.nop()
                        pe.wait_ge(hid_done[s].sem, mine + 2)
                        turn_h(1, hid[s], g["hidt_done"].sem)
                        pick_x(0, pick[1 - s], g["xt_done"].sem, range(4, KC))
                        pe.wait_ge(g["hidt_copied"].sem, done + 1)
                        pe.wait_ge(y_copied[s].sem, mine + 1)
                        down(4 + s, hid_t[s], wd[s], down_done[s].sem)
                after = (l + 1, "n1") if l + 1 < DEPTH else (l, "fin")
                pe.wait_ge(y_copied[1].sem, 16 * (l + 1) + 1)
                def mean_tile(tile):
                    if tile == 0:
                        claim(6)
                    pe.wait_ge(g["sq_done"].sem, g["sq_done"].at(*after, tile))
                    for c in range(KC):
                        mm = pe.matmul(pv_bank[:, tile * P:(tile + 1) * P], mean_w[:, :], sq_tile[tile % 2][:, c, :],
                                       start=(c == 0), stop=(c == KC - 1))
                    mm.then_inc(g["mean_done"].sem, g["mean_done"].tick(*after, tile))

                for tile in range(nt):
                    banks = 2 + 2 * (tile % 2), 3 + 2 * (tile % 2)
                    for bank in banks:
                        claim(bank)
                    pe.wait_ge(g["comb"].sem, g["comb"].at(l, tile))
                    for c in range(KC):
                        mm = pe.transpose(ps[:, banks[c // 4], (c % 4) * P:(c % 4 + 1) * P], hr[:, tile, c * P:(c + 1) * P], ident[:, :])
                    mm.then_inc(g["comb_turned"].sem, g["comb_turned"].tick(l, tile))
                    for bank in banks:
                        free[bank] = (g["comb_added"], (l, tile))
                    if tile:
                        mean_tile(tile - 1)
                for bank in (2, 3, 4, 5):
                    claim(bank)
                mean_tile(nt - 1)
                free[6] = (g["rstd_sqrt"], after)
            for tile in range(2):
                for half in range(2):
                    for c in range(4):
                        pe.wait_ge(g["fin_scaled"].sem, g["fin_scaled"].at(4 * half + c))
                        mm = pe.transpose(ps[:, 2 + 2 * tile + half, c * P:(c + 1) * P],
                                          ht[:, 4 * half + c, tile * P:(tile + 1) * P], ident[:, :])
                    mm.then_inc(g["fin_turned"].sem, g["fin_turned"].tick(tile, half))

        @block.scalar
        def _(act):
            def chain(ins):
                ins.then_inc(g["achain"].sem, g["achain"].tick())
                act.wait_ge(g["achain"].sem, g["achain"].n)

            for c in range(1, KC, 2):
                act.wait_ge(g["in_turned"].sem, g["in_turned"].at(c))
                nc.scalar.activation(xt[:, c, :], tile_bank[c % 2], ACT.Copy).then_inc(g["prep"].sem, g["prep"].tick("xt", c))
            act.wait_ge(g["vecs_in"].sem, 16 * 8)
            nc.scalar.activation(cond_rows[0:2, :], cond_rows[0:2, :], ACT.Silu).then_inc(g["cond_silu"].sem, g["cond_silu"].tick(0))

            def modp_copy(l, n):
                act.wait_ge(g["modp_done"].sem, g["modp_done"].at(l, n))
                prev = (l, n - 1) if n else (l - 1, MOD_BLOCKS - 1)
                if prev[0] >= 0:
                    act.wait_ge(g["modt_done"].sem, g["modt_done"].at(*prev))
                nc.scalar.activation(mrow[:, 0:MB], misc[:, 0:MB], ACT.Copy).then_inc(g["modp_copied"].sem, g["modp_copied"].tick(l, n))

            def squares(l, which):
                w = width(l) if which != "n1" else NTOK
                if which == "n1" and l == 0:
                    act.wait_ge(g["in_copied"].sem, g["in_copied"].at(KC - 2))
                    act.wait_ge(g["prep"].sem, g["prep"].at("xt", KC - 1))
                for c in range(KC):
                    if which == "n2":
                        act.wait_ge(g["added"].sem, g["added"].at(l, c))
                        round_weights(l, ("wo", c))
                    if c >= 3:
                        act.wait_ge(g["mean_done"].sem, g["mean_done"].at(l, which, c - 3))
                    nc.scalar.activation(sq[c % 3][:, 0:w], xt[:, c, 0:w], ACT.Square) \
                        .then_inc(g["sq_done"].sem, g["sq_done"].tick(l, which, c))
                root(l, which, KC - 1)

            def root(l, which, last):
                w = width(l) if which != "n1" else NTOK
                act.wait_ge(g["mean_done"].sem, g["mean_done"].at(l, which, last))
                nc.scalar.activation(rs[:, 0:w], pv_bank[:, 0:w], ACT.Sqrt, bias=eps[:, 0:1]) \
                    .then_inc(g["rstd_sqrt"].sem, g["rstd_sqrt"].tick(l, which))

            def round_weights(l, job, ahead=2):
                i = split_at[(l, job)] + ahead
                if i < len(split_order) and split_order[i][0] == l and (l == 0 or split_order[i][1] != ("g2", 1) or job[0] == "g2"):
                    round_item(i)

            def round_item(i):
                item = split_order[i]
                slot = ws_slots[item]
                act.wait_ge(ws_in[slot].sem, ws_in[slot].at(*item))
                if i >= 2:
                    last, step = ws_release(*split_order[i - 2])
                    act.wait_ge(last.sem, last.at(*step))
                m = 4 if item[1][:2] == ("wb", 8) else KC
                nc.scalar.activation(w_hi[:, i % 2, 0:m], ws[:, slot, 0:m, :], ACT.Copy) \
                    .then_inc(g["w_hi_set"].sem, g["w_hi_set"].tick(*item))

            def shift(l, which, first):
                for c in range(KC):
                    act.wait_ge(g["norm_mul"].sem, g["norm_mul"].at(l, which, c))
                    both = streams(0) if which == "n1" else streams(l)
                    for s, cols in both:
                        ins = nc.scalar.activation(ht[:, c, cols], ht[:, c, cols], ACT.Identity,
                                                   bias=modv[:, l, s, first + c:first + c + 1])
                    ins.then_inc(g["norm_add"].sem, g["norm_add"].tick(l, which, c))
                    if which == "n1":
                        act.wait_ge(g["norm_add"].sem, g["norm_add"].at(l, which, c))
                        nc.scalar.activation(ht_hi[:, c, :], ht[:, c, :], ACT.Copy) \
                            .then_inc(g["h_hi"].sem, g["h_hi"].tick(l, c))

            for l in range(DEPTH):
                w_all = width(l)
                if l == 0:
                    act.wait_ge(g["vec_ready"].sem, g["vec_ready"].at("eps"))
                if l == 0:
                    squares(l, "n1")
                if l == 0:
                    for n in range(FIRST_MODS):
                        modp_copy(0, n)
                round_item(split_at[(l, ("tile", "ck", 0))])
                shift(l, "n1", 0)
                round_item(split_at[(l, ("tile", "cv", 0))])
                for j in mixer_jobs(l):
                    if j[0] == "tile":
                        kind, c = j[1:]
                        act.wait_ge(g["tile_done"].sem, g["tile_done"].at(l, kind, c))
                        if kind in ("u", "aq", "ak", "g"):
                            round_weights(l, j)
                        bank = tile_banks[(l, kind, c)]
                        src = ps[:, bank, :]
                        if kind in ("aq", "cq"):
                            dst = (aq if kind == "aq" else cq)[:, c, 0:w_all]
                            ins = nc.scalar.activation(dst, src[:, 0:w_all], ACT.Copy, scale=SCALE)
                        elif kind == "ak":
                            ins = nc.scalar.activation(ak[:, c, :], src, ACT.Copy)
                        elif kind == "u":
                            ins = nc.scalar.activation(u[:, c, 0:w_all], src[:, 0:w_all], ACT.Copy)
                        elif kind == "ck":
                            ins = nc.scalar.activation(ck_raw, src, ACT.Copy)
                        elif kind == "cv":
                            ins = nc.scalar.activation(cv_raw, src, ACT.Copy)
                        elif kind == "av":
                            ins = nc.scalar.activation(gates[:, c, :], src, ACT.Copy)
                        else:
                            ins = nc.scalar.activation(gates[:, c, 0:w_all], src[:, 0:w_all], ACT.Tanh, scale=0.5)
                        ins.then_inc(g["tile_copied"].sem, g["tile_copied"].tick(l, kind, c))
                        if kind not in ("u", "aq", "ak", "g"):
                            round_weights(l, j)
                    elif j[0] == "vt":
                        kind, c = j[1:]
                        act.wait_ge(g["vt_done"].sem, g["vt_done"].at(l, kind, c))
                        nc.scalar.activation(cv if kind == "cv" else av[:, :, c * P:(c + 1) * P],
                                             misc.rearrange("p (t n) -> p t n", n=P), ACT.Copy) \
                            .then_inc(g["vt_copied"].sem, g["vt_copied"].tick(l, kind, c))
                    elif j[0] == "qk":
                        kind, s, h = j[1:]
                        act.wait_ge(g["max_done"].sem, g["max_done"].at(l, kind, s, h))
                        st, pb = stat[:, h % 2], prob[h % 2]
                        for qt in range(2):
                            if s == "x":
                                nc.scalar.activation(pb[:, qt, 0:SEQ], pb[:, qt, 0:SEQ], ACT.Exp, bias=st[:, qt:qt + 1],
                                                     accum_out=st[:, 2 + qt:3 + qt])
                                ins = nc.scalar.activation(pb[:, qt, SEQ:NTOK], score_bank[:, qt, SEQ:NTOK], ACT.Exp,
                                                           bias=st[:, qt:qt + 1], accum_out=st[:, 4 + qt:5 + qt])
                            else:
                                ins = nc.scalar.activation(pb[:, qt, 0:SEQ], score_bank[:, qt, 0:SEQ], ACT.Exp,
                                                           bias=st[:, qt:qt + 1], accum_out=st[:, 2 + qt:3 + qt])
                        if kind == "c":
                            ins = nc.scalar.activation(st[:, 6:8], st[:, 0:2], ACT.Exp, bias=sink[:, l, h:h + 1])
                        ins.then_inc(g["exp_done"].sem, g["exp_done"].tick(l, kind, s, h))
                    elif j[0] == "tr":
                        kind, s, h = j[1:]
                        act.wait_ge(g["pt_done"].sem, g["pt_done"].at(l, kind, s, h, 0))
                        nc.scalar.activation(prob_t[h % 2][:, 0:2, :], prob_bank[:, 0:2, :], ACT.Copy) \
                            .then_inc(g["pt_copied_a"].sem, g["pt_copied_a"].tick(l, kind, s, h))
                    elif j[0] == "pv":
                        kind, s, pair = j[1:]
                        act.wait_ge(g["pv_done"].sem, g["pv_done"].at(l, kind, s, pair))
                        cols = LATENT if s == "x" else CONTEXT
                        nc.scalar.activation(q_of(kind)[:, pair, cols], pv_bank[:, 0:SEQ], ACT.Copy) \
                            .then_inc(g["pv_copied"].sem, g["pv_copied"].tick(l, kind, s, pair))
                    elif j[0] == "modp":
                        modp_copy(*j[1:])
                    elif j[0] == "ys":
                        b, k = j[1:]
                        if b == 0:
                            act.wait_ge(g["pv_copied"].sem, g["pv_copied"].at(l, "a", "z", k))
                        elif b == 1:
                            act.wait_ge(g["pool_copied"].sem, g["pool_copied"].at(l, k))
                        else:
                            act.wait_ge(g["pv_copied"].sem, g["pv_copied"].at(l, "c", "z", k))
                        nc.scalar.activation(ys_hi[:, 4 * b + k, :], (aq, u, cq)[b][:, k, :], ACT.Copy) \
                            .then_inc(g["ys_hi_set"].sem, g["ys_hi_set"].tick(b, k))
                    elif j[0] == "pool":
                        for gr in range(4):
                            act.wait_ge(g["pool_done"].sem, g["pool_done"].at(l, gr))
                            nc.scalar.activation(u[:, gr, 0:w_all], ps[:, tile_banks[(l, "pool", gr)], 0:w_all], ACT.Copy,
                                                 scale=colv[:, 136 + 4 * l + gr:137 + 4 * l + gr]) \
                                .then_inc(g["pool_copied"].sem, g["pool_copied"].tick(l, gr))

                def round_merged(n):
                    act.wait_ge(g["merged"].sem, g["merged"].at(l, n))
                    nc.scalar.activation(mt_hi[:, n, 0:w_all], mt[:, n, 0:w_all], ACT.Copy) \
                        .then_inc(g["mt_hi_set"].sem, g["mt_hi_set"].tick(l, n))

                for n in range(KC):
                    act.wait_ge(g["gate_done"].sem, g["gate_done"].at(l, n))
                    if n >= 2:
                        act.wait_ge(g["merged"].sem, g["merged"].at(l, n - 2))
                    nc.scalar.activation(aux[:, n % 2, 0:w_all], ps[:, tile_banks[(l, "g2", n)], 0:w_all], ACT.Tanh, scale=0.5) \
                        .then_inc(g["gate_tanh"].sem, g["gate_tanh"].tick(l, n))
                    if l == 0:
                        round_weights(l, ("g2", n))
                        round_weights(l, ("wb", 0, n))
                        if n:
                            round_merged(n - 1)
                        if n < KC - 1:
                            round_weights(l, ("wb", 8, n))
                        continue
                    round_weights(l, ("g2", n), 1)
                    if n:
                        round_merged(n - 1)
                round_merged(KC - 1)
                round_weights(l, *((("wo", 0), 1) if l else (("wb", 8, KC - 1), 2)))
                squares(l, "n2")
                shift(l, "n2", 3 * KC)
                nt = w_all // P
                act.wait_ge(g["logits_t"].sem, g["logits_t"].at(l))
                nc.scalar.activation(mrow[0:NG + NE, 0:w_all], ps[0:NG + NE, 6, 0:w_all], ACT.Copy) \
                    .then_inc(g["logits_copied"].sem, g["logits_copied"].tick(l))
                for tile in range(nt):
                    for half in range(2):
                        act.wait_ge(g["hturn_done"].sem, g["hturn_done"].at(l, tile, half))
                        nc.scalar.activation(hr[:, tile, 512 * half:512 * half + 512], ps[:, 2 + (2 * tile + half) % 4, :], ACT.Copy) \
                            .then_inc(g["hrow_copied"].sem, g["hrow_copied"].tick(l, tile, half))
                for step in range(2):
                    act.wait_ge(g["r_exp"].sem, g["r_exp"].at(l, "in", step))
                    buf = r[:, 256:256 + 4 * nt] if step == 0 else r[:, 288:288 + nt]
                    nc.scalar.activation(buf, buf, ACT.Exp).then_inc(g["r_exp_done"].sem, g["r_exp_done"].tick(l, step))
                act.wait_ge(g["routed"].sem, g["routed"].at(l))
                nb = w_all // BLK

                def save_rows(src, row, signal, first=0, rows=BLK):
                    for j in range(2):
                        at = BLK * j + first
                        act.dma_start(y_rows[bass.ds(row, rows), j * 512:(j + 1) * 512], src[at:at + rows, :]) \
                            .then_inc(signal.sem, 16)

                if l == 0:
                    n_more = act.alloc_register("act_more")
                    act.reg_mov(n_more, 0)
                    for s in range(2):
                        act.sem_inc(y_copied[s].sem, 1)
                        act.sem_inc(y_saved[s].sem, 32)
                    act.sem_inc(g["yo_copied"].sem, 1)
                    act.sem_inc(g["yo_saved"].sem, 32)
                    act.sem_inc(g["yt_saved"].sem, 32)
                    n_tails = act.alloc_register("act_tails")
                    act.reg_mov(n_tails, 0)
                with act.Fori(0, NE // 2) as i:
                    for s in range(2):
                        e, done, mine = 2 * i + s, NE * l + 2 * i + s, 16 * l + i
                        other = mine + 1 if s == 0 else mine + 2
                        act.wait_ge(g["gu_done"].sem, done + 1)
                        act.wait_ge(hid_done[s].sem, mine + 1)
                        nc.scalar.activation(act_g[s], ps[:, 2 + s, 0:256], ACT.Silu).then_inc(g["silu_done"].sem, 1)
                        n = act.value_load(n_of[0:1, bass.ds(e, 1)], min_val=0, max_val=NTOK)
                        row = act.value_load(start_of[0:1, bass.ds(e, 1)], min_val=0, max_val=2 * NTOK)
                        act.wait_ge(y_saved[1 - s].sem, other * 32)
                        act.wait_ge(g["yt_saved"].sem, act.snap(n_tails, min_val=0, max_val=64) * 32 + 32)
                        act.nop(nofuse=True)
                        with act.If(n > BLK):
                            with act.Fori(1, nb) as b:
                                with act.If(n > b * BLK):
                                    more = act.snap(n_more, min_val=0, max_val=64)
                                    act.wait_ge(g["guo_done"].sem, more + 1)
                                    nc.scalar.activation(act_g[2], ps[:, 6, 0:256], ACT.Silu).then_inc(g["siluo_done"].sem, 1)
                                    act.wait_ge(g["downo_done"].sem, more + 1)
                                    act.wait_ge(g["yo_saved"].sem, more * 32 + 32)
                                    nc.scalar.activation(ysb[2], ps[:, 6, :], ACT.Copy).then_inc(g["yo_copied"].sem, 1)
                                    act.wait_ge(g["yo_copied"].sem, more + 2)
                                    save_rows(ysb[2], act.snap(row + b * BLK, min_val=0, max_val=2 * NTOK), g["yo_saved"])
                                    act.reg_add(n_more, n_more, 1)
                                act.nop()
                        act.nop()
                        act.wait_ge(down_done[s].sem, mine + 1)
                        act.wait_ge(y_saved[s].sem, mine * 32 + 32)
                        nc.scalar.activation(ysb[s], ps[:, 4 + s, :], ACT.Copy).then_inc(y_copied[s].sem, 1)
                        act.wait_ge(y_copied[s].sem, mine + 2)
                        act.wait_ge(g["yo_saved"].sem, act.snap(n_more, min_val=0, max_val=64) * 32 + 32)
                        save_rows(ysb[s], row, y_saved[s], rows=HALF)
                        with act.If(n > HALF):
                            save_rows(ysb[s], act.snap(row + HALF, min_val=0, max_val=2 * NTOK), g["yt_saved"], first=HALF, rows=HALF)
                            act.reg_add(n_tails, n_tails, 1)
                        act.nop()
                act.wait_ge(y_saved[0].sem, 32 * 16 * (l + 1) + 32)
                act.wait_ge(y_saved[1].sem, 32 * 16 * (l + 1) + 32)
                act.wait_ge(g["yt_saved"].sem, act.snap(n_tails, min_val=0, max_val=64) * 32 + 32)
                act.wait_ge(g["yo_saved"].sem, act.snap(n_more, min_val=0, max_val=64) * 32 + 32)
                act.sem_inc(g["prep"].sem, g["prep"].tick("y", l))
                after = (l + 1, "n1") if l + 1 < DEPTH else (l, "fin")

                def square_tile(tile):
                    act.wait_ge(g["comb_added"].sem, g["comb_added"].at(l, tile))
                    if tile >= 2:
                        act.wait_ge(g["mean_done"].sem, g["mean_done"].at(*after, tile - 2))
                    nc.scalar.activation(sq_tile[tile % 2], xt[:, :, tile * P:(tile + 1) * P], ACT.Square) \
                        .then_inc(g["sq_done"].sem, g["sq_done"].tick(*after, tile))

                act.wait_ge(g["dest_set"].sem, g["dest_set"].at(l, 2))
                for tile in range(nt):
                    got = yg_got[tile % 2]
                    act.wait_ge(got.sem, got.at(l, tile, 1))
                    nc.scalar.activation(hr[:, tile, :], yg[tile % 2][0], ACT.Copy, scale=route_w[:, 0, tile:tile + 1]) \
                        .then_inc(g["comb_half"].sem, g["comb_half"].tick(l, tile))
                    if tile:
                        square_tile(tile - 1)
                square_tile(nt - 1)
                root(*after, nt - 1)
            for tile in range(2):
                act.wait_ge(g["fin_turned"].sem, g["fin_turned"].at(tile, 1))
                nc.scalar.activation(hr[:, tile, 512:1024], ps[:, 3 + 2 * tile, :], ACT.Copy) \
                    .then_inc(g["prep"].sem, g["prep"].tick("fin", tile))

        @block.vector
        def _(dve):
            v = nc.vector

            def chain(ins):
                ins.then_inc(g["dchain"].sem, g["dchain"].tick())
                dve.wait_ge(g["dchain"].sem, g["dchain"].n)

            v.memset(eps[:, :], EPS).then_inc(g["vec_ready"].sem, g["vec_ready"].tick("eps"))
            chain(v.memset(cond[:, :, :], 0.0))
            chain(v.memset(ones_b[:, :], 1.0))
            for c in range(0, KC, 2):
                dve.wait_ge(g["in_turned"].sem, g["in_turned"].at(c))
                v.tensor_copy(xt[:, c, :], tile_bank[c % 2]).then_inc(g["in_copied"].sem, g["in_copied"].tick(c))
            dve.wait_ge(g["cond_turned"].sem, g["cond_turned"].at(0))
            chain(v.tensor_copy(colv[:, :], misc[:, 0:144]))
            v.tensor_copy(cond[:, :, 0:2], misc[:, 144:160].rearrange("p (k s) -> p k s", s=2)) \
                .then_inc(g["cond_cols"].sem, g["cond_cols"].tick(0))

            def mod_sum(l, n):
                dve.wait_ge(g["modt_done"].sem, g["modt_done"].at(l, n))
                cols = slice(MBC * n, MBC * n + MBC)
                v.tensor_reduce(modv[:, l, :, cols], misc[:, 0:MB].rearrange("p (q j r) -> p r q j", q=MBC, j=4)[:, 0:2], AX, ALU.add) \
                    .then_inc(g["mod_summed"].sem, g["mod_summed"].tick(l, n))
                dve.wait_ge(g["mod_summed"].sem, g["mod_summed"].at(l, n))
                bm = colv[:, 48 * l + MBC * n:48 * l + MBC * n + MBC].unsqueeze(1).broadcast_to([P, 2, MBC])
                v.tensor_tensor(modv[:, l, :, cols], modv[:, l, :, cols], bm, ALU.add) \
                    .then_inc(g["mod_ready"].sem, g["mod_ready"].tick(l, n))

            def leave_weights(l, job, ahead=2):
                i = split_at[(l, job)] + ahead
                if i < len(split_order) and split_order[i][0] == l and (l == 0 or split_order[i][1] != ("g2", 1) or job[0] == "g2"):
                    leave_item(i)

            def leave_item(i):
                item = split_order[i]
                dve.wait_ge(g["w_hi_set"].sem, g["w_hi_set"].at(*item))
                m = 4 if item[1][:2] == ("wb", 8) else KC
                v.tensor_tensor(w_lo[:, ws_slots[item], 0:m], ws[:, ws_slots[item], 0:m, :], w_hi[:, i % 2, 0:m].bitcast(F32),
                                ALU.subtract).then_inc(g["w_lo_set"].sem, g["w_lo_set"].tick(*item))

            def gains(l, norm):
                dve.wait_ge(g["mod_ready"].sem, g["mod_ready"].at(l, (MOD_BLOCKS if l or norm else FIRST_MODS) - 1))
                first = KC * (1 + 3 * norm)
                for s in range(2):
                    ins = v.scalar_tensor_tensor(gain[:, norm, s, :], modv[:, l, s, first:first + KC], 1.0,
                                                 colv[:, 96 + 16 * norm + KC * l:96 + 16 * norm + KC * (l + 1)], ALU.add, ALU.mult)
                if norm:
                    chain(v.tensor_scalar(half_gate[:, :, :], modv[:, l, :, 2 * KC:3 * KC], 0.5, None, ALU.mult))
                else:
                    chain(ins)

            def reciprocal_rms(l, which):
                w = width(l) if which != "n1" else NTOK
                dve.wait_ge(g["rstd_sqrt"].sem, g["rstd_sqrt"].at(l, which))
                v.reciprocal(rs[:, 0:w], rs[:, 0:w]).then_inc(g["rstd_done"].sem, g["rstd_done"].tick(l, which))
                dve.wait_ge(g["rstd_done"].sem, g["rstd_done"].at(l, which))

            def leave_h(l, c):
                dve.wait_ge(g["h_hi"].sem, g["h_hi"].at(l, c))
                v.tensor_tensor(ht_lo[:, c, :], ht[:, c, :], ht_hi[:, c, :].bitcast(F32), ALU.subtract) \
                    .then_inc(g["h_lo"].sem, g["h_lo"].tick(l, c))

            def scale_norm(l, which):
                w = width(l) if which != "n1" else NTOK
                for c in range(KC):
                    if which == "fin":
                        v.scalar_tensor_tensor(ht[:, c, 0:w], xt[:, c, 0:w], colv[:, 128 + c:129 + c], rs[:, 0:w], ALU.mult, ALU.mult) \
                            .then_inc(g["fin_scaled"].sem, g["fin_scaled"].tick(c))
                        continue
                    for s, cols in (streams(0) if which == "n1" else streams(l)):
                        ins = v.scalar_tensor_tensor(ht[:, c, cols], xt[:, c, cols], gain[:, int(which == "n2"), s, c:c + 1],
                                                     rs[:, cols], ALU.mult, ALU.mult)
                    ins.then_inc(g["norm_mul"].sem, g["norm_mul"].tick(l, which, c))
                    if which == "n1" and c >= 2:
                        leave_h(l, c - 2)
                if which == "n1":
                    leave_h(l, KC - 2)
                    leave_h(l, KC - 1)

            reciprocal_rms(0, "n1")
            for n in range(FIRST_MODS):
                mod_sum(0, n)
            for l in range(DEPTH):
                w_all = width(l)
                gains(l, 0)
                if l:
                    gains(l, 1)
                    reciprocal_rms(l, "n1")
                leave_item(split_at[(l, ("tile", "ck", 0))])
                scale_norm(l, "n1")
                leave_item(split_at[(l, ("tile", "cv", 0))])
                if l == 0:
                    dve.wait_ge(g["consts_in"].sem, g["consts_in"].at("tri"))
                    chain(v.tensor_copy(tri_b[:, :], arena[:, 0:P]))
                last_tr = {}
                for j in mixer_jobs(l):
                    if j[0] == "tile":
                        leave_weights(l, j)
                    elif j[0] == "rope":
                        kind, c = j[1:]
                        dve.wait_ge(g["rope_done"].sem, g["rope_done"].at(l, kind, c))
                        src = ck_raw[:, 0:SEQ] if kind == "ck" else cq[:, c, 0:SEQ]
                        v.tensor_tensor(rt0, misc[:, 0:SEQ], sin[:, :], ALU.mult)
                        chain(v.tensor_tensor(rt1, src, cos[:, :], ALU.mult))
                        if kind == "cq":
                            ins = v.tensor_tensor(src, rt0, rt1, ALU.add)
                        else:
                            for kv in range(2):
                                rows = slice(HD * kv, HD * kv + HD)
                                for half in range(2):
                                    to = slice(HD * half, HD * half + HD)
                                    v.tensor_copy(ck[to, kv, CONTEXT], ck_raw[rows, CONTEXT])
                                    ins = v.tensor_tensor(ck[to, kv, LATENT], rt0[rows], rt1[rows], ALU.add)
                        ins.then_inc(g["rope_out"].sem, g["rope_out"].tick(l, kind, c))
                        dve.wait_ge(g["rope_out"].sem, g["rope_out"].at(l, kind, c))
                    elif j[0] == "qk":
                        kind, s, h = j[1:]
                        st, pb = stat[:, h % 2], prob[h % 2]
                        if h % 2 in last_tr:
                            dve.wait_ge(g["pt_done"].sem, g["pt_done"].at(*last_tr[h % 2]))
                        if s == "x" and h == 0:
                            if kind == "c":
                                dve.wait_ge(g["swa_in"].sem, g["swa_in"].at(l))
                                dve.wait_ge(g["rope_out"].sem, g["rope_out"].at(l, "cq", 3))
                        if kind == "a" and s == "x":
                            dve.wait_ge(g["bias_ready"].sem, g["bias_ready"].at(l, h))
                        dve.wait_ge(g["qk_done"].sem, g["qk_done"].at(l, kind, s, h))
                        if s == "x":
                            for qt in range(2):
                                add = swa[:, qt, :] if kind == "c" else bias[h % 4][:, qt].rearrange("p r k -> p (r k)")
                                v.tensor_tensor_reduce(pb[:, qt, 0:SEQ], score_bank[:, qt, 0:SEQ], add, 1.0, NEG, ALU.add, ALU.max,
                                                       st[:, 8 + qt:9 + qt])
                            chain(v.tensor_reduce(st[:, 10:12], score_bank[:, :, SEQ:NTOK], AX, ALU.max))
                            chain(v.tensor_tensor(st[:, 8:10], st[:, 8:10], st[:, 10:12], ALU.max))
                        else:
                            chain(v.tensor_reduce(st[:, 8:10], score_bank[:, :, 0:SEQ], AX, ALU.max))
                        if kind == "c":
                            ins = v.tensor_scalar(st[:, 0:2], st[:, 8:10], sink[:, l, h:h + 1], -1.0, ALU.max, ALU.mult)
                        else:
                            ins = v.tensor_scalar(st[:, 0:2], st[:, 8:10], -1.0, None, ALU.mult)
                        ins.then_inc(g["max_done"].sem, g["max_done"].tick(l, kind, s, h))
                        dve.wait_ge(g["exp_done"].sem, g["exp_done"].at(l, kind, s, h))
                        total = st[:, 2:4]
                        if s == "x":
                            chain(v.tensor_tensor(st[:, 12:14], total, st[:, 4:6], ALU.add))
                            total = st[:, 12:14]
                        if kind == "c":
                            chain(v.tensor_tensor(st[:, 12:14], total, st[:, 6:8], ALU.add))
                            total = st[:, 12:14]
                        chain(v.reciprocal(st[:, 14:16], total))
                        n = NTOK if s == "x" else SEQ
                        for qt in range(2):
                            ins = v.tensor_scalar(pb[:, qt, 0:n], pb[:, qt, 0:n], st[:, 14 + qt:15 + qt], None, ALU.mult)
                        ins.then_inc(g["scaled"].sem, g["scaled"].tick(l, kind, s, h))
                    elif j[0] == "tr":
                        kind, s, h = j[1:]
                        if s == "x":
                            dve.wait_ge(g["pt_done"].sem, g["pt_done"].at(l, kind, s, h, 1))
                            v.tensor_copy(prob_t[h % 2][:, 2:4, :], prob_bank[:, 2:4, :]) \
                                .then_inc(g["pt_copied_d"].sem, g["pt_copied_d"].tick(l, kind, s, h))
                        last_tr[h % 2] = (l, kind, s, h, 1 if s == "x" else 0)
                    elif j[0] == "modt":
                        mod_sum(*j[1:])
                    elif j[0] == "ys":
                        b, k = j[1:]
                        dve.wait_ge(g["ys_hi_set"].sem, g["ys_hi_set"].at(b, k))
                        v.tensor_tensor(ys_lo[b][:, k, :], (aq, u, cq)[b][:, k, :], ys_hi[:, 4 * b + k, :].bitcast(F32), ALU.subtract) \
                            .then_inc(g["ys_lo_set"].sem, g["ys_lo_set"].tick(b, k))
                if l == 0:
                    gains(0, 1)

                def leave_merged(n):
                    dve.wait_ge(g["mt_hi_set"].sem, g["mt_hi_set"].at(l, n))
                    v.tensor_tensor(mt_lo[:, n, 0:w_all], mt[:, n, 0:w_all], mt_hi[:, n, 0:w_all].bitcast(F32), ALU.subtract) \
                        .then_inc(g["mt_lo_set"].sem, g["mt_lo_set"].tick(l, n))

                for n in range(KC):
                    if l == 0:
                        leave_weights(l, ("g2", n))
                        leave_weights(l, ("wb", 0, n))
                        if n < KC - 1:
                            leave_weights(l, ("wb", 8, n))
                    else:
                        leave_weights(l, ("g2", n), 1)
                    dve.wait_ge(g["branch_done"].sem, g["branch_done"].at(l, n))
                    dve.wait_ge(g["gate_tanh"].sem, g["gate_tanh"].at(l, n))
                    if n:
                        dve.wait_ge(g["merged"].sem, g["merged"].at(l, n - 1))
                    b0 = 2 + 3 * (n % 2)
                    for b, (gt, to) in enumerate(((gates[:, n], mt[:, n]), (gates[:, 8 + n], aux[:, 2]), (aux[:, n % 2], aux[:, 3]))):
                        ins = v.scalar_tensor_tensor(to[:, 0:w_all], gt[:, 0:w_all], 1.0, ps[:, b0 + b, 0:w_all], ALU.add, ALU.mult)
                    chain(ins)
                    chain(v.tensor_tensor(mt[:, n, 0:w_all], mt[:, n, 0:w_all], aux[:, 2, 0:w_all], ALU.add))
                    v.tensor_tensor(mt[:, n, 0:w_all], mt[:, n, 0:w_all], aux[:, 3, 0:w_all], ALU.add) \
                        .then_inc(g["merged"].sem, g["merged"].tick(l, n))
                    if n:
                        leave_merged(n - 1)
                leave_merged(KC - 1)
                leave_weights(l, *((("wo", 0), 1) if l else (("wb", 8, KC - 1), 2)))
                for n in range(KC):
                    dve.wait_ge(g["out_done"].sem, g["out_done"].at(l, n))
                    for s, cols in streams(l):
                        ins = v.scalar_tensor_tensor(xt[:, n, cols], ps[:, tile_banks[(l, "wo", n)], cols], half_gate[:, s, n:n + 1],
                                                     xt[:, n, cols], ALU.mult, ALU.add)
                    ins.then_inc(g["added"].sem, g["added"].tick(l, n))
                    leave_weights(l, ("wo", n))
                dve.wait_ge(g["added"].sem, g["added"].at(l, KC - 1))
                reciprocal_rms(l, "n2")
                scale_norm(l, "n2")
                nt, nb = w_all // P, w_all // BLK
                dve.wait_ge(g["logits_done"].sem, g["logits_done"].at(l))

                def tmp(at, *dims):
                    a = r[:, at:at + dims[0] * (dims[1] if len(dims) > 1 else 1)]
                    return a.rearrange("p (a b) -> p a b", b=dims[1]) if len(dims) > 1 else a

                def spread(a, m):
                    return a.unsqueeze(2).broadcast_to([P, nt, m])

                lg = tmp(0, nt, 36)
                gmax, gtop, emax, etop = tmp(144, nt), tmp(148, nt), tmp(152, nt), tmp(156, nt)
                p_grp, w_sum, emax2 = tmp(160, nt), tmp(164, nt), tmp(168, nt)
                gexp, goh, gsc = tmp(256, nt, 4), tmp(608, nt, 4), tmp(624, nt, 4)
                gap = tmp(288, nt)
                le, le2, esc = tmp(448, nt, 8), tmp(576, nt, 8), tmp(544, nt, 8)
                oh = [tmp(480, nt, 8), tmp(512, nt, 8)]
                ohe = [tmp(640, nt, NE), tmp(768, nt, NE)]
                wide = tmp(896, nt, NE)
                both = tmp(1152, nt, NE)
                msk = r[:, 1024:1088].bitcast(BF16).rearrange("p (t e) -> p t e", e=NE)
                cnt, incl, start, one = tmp(1408, NE), tmp(1440, NE), tmp(1472, NE), tmp(1504, NE)
                pos = tmp(1536, nt, NE)
                pos_k = [tmp(1664, nt), tmp(1668, nt)]
                dest_k = [tmp(1680, nt), tmp(1684, nt)]
                down4, down8 = small[:, 0:4], small[:, 4:12]

                dve.wait_ge(g["router_in"].sem, g["router_in"].at(l, 3))
                chain(v.tensor_tensor(lg, misc[:, 0:64 * nt].rearrange("p (t n) -> p t n", n=64)[:, :, 0:36],
                                      br[:, :].unsqueeze(1).broadcast_to([P, nt, 36]), ALU.add))

                def top_one_hot(values, best, score, order, top, out, m):
                    chain(v.tensor_reduce(best, values, AX, ALU.max))
                    chain(v.tensor_tensor(score, values, spread(best, m), ALU.is_ge))
                    chain(v.tensor_tensor(score, score, order.unsqueeze(1).broadcast_to([P, nt, m]), ALU.mult))
                    chain(v.tensor_reduce(top, score, AX, ALU.max))
                    chain(v.tensor_tensor(out, score, spread(top, m), ALU.is_equal))

                top_one_hot(lg[:, :, 0:4], gmax, gsc, down4, gtop, goh, 4)
                v.tensor_tensor(gexp, lg[:, :, 0:4], spread(gmax, 4), ALU.subtract) \
                    .then_inc(g["r_exp"].sem, g["r_exp"].tick(l, "in", 0))
                chain(v.tensor_tensor(wide.rearrange("p t (g i) -> p t g i", i=8), lg[:, :, 4:36].rearrange("p t (g i) -> p t g i", i=8),
                                      goh.unsqueeze(3).broadcast_to([P, nt, 4, 8]), ALU.mult))
                chain(v.tensor_reduce(le, wide.rearrange("p t (g i) -> p t i g", i=8), AX, ALU.add))
                top_one_hot(le, emax, esc, down8, etop, oh[0], 8)
                chain(v.scalar_tensor_tensor(le2, oh[0], NEG, le, ALU.mult, ALU.add))
                top_one_hot(le2, emax2, esc, down8, etop, oh[1], 8)
                v.tensor_tensor(gap, emax2, emax, ALU.subtract).then_inc(g["r_exp"].sem, g["r_exp"].tick(l, "in", 1))
                for k in range(2):
                    chain(v.tensor_tensor(ohe[k].rearrange("p t (g i) -> p t g i", i=8), goh.unsqueeze(3).broadcast_to([P, nt, 4, 8]),
                                          oh[k].unsqueeze(2).broadcast_to([P, nt, 4, 8]), ALU.mult))
                v.tensor_tensor(msk[:, 0:nt], ohe[0], ohe[1], ALU.add).then_inc(g["r_onehot"].sem, g["r_onehot"].tick(l))
                chain(v.tensor_tensor(both, ohe[0], ohe[1], ALU.add))
                chain(v.memset(place1[:, :, :], 0.0))
                chain(v.memset(one, 1.0))
                dve.wait_ge(g["r_pos"].sem, g["r_pos"].at(l))
                chain(v.tensor_copy(pos, ps[:, 6, 0:nt * NE].rearrange("p (t e) -> p t e", e=NE)))
                chain(v.tensor_copy(cnt, ps[:, 6, 4 * NE:5 * NE]))
                chain(v.tensor_tensor_scan(incl, one, cnt, 0.0, ALU.mult, ALU.add))
                chain(v.tensor_tensor(start, incl, cnt, ALU.subtract))
                chain(v.tensor_copy(n_of[:, :], cnt[0:1]))
                v.tensor_copy(start_of[:, :], start[0:1]).then_inc(g["routed"].sem, g["routed"].tick(l))
                chain(v.scalar_tensor_tensor(place1[:, 0:nt, 0:NE], pos, 1.0, both, ALU.add, ALU.mult))

                def set_pick(i, e, first, signal):
                    v.tensor_tensor(pick[i][:, 0:nt, :], place1[:, 0:nt, bass.ds(e, 1)].broadcast_to([P, nt, BLK]),
                                    slots1[:, bass.ds(first, BLK)].unsqueeze(1).broadcast_to([P, nt, BLK]), ALU.is_equal) \
                        .then_inc(signal.sem, 1)

                for i in range(2):
                    v.tensor_tensor(pick[i][:, 0:nt, :], place1[:, 0:nt, i:i + 1].broadcast_to([P, nt, BLK]),
                                    slots1[:, 0:BLK].unsqueeze(1).broadcast_to([P, nt, BLK]), ALU.is_equal) \
                        .then_inc(g["pick_set"].sem, 1)
                for k in range(2):
                    chain(v.tensor_tensor(wide, ohe[k], pos, ALU.mult))
                    chain(v.tensor_reduce(pos_k[k], wide, AX, ALU.add))
                    chain(v.tensor_tensor(wide, ohe[k], start.unsqueeze(1).broadcast_to([P, nt, NE]), ALU.mult))
                    chain(v.tensor_reduce(dest_k[k], wide, AX, ALU.add))
                    ins = v.tensor_tensor(dest[:, k, 0:nt], dest_k[k], pos_k[k], ALU.add)
                    ins.then_inc(g["dest_set"].sem, g["dest_set"].tick(l, k))
                dve.wait_ge(g["r_exp_done"].sem, g["r_exp_done"].at(l, 1))
                chain(v.tensor_reduce(p_grp, gexp, AX, ALU.add))
                chain(v.reciprocal(p_grp, p_grp))
                chain(v.tensor_scalar(w_sum, gap, 1.0, None, ALU.add))
                chain(v.reciprocal(w_sum, w_sum))
                chain(v.tensor_tensor(route_w[:, 0, 0:nt], p_grp, w_sum, ALU.mult))
                v.tensor_tensor(route_w[:, 1, 0:nt], route_w[:, 0, 0:nt], gap, ALU.mult) \
                    .then_inc(g["dest_set"].sem, g["dest_set"].tick(l, 2))
                dve.wait_ge(g["dest_set"].sem, g["dest_set"].at(l, 2))

                if l == 0:
                    n_more = dve.alloc_register("dve_more")
                    dve.reg_mov(n_more, 0)
                    for s in range(2):
                        dve.sem_inc(hid_done[s].sem, 1)
                dve.wait_ge(g["xt_done"].sem, (NE + 1) * l + 1)
                v.tensor_copy(xg[0], ps[:, 0, :].rearrange("p (k n) -> p k n", n=BLK)).then_inc(g["xt_copied"].sem, 1)
                with dve.Fori(0, NE // 2) as i:
                    for s in range(2):
                        e, done = 2 * i + s, NE * l + 2 * i + s
                        dve.wait_ge(g["silu_done"].sem, done + 1)
                        v.tensor_tensor(hid[s], act_g[s], ps[:, 2 + s, 256:512], ALU.mult).then_inc(hid_done[s].sem, 1)
                        n = dve.value_load(n_of[0:1, bass.ds(e, 1)], min_val=0, max_val=NTOK)
                        with dve.If(n > BLK):
                            with dve.Fori(1, nb) as b:
                                with dve.If(n > b * BLK):
                                    more = dve.snap(n_more, min_val=0, max_val=64)
                                    set_pick(2, e, b * BLK, g["picko_set"])
                                    dve.wait_ge(g["xto_done"].sem, more + 1)
                                    v.tensor_copy(xg[2], ps[:, 7, :].rearrange("p (k n) -> p k n", n=BLK)).then_inc(g["xto_copied"].sem, 1)
                                    dve.wait_ge(g["siluo_done"].sem, more + 1)
                                    v.tensor_tensor(hid[2], act_g[2], ps[:, 6, 256:512], ALU.mult).then_inc(g["hido_done"].sem, 1)
                                    dve.wait_ge(g["hidto_done"].sem, more + 1)
                                    v.tensor_copy(hid_t[2], ps[:, 7, 0:256].rearrange("p (c n) -> p c n", n=P)) \
                                        .then_inc(g["hidto_copied"].sem, 1)
                                    dve.reg_add(n_more, n_more, 1)
                                dve.nop()
                        dve.nop()
                        dve.wait_ge(g["hidt_done"].sem, done + 1)
                        v.tensor_copy(hid_t[s], ps[:, 1, 0:256].rearrange("p (c n) -> p c n", n=P)).then_inc(g["hidt_copied"].sem, 1)
                        dve.wait_ge(g["xt_done"].sem, done + l + 2)
                        v.tensor_copy(xg[1 - s], ps[:, 0, :].rearrange("p (k n) -> p k n", n=BLK)).then_inc(g["xt_copied"].sem, 1)
                        set_pick(s, e + 2, 0, g["pick_set"])
                def add_tile(tile):
                    cols, s = slice(tile * P, (tile + 1) * P), tile // 2
                    dve.wait_ge(g["comb_turned"].sem, g["comb_turned"].at(l, tile))
                    for c in range(KC):
                        ins = v.scalar_tensor_tensor(xt[:, c, cols], ps[:, 2 + 2 * (tile % 2) + c // 4, (c % 4) * P:(c % 4 + 1) * P],
                                                     modv[:, l, s, 5 * KC + c:5 * KC + c + 1], xt[:, c, cols], ALU.mult, ALU.add)
                    ins.then_inc(g["comb_added"].sem, g["comb_added"].tick(l, tile))

                for tile in range(nt):
                    dve.wait_ge(g["comb_half"].sem, g["comb_half"].at(l, tile))
                    v.scalar_tensor_tensor(hr[:, tile, :], yg[tile % 2][1], route_w[:, 1, tile:tile + 1], hr[:, tile, :], ALU.mult, ALU.add) \
                        .then_inc(g["comb"].sem, g["comb"].tick(l, tile))
                    if tile:
                        add_tile(tile - 1)
                add_tile(nt - 1)
                dve.wait_ge(g["comb_added"].sem, g["comb_added"].at(l, nt - 1))
            reciprocal_rms(DEPTH - 1, "fin")
            scale_norm(DEPTH - 1, "fin")
            for tile in range(2):
                dve.wait_ge(g["fin_turned"].sem, g["fin_turned"].at(tile, 0))
                v.tensor_copy(hr[:, tile, 0:512], ps[:, 2 + 2 * tile, :]).then_inc(g["fin_copied"].sem, g["fin_copied"].tick(tile))

        @block.gpsimd
        def _(pool):
            q = nc.gpsimd

            def chain(ins):
                ins.then_inc(g["pchain"].sem, g["pchain"].tick())
                pool.wait_ge(g["pchain"].sem, g["pchain"].n)

            for l in range(DEPTH):
                w_all = width(l)
                nt, nb = w_all // P, w_all // BLK
                if l:
                    pool.wait_ge(g["routed"].sem, g["routed"].at(l - 1))
                for i, (dst, src) in enumerate((
                        (wr[:, :, 0:NG], t["w_router_group"][l].rearrange("(k p) n -> p k n", p=P)),
                        (wr[:, :, NG:], t["w_router_expert"][l].rearrange("(k p) n -> p k n", p=P)),
                        (br[:, 0:NG], t["b_router_group"][l].partition_broadcast(P)),
                        (br[:, NG:], t["b_router_expert"][l].partition_broadcast(P)))):
                    pool.dma_start(dst, src).then_inc(g["router_in"].sem, g["router_in"].tick(l, i, by=16))
                pool.wait_ge(g["norm_mul"].sem, g["norm_mul"].at(l, "n1", KC - 1))
                a, b = CONST_AT["swa"]
                pool.dma_start(aux[:, 3, :], t["consts"][:, a:b]).then_inc(g["swa_in"].sem, g["swa_in"].tick(l, by=16))
                ns = w_all // SEQ
                uv = u.rearrange("p g (s n) -> p g s n", n=SEQ)
                n_pad = SEQ + 16
                pool.wait_ge(g["tile_copied"].sem, g["tile_copied"].at(l, "u", 3))
                for gr in range(4):
                    one, two = pad
                    chain(q.memset(one[:, 0:ns, :], 0.0))
                    chain(q.tensor_copy(one[:, 0:ns, 8:8 + SEQ], uv[:, gr, 0:ns, :]))
                    lo, hi, off = 1, n_pad, (1, 0)
                    reach = 1
                    for step in range(gr + 1):
                        back, ahead = ((1, 0), (1, 1), (2, 2), (4, 4))[step]
                        lo, hi = ((1, 272), (2, 271), (4, 269), (8, 264))[step]
                        chain(q.tensor_tensor(two[:, 0:ns, lo:hi], one[:, 0:ns, lo - back:hi - back], one[:, 0:ns, lo + ahead:hi + ahead], ALU.add))
                        one, two = two, one
                    chain(q.tensor_scalar(two[:, 0:ns, 8:8 + SEQ], one[:, 0:ns, 8:8 + SEQ], 1.0 / (2 << gr), None, ALU.mult))
                    for side, at in ((0, 8), (1, SEQ)):
                        e = edge[:, gr, 8 * side:8 * side + 8].unsqueeze(1).broadcast_to([P, ns, 8])
                        chain(q.tensor_tensor(two[:, 0:ns, at:at + 8], two[:, 0:ns, at:at + 8], e, ALU.mult))
                    q.tensor_tensor(uv[:, gr, 0:ns, :], two[:, 0:ns, 8:8 + SEQ], uv[:, gr, 0:ns, :], ALU.subtract) \
                        .then_inc(g["pooled"].sem, g["pooled"].tick(l, gr))
                    pool.wait_ge(g["pooled"].sem, g["pooled"].at(l, gr))
                rpb = t["rpb_a"]

                def load_bias(h):
                    if h >= 4:
                        pool.wait_ge(g["max_done"].sem, g["max_done"].at(l, "a", "x", h - 4))
                    elif h == 3:
                        pool.wait_ge(g["max_done"].sem, g["max_done"].at(l, "c", "x", HEADS - 1))
                    for qt in range(2):
                        for j in range(2):
                            row = 7 - (2 * qt + j)
                            at = ((l * HEADS + h) * 15 + row) * RPB_REPEATS * 31 + 15
                            src = bass.AP(rpb.tensor, at, [[30, GW], [RPB_REPEATS * 31, ROWS], [1, GW]])
                            pool.dma_start(bias[h % 4][GW * j:GW * j + GW, qt], src) \
                                .then_inc(bias_in[h % 4].sem, bias_in[h % 4].tick(l, h, qt, j, by=16))

                load_bias(0)
                for h in range(HEADS):
                    if h + 1 < HEADS:
                        load_bias(h + 1)
                    pool.wait_ge(bias_in[h % 4].sem, bias_in[h % 4].at(l, h, 1, 1))
                    b8 = bias[h % 4].rearrange("p q r k -> p (q r) k")
                    chain(q.tensor_tensor(b8, b8, colok[:, :].unsqueeze(1).broadcast_to([P, 8, GW]), ALU.mult))
                    q.tensor_tensor(b8, b8, colneg[:, :].unsqueeze(1).broadcast_to([P, 8, GW]), ALU.add) \
                        .then_inc(g["bias_ready"].sem, g["bias_ready"].tick(l, h))
                pool.wait_ge(g["dest_set"].sem, g["dest_set"].at(l, 1))
                pool.wait_ge(g["prep"].sem, g["prep"].at("y", l))
                pool.wait_ge(g["pick_set"].sem, (NE + 2) * (l + 1))
                pool.wait_ge(g["xt_copied"].sem, (NE + 1) * (l + 1))
                for tile in range(nt):
                    if tile >= 2:
                        pool.wait_ge(g["comb"].sem, g["comb"].at(l, tile - 2))
                    for k in range(2):
                        pool.indirect_dma_start(out=yg[tile % 2][k], out_offset=None, in_=y_rows[0:2 * w_all, :],
                                                in_offset=bass.IndirectOffsetOnAxis(ap=dest[:, k, tile:tile + 1], axis=0)) \
                            .then_inc(yg_got[tile % 2].sem, yg_got[tile % 2].tick(l, tile, k, by=16))
    return {n: s.seen for n, s in signals.items()}


def constants():
    import numpy as np

    c = np.zeros((P, NCONST), np.float32)

    def put(name, a):
        lo, hi = CONST_AT[name]
        a = np.asarray(a, np.float32).reshape(P, -1)
        c[:, lo:lo + a.shape[1]] = a

    p = np.arange(P)
    put("ident", np.eye(P))
    rot = np.zeros((P, P))
    for m in range(P):
        rot[m + 16 if m % 32 < 16 else m - 16, m] = -1.0 if m % 32 < 16 else 1.0
    put("rot", rot)
    put("mean", np.full((P, P), 1.0 / D))
    tok = np.arange(SEQ)
    inv = (np.float32(10000.0) ** (-np.arange(0, 32, 2, dtype=np.float32) / np.float32(32))).astype(np.float32)
    where = np.where((p % 64 < 32)[:, None], (tok // GW)[None, :], (tok % GW)[None, :]).astype(np.float32)
    ang = where * inv[p % 16][:, None]
    put("cos", np.cos(ang))
    put("sin", np.sin(ang))
    col = np.arange(GW)
    start = np.clip(col - 8, 0, GW - 16)
    ok = (col[None, :] >= start[:, None]) & (col[None, :] < start[:, None] + 16)
    ok = np.concatenate([ok, ok])
    put("colok", ok)
    put("colneg", np.where(ok, 0.0, NEG))
    edge = np.ones((4, 16))
    for g in range(4):
        w = 2 << g
        for i in range(8):
            edge[g, i] = w / min(w, i + w // 2)
            edge[g, 8 + i] = w / min(w, 8 - i + w // 2)
    put("edge", np.broadcast_to(edge.reshape(1, 64), (P, 64)))
    small = np.zeros((P, 32))
    small[:, 0:4] = 4 - np.arange(4)
    small[:, 4:12] = 8 - np.arange(8)
    put("small", small)
    key = np.arange(SEQ)
    put("swa", np.stack([np.where(np.abs(key[None, :] - (128 * q + p)[:, None]) <= 128, 0.0, NEG) for q in range(2)], 1))
    put("tri", p[:, None] < p[None, :])
    put("slots1", np.broadcast_to(1 + np.arange(512), (P, 512)))
    return c


_INS = ["x", "c", "ctx", "c_ctx", "w_mod", "b_mod", "norm1_g", "norm2_g", "w_in", "rpb_a", "w_pool", "pool_scale",
        "sink_c", "w_branch", "w_out", "w_router_group", "b_router_group", "w_router_expert", "b_router_expert",
        "w_exp_gate", "w_exp_up", "w_exp_down", "final_g"]


def kernel(**inputs):
    import numpy as _np
    import concourse.bacc as _bacc
    from concourse import mybir as _mybir
    from concourse.bass_utils import run_bass_kernel_spmd as _run

    arrays = {f"in_{n}_dram": _np.ascontiguousarray(inputs[n]) for n in _INS}
    arrays["in_rpb_a_dram"] = _np.tile(inputs["rpb_a"], (1, 1, 1, RPB_REPEATS))
    arrays["in_consts_dram"] = constants()

    def build(counts):
        nc = _bacc.Bacc("TRN2", target_bir_lowering=False, num_devices=1)
        t = {n[3:-5]: nc.dram_tensor(n, a.shape, _mybir.dt.from_np(a.dtype), kind="ExternalInput").ap() for n, a in arrays.items()}
        out = nc.dram_tensor("out_0_dram", (1, SEQ, D), F32, kind="ExternalOutput").ap()
        return nc, hybrid_block(nc, t, out, counts)

    _, counts = build(None)
    nc, _ = build(counts)
    r = _run(nc, [arrays], core_ids=[0])
    return r.results[0]["out_0_dram"]
```
